# Optimizing a Trainium2 kernel written in Bass

```python
import math
import jax, jax.numpy as jnp
from jax import lax
import numpy as np

D_MODEL = 2048
BATCH = 1
SEQ = 512
DEPTH = 1

DN_HEADS = 8
DN_HEAD_DIM = 128
DN_WIDTH = DN_HEADS * DN_HEAD_DIM
CONV_WIDTH = 4
CHUNK = 64
DA_HEADS = 4
DA_HEAD_DIM = 128
DA_V_DIM = 2 * DA_HEAD_DIM
DA_QK_WIDTH = DA_HEADS * 2 * DA_HEAD_DIM
DA_WIDTH = DA_HEADS * DA_V_DIM
Q_BLOCK = 128
D_MIX = DN_WIDTH + DA_WIDTH
OFF_DN_QKV = 0
OFF_DN_Z = OFF_DN_QKV + 3 * DN_WIDTH
OFF_DN_B = OFF_DN_Z + DN_WIDTH
OFF_DN_A = OFF_DN_B + DN_HEADS
OFF_DA_Q = OFF_DN_A + DN_HEADS
OFF_DA_K = OFF_DA_Q + DA_QK_WIDTH
OFF_DA_V = OFF_DA_K + DA_QK_WIDTH
D_IN = OFF_DA_V + DA_WIDTH
D_FF = (((8 * D_MODEL + 2) // 3 + 255) // 256) * 256
EPS = 1e-6

kernel_name = "hymba_gdn_diffattn_alibi_swiglu"

def rmsnorm(x, w):
    xf = x.astype(jnp.float32)
    y = xf * lax.rsqrt(jnp.mean(xf * xf, axis=-1, keepdims=True) + EPS)
    return (y * w.astype(jnp.float32)).astype(x.dtype)

def l2norm(x):
    return x * lax.rsqrt(jnp.sum(x * x, axis=-1, keepdims=True) + EPS)

def causal_depthwise_conv(x, w):
    K = w.shape[0]
    T = x.shape[1]
    xp = jnp.pad(x, ((0, 0), (K - 1, 0), (0, 0)))
    return sum(xp[:, i:i + T] * w[i] for i in range(K))

def gated_delta_rule(q, k, v, g, beta):
    B, T, H, dk = q.shape
    dv = v.shape[-1]
    N = T // CHUNK

    def chunks(a):
        return a.reshape(B, N, CHUNK, H, a.shape[-1]).transpose(0, 3, 1, 2, 4)

    qc, kc, vc = chunks(q), chunks(k), chunks(v)
    gc = jnp.cumsum(g.reshape(B, N, CHUNK, H).transpose(0, 3, 1, 2), axis=-1)
    bc = beta.reshape(B, N, CHUNK, H).transpose(0, 3, 1, 2)[..., None]

    tri_incl = jnp.tril(jnp.ones((CHUNK, CHUNK), dtype=bool))
    tri_strict = jnp.tril(jnp.ones((CHUNK, CHUNK), dtype=bool), k=-1)
    decay = jnp.exp(jnp.where(tri_incl, gc[..., :, None] - gc[..., None, :], -jnp.inf))

    kb = kc * bc
    m = jnp.where(tri_strict, jnp.einsum('bhnid,bhnjd->bhnij', kb, kc) * decay, 0.0)
    eye_m = m + jnp.eye(CHUNK, dtype=m.dtype)
    u = lax.linalg.triangular_solve(eye_m, vc * bc, left_side=True, lower=True, unit_diagonal=True)
    w = lax.linalg.triangular_solve(eye_m, kb * jnp.exp(gc)[..., None], left_side=True, lower=True,
                                    unit_diagonal=True)
    a_qk = jnp.einsum('bhnid,bhnjd->bhnij', qc, kc) * decay
    glast = gc[..., -1]
    q_dec = qc * jnp.exp(gc)[..., None]
    k_dec = kc * jnp.exp(glast[..., None] - gc)[..., None]

    def step(S, inp):
        q_i, k_i, u_i, w_i, a_i, gl_i = inp
        v_new = u_i - jnp.einsum('bhcd,bhde->bhce', w_i, S)
        o_i = jnp.einsum('bhcd,bhde->bhce', q_i, S) + jnp.einsum('bhij,bhje->bhie', a_i, v_new)
        S = S * jnp.exp(gl_i)[..., None, None] + jnp.einsum('bhcd,bhce->bhde', k_i, v_new)
        return S, o_i

    xs = tuple(jnp.moveaxis(a, 2, 0) for a in (q_dec, k_dec, u, w, a_qk, glast))
    S0 = jnp.zeros((B, H, dk, dv), dtype=jnp.float32)
    _, o = lax.scan(step, S0, xs)
    return o.transpose(1, 0, 3, 2, 4).reshape(B, T, H, dv)

def differential_attention(q, k, v, lam):
    B, T, H, _, d = q.shape
    NB = T // Q_BLOCK
    scale = d ** -0.5
    slopes = 2.0 ** (-8.0 * jnp.arange(1, H + 1, dtype=jnp.float32) / H)
    kf = k.astype(jnp.float32)
    vf = v.astype(jnp.float32)
    kpos = jnp.arange(T)
    q_blocks = q.astype(jnp.float32).reshape(B, NB, Q_BLOCK, H, 2, d).transpose(1, 0, 2, 3, 4, 5)

    def block(args):
        qb, bi = args
        s = jnp.einsum('bqhcd,bkhcd->bhcqk', qb, kf) * scale
        qpos = bi * Q_BLOCK + jnp.arange(Q_BLOCK)
        dist = (qpos[:, None] - kpos[None, :]).astype(jnp.float32)
        s = s - slopes[None, :, None, None, None] * dist
        s = jnp.where(dist >= 0, s, -jnp.inf)
        p = jax.nn.softmax(s, axis=-1)
        p = p[:, :, 0] - lam * p[:, :, 1]
        return jnp.einsum('bhqk,bkhe->bqhe', p, vf)

    out = lax.map(block, (q_blocks, jnp.arange(NB)))
    return out.transpose(1, 0, 2, 3, 4).reshape(B, T, H, v.shape[-1])

def setup_inputs(seed: int = 0) -> dict:
    key = jax.random.key(seed)
    ks = jax.random.split(key, 20)
    f32 = jnp.float32
    L = DEPTH

    def nrm(k, shape, scale):
        return jax.random.normal(k, shape, f32) * scale

    dt = jnp.exp(jax.random.uniform(ks[5], (L, DN_HEADS), f32, math.log(1e-3), math.log(1e-1)))
    return {
        "x": nrm(ks[0], (BATCH, SEQ, D_MODEL), 1.0),
        "attn_norm_w": 1.0 + nrm(ks[1], (L, D_MODEL), 0.02),
        "w_in": nrm(ks[2], (L, D_MODEL, D_IN), D_MODEL ** -0.5),
        "conv_w": nrm(ks[3], (L, CONV_WIDTH, 3 * DN_WIDTH), CONV_WIDTH ** -0.5),
        "a_log": jnp.log(jax.random.uniform(ks[4], (L, DN_HEADS), f32, 1.0, 16.0)),
        "dt_bias": dt + jnp.log(-jnp.expm1(-dt)),
        "dn_norm_w": 1.0 + nrm(ks[6], (L, DN_HEAD_DIM), 0.02),
        "lam_q1": nrm(ks[7], (L, DA_HEAD_DIM), 0.1),
        "lam_k1": nrm(ks[8], (L, DA_HEAD_DIM), 0.1),
        "lam_q2": nrm(ks[9], (L, DA_HEAD_DIM), 0.1),
        "lam_k2": nrm(ks[10], (L, DA_HEAD_DIM), 0.1),
        "da_norm_w": 1.0 + nrm(ks[11], (L, DA_V_DIM), 0.02),
        "w_out": nrm(ks[12], (L, D_MIX, D_MODEL), D_MIX ** -0.5),
        "ffn_norm_w": 1.0 + nrm(ks[13], (L, D_MODEL), 0.02),
        "w_gate": nrm(ks[14], (L, D_MODEL, D_FF), D_MODEL ** -0.5),
        "w_up": nrm(ks[15], (L, D_MODEL, D_FF), D_MODEL ** -0.5),
        "w_down": nrm(ks[16], (L, D_FF, D_MODEL), D_FF ** -0.5),
        "final_norm_w": 1.0 + nrm(ks[17], (D_MODEL,), 0.02),
    }

def reference(x, attn_norm_w, w_in, conv_w, a_log, dt_bias, dn_norm_w, lam_q1, lam_k1, lam_q2, lam_k2,
              da_norm_w, w_out, ffn_norm_w, w_gate, w_up, w_down, final_norm_w):
    B, T, _ = x.shape
    f32 = jnp.float32
    for l in range(DEPTH):
        lam_init = 0.8 - 0.6 * math.exp(-0.3 * l)
        h = rmsnorm(x, attn_norm_w[l])
        proj = h @ w_in[l]

        qkv = jax.nn.silu(causal_depthwise_conv(proj[..., OFF_DN_QKV:OFF_DN_Z], conv_w[l])).astype(f32)
        dq, dk_, dv_ = jnp.split(qkv, 3, axis=-1)
        dq = l2norm(dq.reshape(B, T, DN_HEADS, DN_HEAD_DIM)) * (DN_HEAD_DIM ** -0.5)
        dk_ = l2norm(dk_.reshape(B, T, DN_HEADS, DN_HEAD_DIM))
        dv_ = dv_.reshape(B, T, DN_HEADS, DN_HEAD_DIM)
        z = proj[..., OFF_DN_Z:OFF_DN_B].reshape(B, T, DN_HEADS, DN_HEAD_DIM).astype(f32)
        beta = jax.nn.sigmoid(proj[..., OFF_DN_B:OFF_DN_A].astype(f32))
        g = -jnp.exp(a_log[l].astype(f32)) * jax.nn.softplus(
            proj[..., OFF_DN_A:OFF_DA_Q].astype(f32) + dt_bias[l].astype(f32))
        o_dn = gated_delta_rule(dq, dk_, dv_, g, beta)
        o_dn = rmsnorm(o_dn, dn_norm_w[l]) * jax.nn.silu(z)
        o_dn = o_dn.reshape(B, T, DN_WIDTH).astype(x.dtype)

        qa = proj[..., OFF_DA_Q:OFF_DA_K].reshape(B, T, DA_HEADS, 2, DA_HEAD_DIM)
        ka = proj[..., OFF_DA_K:OFF_DA_V].reshape(B, T, DA_HEADS, 2, DA_HEAD_DIM)
        va = proj[..., OFF_DA_V:D_IN].reshape(B, T, DA_HEADS, DA_V_DIM)
        lam = (jnp.exp(jnp.sum(lam_q1[l].astype(f32) * lam_k1[l].astype(f32)))
               - jnp.exp(jnp.sum(lam_q2[l].astype(f32) * lam_k2[l].astype(f32))) + lam_init)
        o_da = differential_attention(qa, ka, va, lam)
        o_da = rmsnorm(o_da, da_norm_w[l]) * (1.0 - lam_init)
        o_da = o_da.reshape(B, T, DA_WIDTH).astype(x.dtype)

        x = x + jnp.concatenate([o_dn, o_da], axis=-1) @ w_out[l]

        h2 = rmsnorm(x, ffn_norm_w[l])
        x = x + (jax.nn.silu(h2 @ w_gate[l]) * (h2 @ w_up[l])) @ w_down[l]
    return rmsnorm(x, final_norm_w)


_drawn_inputs = setup_inputs


def setup_inputs(seed=0):
    import zlib

    import numpy as np

    out = dict(_drawn_inputs(seed))
    spreads = {}
    factors = {'dn_norm_w': 7.511,
     'lam_k1': 3.54,
     'lam_q2': 3.453,
     'da_norm_w': 5.502,
     'ffn_norm_w': 4.393,
     'final_norm_w': 2.827}
    for name, (base, spread) in spreads.items():
        noise = np.random.default_rng([zlib.crc32(name.encode()), seed]).standard_normal(out[name].shape)
        drawn = base * np.exp(spread * noise) if base else spread * noise
        out[name] = __import__('jax').numpy.asarray(drawn.astype(out[name].dtype))
    for name, factor in factors.items():
        out[name] = (out[name] * factor).astype(out[name].dtype)
    return out
```

```python
import math
from contextlib import ExitStack

import concourse.bass as bass
from concourse import mybir

F32 = mybir.dt.float32
F32R = mybir.dt.float32r
ACT = mybir.ActivationFunctionType
ALU = mybir.AluOpType
AX = mybir.AxisListType

P = 128
T = 512
D = 2048
TB = T // P
KT = D // P
DN_HEADS, DA_HEADS = 8, 4
TAPS = 4
D_FF = 5632
DN_WIDTH = DN_HEADS * P
OFF_Z = 3 * DN_WIDTH
OFF_B = OFF_Z + DN_WIDTH
OFF_Q = OFF_B + 2 * DN_HEADS
OFF_K = OFF_Q + DA_HEADS * 2 * P
OFF_V = OFF_K + DA_HEADS * 2 * P
EPS = 1e-6
LAM_INIT = 0.8 - 0.6 * math.exp(0.0)
FAR = -1e30

UNIT = 2048
HALF = UNIT // 2
SLOTS = 4
LEAD = 3
CHUNKS = 4
FF_GROUPS = D_FF // (4 * P)
U_HEADS = 1
U_ATT = U_HEADS + 4 * DN_HEADS
U_OUT = U_ATT + 6 * DA_HEADS
U_FF = U_OUT + 16
UNITS = U_FF + 12 * FF_GROUPS
HALVES = 2 * UNITS
EXP_WIDTH = P * TB * (TB + 1) // 2

DN_PE = (["k_squares", "q_squares", "gate_rows", "beta_rows", "v_turn", "kk", "kq", "k_turn", "y_turn"]
         + [f"{s}{l}" for l in range(1, 6) for s in ("mx", "xmx", "xmx_turn")] + ["mx6", "xmx_turn6"]
         + ["vn0", "o0", "kv0"] + [f"{s}{c}" for c in (1, 2) for s in ("ks", "vn", "o", "kv")]
         + ["ks3", "vn3", "o3", "o_squares"])
DN_ACT = (["k_square", "q_square", "k_log", "k_rstd", "q_log", "q_rstd", "decay", "decay_start", "decay_end", "x0"]
          + [f"mx{l}" for l in range(1, 7)] + [f"vn{c}" for c in range(4)] + ["o_square", "o_log", "o_rstd"])
DN_DVE = (["gate_pick", "beta_pick", "columns", "k", "q", "gaps", "gap_end", "decay_mask", "decay_beta", "m", "a",
           "bv", "k_dec", "chunk_decay", "q_dec"]
          + [s for l in range(1, 6) for s in (f"x{l}", f"y{l}")] + ["y6"]
          + ["s0"] + [s for c in (1, 2) for s in (f"r{c}", f"s{c}")] + ["r3", "o_scaled", "o"])
DN_POOL = ["level0", "y0"] + [f"level{l}" for l in range(1, 7)]

SC = [(m, qb) for m in range(2) for qb in range(TB)]
AT_PE = (["v_turn0", "v_turn1"] + [f"score{i}" for i in range(8)] + [f"p_turn{k}" for k in range(TB)]
         + ["pv0", "pv1", "squares"])
AT_ACT = (["v0", "v1"] + [f"exp{i}" for i in range(8)] + [f"p{k}" for k in range(TB)]
          + ["square0", "square1", "log", "rstd"])
AT_DVE = (["bias"] + [s for i in range(8) for s in (f"score{i}", f"max{i}")] + ["rsum", "rsum_lam"]
          + [s for q in range(TB) for s in (f"p_low{q}", f"p{q}")] + ["o0", "o1"])


PT_OFF = [sum(TB - i for i in range(k)) * P for k in range(TB)]


def ex_block(qb):
    return slice(P * qb * (qb + 1) // 2, P * (qb + 1) * (qb + 2) // 2)


def after(steps, head, name):
    return head * len(steps) + steps.index(name) + 1 + FIRST[id(steps)]


CONSTS = 3 + 3 * 7 + 2 + DA_HEADS
FIRST = {id(DN_PE): 0, id(DN_ACT): 0, id(DN_DVE): 1, id(DN_POOL): 0, id(AT_PE): 0, id(AT_ACT): 0, id(AT_DVE): 1}


def all_done(steps, heads):
    return heads * len(steps) + FIRST[id(steps)]


def build(nc, x, attn_norm_w, w_in, conv_w, a_log, dt_bias, dn_norm_w, lam_q1, lam_k1, lam_q2, lam_k2,
          da_norm_w, w_out, ffn_norm_w, w_gate, w_up, w_down, final_norm_w, out):
    stack = ExitStack()

    def sb(name, shape, dt=F32, where=stack):
        return where.enter_context(nc.sbuf_tensor(name, shape, dt))

    def sem(name):
        return stack.enter_context(nc.semaphore(name))

    with stack:
        bank = [stack.enter_context(nc.psum_tensor(f"bank{i}", [P, 512], F32)) for i in range(8)]

        raw = sb("raw", [P, 2, UNIT])
        w_high = sb("w_high", [P, SLOTS, HALF], F32R)
        w_low = sb("w_low", [P, SLOTS, HALF], F32R)
        h_high = sb("h_high", [P, KT, T], F32R)
        h_low = sb("h_low", [P, KT, T], F32R)
        x1 = sb("x1", [P, TB, D])
        mix = x1[:].rearrange("p t (k n) -> p (t k) n", n=T)
        ident = sb("ident", [P, P])
        ones = sb("ones", [P, P])
        small = sb("small", [P, 64])
        conv_rows = sb("conv_rows", [P, P])
        conv_t = sb("conv_t", [P, TAPS, 3, DN_HEADS])
        dn_w = sb("dn_w", [P, 1])
        da_w = sb("da_w", [P, 2])
        lam_v = sb("lam_v", [P, 4, P])
        slopes = sb("slopes", [P, DA_HEADS])
        base_bias = sb("base_bias", [P, T])
        incl = sb("incl", [P, P])
        levels = sb("levels", [P, 7, P])
        sum_sq = small[:, 0:4]
        rstd_log = small[:, 4:8]
        rstd = small[:, 8:12]
        lam_dot = small[:, 12:14]
        lam_exp = small[:, 14:16]
        lam = small[:, 16:17]
        rate = small[:, 17:18]
        dt_col = small[:, 18:19]
        alog_col = small[:, 19:20]

        heads = ExitStack()
        stack.enter_context(heads)
        pre = sb("pre", [P, 6, T], where=heads)
        deltanet = ExitStack()
        heads.enter_context(deltanet)
        d = lambda name, shape: sb(name, shape, where=deltanet)
        conv_acc = d("conv_acc", [P, T])
        gates = d("gates", [16, T])
        betas = d("betas", [16, T])
        head_cols = d("head_cols", [P, 12, DN_HEADS])
        cols = d("cols", [P, 12])
        taps = d("taps", [P, TAPS, 3])
        ba_t = d("ba_t", [P, 8, 16])
        picked = d("picked", [16, 2, T])
        sq = d("sq", [P, 2, T])
        rs = d("rs", [P, 2, T])
        kT, qT = d("kT", [P, T]), d("qT", [P, T])
        decay = d("decay", [P, T])
        m_t = d("m_t", [P, T])
        q_dec = d("q_dec", [P, T])
        k_dec, bv = d("k_dec", [P, T]), d("bv", [P, T])
        level_m, mxs = sq, rs[:, 1, :]
        xi, yi = d("xi", [P, T]), d("yi", [P, T])
        state, resid = d("state", [P, P]), d("resid", [P, P])
        v_new = d("v_new", [P, 2, P])
        ends = d("ends", [P, 3, TB])
        deltanet.close()
        attention = ExitStack()
        heads.enter_context(attention)
        a = lambda name, shape: sb(name, shape, where=attention)
        v_tok = a("v_tok", [P, TB, 2 * P])
        ex = a("ex", [P, 2, EXP_WIDTH])
        p_t = a("p_t", [P, EXP_WIDTH])
        bias_h = a("bias_h", [P, T])
        att_sq = a("att_sq", [P, 2, T])
        att_rs = a("att_rs", [P, 2, T])
        att_o = a("att_o", [P, 2, T])
        neg_max = a("neg_max", [P, 8])
        row_sum = a("row_sum", [P, 8])
        inv_sum = a("inv_sum", [P, 8])
        attention.close()
        heads.close()
        norms = ExitStack()
        stack.enter_context(norms)
        w_row = sb("w_row", [P, D], where=norms)
        xn = sb("xn", [P, 2, D], where=norms)
        norms.close()
        ffn = ExitStack()
        stack.enter_context(ffn)
        hid_high = sb("hid_high", [P, 4, T], F32R, where=ffn)
        hid_low = sb("hid_low", [P, 4, T], F32R, where=ffn)
        gate_act = sb("gate_act", [P, 2, T], where=ffn)
        hidden = sb("hidden", [P, 2, T], where=ffn)
        ffn.close()

        raw_landed = [sem("raw_landed0"), sem("raw_landed1")]
        w_high_ready = sem("w_high_ready")
        w_low_ready = sem("w_low_ready")
        chunks_done = sem("chunks_done")
        x_landed = [sem(f"x_landed{t}") for t in range(TB)]
        row_landed = sem("row_landed")
        params_landed = sem("params_landed")
        const_step = sem("const_step")
        dve_const = sem("dve_const")
        norm_sq = sem("norm_sq")
        norm_log = sem("norm_log")
        norm_rstd = sem("norm_rstd")
        norm_scaled = sem("norm_scaled")
        norm_turned = sem("norm_turned")
        norm_high = sem("norm_high")
        norm_low = sem("norm_low")
        conv_first = sem("conv_first")
        conv_tap = sem("conv_tap")
        pre_ready = sem("pre_ready")
        att_pre_ready = sem("att_pre_ready")
        param_turned = sem("param_turned")
        conv_ready = sem("conv_ready")
        taps_ready = sem("taps_ready")
        lam_step = sem("lam_step")
        lam_act = sem("lam_act")
        ba_act = sem("ba_act")
        ba_dve = sem("ba_dve")
        ba_turned = sem("ba_turned")
        dn_pe, dn_act, dn_dve, dn_pool = sem("dn_pe"), sem("dn_act"), sem("dn_dve"), sem("dn_pool")
        at_pe, at_act, at_dve = sem("at_pe"), sem("at_act"), sem("at_dve")
        mix_high = sem("mix_high")
        mix_low = sem("mix_low")
        out_added = sem("out_added")
        gate_ready = sem("gate_ready")
        hid_ready = sem("hid_ready")
        hid_high_ready = sem("hid_high_ready")
        hid_low_ready = sem("hid_low_ready")
        stored = sem("stored")

        by_k = lambda w: w[0].rearrange("(k p) n -> p k n", p=P)
        in_v, gate_v, up_v = by_k(w_in), by_k(w_gate), by_k(w_up)
        out_v, down_v = by_k(w_out), by_k(w_down)

        def in_column(kind, head):
            return {"q": 0, "k": DN_WIDTH, "v": 2 * DN_WIDTH, "z": OFF_Z}[kind] + head * P

        def att_column(u, head):
            return (OFF_V, OFF_V + P, OFF_Q, OFF_K, OFF_Q + P, OFF_K + P)[u] + head * 2 * P

        OUT_BANKS = (0, 1, 6, 7)

        block = stack.enter_context(nc.Block())

        def count(span, j, scale=1, plus=0):
            base, i, per = span
            return scale * (base + j) + plus + i * (per * scale)

        def last_halves(span, j):
            return isinstance(span[1], int) and count(span, j + LEAD) >= HALVES

        def half_done(eng, span, j):
            eng.wait_ge(chunks_done, count(span, j + 1, CHUNKS))

        def chunk_done(eng, span, j, c):
            eng.wait_ge(chunks_done, count(span, j, CHUNKS, c + 1))

        S_HEADS = lambda h: (2 * U_HEADS, h, 8)
        S_ATT = lambda n: (2 * U_ATT, n, 12)
        S_OUT0 = (2 * U_OUT, 0, 4)
        S_OUT1 = lambda g: (2 * U_OUT + 16, g, 4)
        S_FF0 = (2 * U_FF, 0, 24)
        S_FF = lambda n: (2 * U_FF + 16 - 24, n, 24)
        S_END = (HALVES - 8, 0, 8)
        PARAMS = 16 * 10
        by_chunk = lambda t: t.rearrange("p (c i) -> p c i", c=TB)

        @block.sync
        def _(sp):
            def load(u, slot, src, blocks=KT):
                if not isinstance(u, int) or u >= 2:
                    sp.wait_ge(w_low_ready, 2 * u - 2)
                sp.dma_start(raw[:, slot, :].rearrange("p (k n) -> p k n", k=blocks), src
                             ).then_inc(raw_landed[slot], 16)

            def columns(view, col):
                return view[:, :, bass.ds(col, P)]

            def load_head(h):
                for j, kind in enumerate("qkvz"):
                    load(4 * h + U_HEADS + j, (U_HEADS + j) % 2, columns(in_v, in_column(kind, h)))

            def load_attention(n):
                for j in range(6):
                    load(6 * n + U_ATT + j, (U_ATT + j) % 2, columns(in_v, att_column(j, n)))

            def load_out(g, half_k):
                for j in range(2):
                    load(2 * g + U_OUT + 8 * half_k + j, (U_OUT + j) % 2,
                         out_v[:, 8 * half_k + 4 * j:8 * half_k + 4 * j + 4, bass.ds(g * T, T)], 4)

            def load_pair(u, n, fb):
                load(u, U_FF % 2, columns(gate_v, n * (4 * P) + fb * P))
                load(u + 1, 1 - U_FF % 2, columns(up_v, n * (4 * P) + fb * P))

            def load_down(u, n):
                for c in range(4):
                    load(u + c, (U_FF + c) % 2, down_v[:, bass.ds(n * 4, 4), c * T:(c + 1) * T], 4)

            load(0, 0, columns(in_v, OFF_B))
            load_head(0)
            with sp.Fori(1, DN_HEADS) as h:
                load_head(h)
            with sp.Fori(0, DA_HEADS) as n:
                load_attention(n)
            for half_k in range(2):
                with sp.Fori(0, 4) as g:
                    load_out(g, half_k)
            for fb in range(4):
                load_pair(U_FF + 2 * fb, 0, fb)
            with sp.Fori(1, FF_GROUPS) as n:
                u = 12 * n + (U_FF + 8 - 12)
                load_pair(u, n, 0)
                load_down(u + 2, n - 1)
                for fb in range(1, 4):
                    load_pair(u + 4 + 2 * fb, n, fb)
            load_down(UNITS - 4, FF_GROUPS - 1)
            for t in range(TB):
                sp.wait_ge(norm_scaled, 2 * TB + t + 1)
                sp.dma_start(out[0, t * P:(t + 1) * P, :], x1[:, t, :]).then_inc(stored, 16)
            sp.wait_ge(stored, 16 * TB)

        @block.gpsimd
        def _(pool):
            steps = [0]

            def const(ins):
                ins.then_inc(const_step, 1)
                steps[0] += 1
                pool.wait_ge(const_step, steps[0])

            const(pool.memset(ident[:], 0.0))
            const(pool.affine_select(out=ident[:], in_=ident[:], compare_op=ALU.not_equal, fill=1.0, base=0,
                                     pattern=[[-1, P]], channel_multiplier=1))
            pool.wait_ge(dve_const, 1)
            const(pool.affine_select(out=incl[:], in_=ones[:], compare_op=ALU.is_ge, fill=0.0, base=0,
                                     pattern=[[1, P]], channel_multiplier=-1))
            for l in range(7):
                s = 1 << l
                odd = levels[:, l, :].rearrange("p (g b s) -> p g b s", b=2, s=s)[:, :, 1, :]
                src = ones[:].rearrange("p (g b s) -> p g b s", b=2, s=s)[:, :, 1, :]
                const(pool.memset(levels[:, l, :], 0.0))
                const(pool.affine_select(out=odd, in_=src, compare_op=ALU.is_ge, fill=0.0, base=0,
                                         pattern=[[-2 * s, P // (2 * s)], [0, s]], channel_multiplier=1))
                const(pool.affine_select(out=odd, in_=odd, compare_op=ALU.is_ge, fill=0.0, base=s - 1,
                                         pattern=[[2 * s, P // (2 * s)], [0, s]], channel_multiplier=-1))
            const(pool.iota(base_bias[:], pattern=[[1, T]], base=P - T, channel_multiplier=-1,
                            allow_small_or_imprecise_dtypes=True))
            const(pool.affine_select(out=base_bias[:], in_=base_bias[:], compare_op=ALU.is_ge, fill=FAR, base=T - P,
                                     pattern=[[-1, T]], channel_multiplier=1))
            for n in range(DA_HEADS):
                const(pool.memset(slopes[:, n:n + 1], 2.0 ** (-8.0 * (n + 1) / DA_HEADS)))
            assert steps[0] == CONSTS

            def mask(l):
                return levels[:, l:l + 1, :].to_broadcast([P, TB, P])

            with pool.Fori(0, DN_HEADS) as h:
                pool.wait_ge(dn_dve, after(DN_DVE, h, "m"))
                pool.tensor_tensor(by_chunk(level_m[:, 0, :]), by_chunk(m_t[:]), mask(0), ALU.mult).then_inc(dn_pool, 1)
                pool.wait_ge(dn_pool, after(DN_POOL, h, "level0"))
                pool.tensor_tensor(by_chunk(yi[:]), ident[:].rearrange("p (c i) -> p c i", c=1).to_broadcast([P, TB, P]),
                                   by_chunk(level_m[:, 0, :]), ALU.subtract).then_inc(dn_pool, 1)
                for l in range(1, 7):
                    if l >= 3:
                        pool.wait_ge(dn_pe, after(DN_PE, h, f"mx{l - 2}"))
                    if l == 2:
                        pool.wait_ge(dn_pool, after(DN_POOL, h, "y0"))
                    pool.tensor_tensor(by_chunk(level_m[:, l % 2, :]), by_chunk(m_t[:]), mask(l), ALU.mult
                                       ).then_inc(dn_pool, 1)

        @block.scalar
        def _(act):
            A = nc.scalar.activation

            def high(span, j):
                if last_halves(span, j):
                    return
                s = span[0] + j + LEAD
                act.wait_ge(raw_landed[(s // 2) % 2], 16 * (s // 4 + 1) + span[1] * (span[2] * 4))
                if not isinstance(span[1], int) or s >= SLOTS:
                    half_done(act, span, j + LEAD - SLOTS)
                A(w_high[:, s % SLOTS, :], raw[:, (s // 2) % 2, (s % 2) * HALF:(s % 2 + 1) * HALF], ACT.Copy
                  ).then_inc(w_high_ready, 1)

            for t in range(TB):
                act.dma_start(x1[:, t, :], x[0, t * P:(t + 1) * P, :]).then_inc(x_landed[t], 16)
                if t == 0:
                    act.dma_start(w_row[:], attn_norm_w[0:1, :].to_broadcast([P, D])).then_inc(row_landed, 16)
            act.dma_start(conv_rows[0:TAPS * 24, :], conv_w[0].rearrange("t (b c) -> (t b) c", c=P)).then_inc(params_landed, 16)
            act.dma_start(dn_w[:], dn_norm_w[0].rearrange("(c a) -> c a", a=1)).then_inc(params_landed, 16)
            for e in range(2):
                act.dma_start(da_w[:, e:e + 1], da_norm_w[0, e * P:(e + 1) * P].rearrange("(c a) -> c a", a=1)
                              ).then_inc(params_landed, 16)
            for i, v in enumerate((lam_q1, lam_k1, lam_q2, lam_k2)):
                act.dma_start(lam_v[:, i, :], v[0:1, :].to_broadcast([P, P])).then_inc(params_landed, 16)
            act.wait_ge(dve_const, 2)
            act.dma_start(dt_col[8:16, :], dt_bias[0].rearrange("(c a) -> c a", a=1)).then_inc(params_landed, 16)
            act.dma_start(alog_col[8:16, :], a_log[0].rearrange("(c a) -> c a", a=1)).then_inc(params_landed, 16)

            def norm(r, turned=True):
                def high_parts(t):
                    for g in range(4):
                        act.wait_ge(norm_turned, 16 * r + 4 * t + g + 1)
                        A(h_high[:, 4 * g:4 * g + 4, t * P:(t + 1) * P],
                          bank[2 + g][:].rearrange("p (k i) -> p k i", k=4), ACT.Copy).then_inc(norm_high, 1)

                for t in range(TB):
                    if r == 0:
                        act.wait_ge(x_landed[t], 16)
                    if t >= 2 and turned:
                        act.wait_ge(norm_turned, 16 * r + 4 * (t - 1))
                    elif t >= 2:
                        act.wait_ge(norm_sq, TB * r + t - 1)
                    A(xn[:, t % 2, :], x1[:, t, :], ACT.Square, accum_out=sum_sq[:, t:t + 1]).then_inc(norm_sq, 1)
                    act.wait_ge(norm_sq, TB * r + t + 1)
                    A(rstd_log[:, t:t + 1], sum_sq[:, t:t + 1], ACT.Ln, scale=1.0 / D, bias=EPS).then_inc(norm_log, 1)
                    act.wait_ge(norm_log, TB * r + t + 1)
                    if r > 0:
                        act.wait_ge(norm_scaled, TB * (r - 1) + t + 1)
                    A(rstd[:, t:t + 1], rstd_log[:, t:t + 1], ACT.Exp, scale=-0.5).then_inc(norm_rstd, 1)
                    if turned and t > 0:
                        high_parts(t - 1)
                if turned:
                    high_parts(TB - 1)

            for j in range(-LEAD, 0):
                high((0, 0, 4), j)
            norm(0)

            act.wait_ge(lam_step, 4)
            A(lam_exp, lam_dot, ACT.Exp).then_inc(lam_act, 1)
            act.wait_ge(params_landed, PARAMS)
            A(rate, alog_col, ACT.Exp).then_inc(lam_act, 1)
            high((0, 0, 4), 0)
            high((0, 0, 4), 1)

            def gates_beta():
                half_done(act, (0, 0, 4), 1)
                A(betas[:], bank[0][0:16, :], ACT.Exp, scale=-1.0).then_inc(ba_act, 1)
                A(picked[:, 0, :], bank[0][0:16, :], ACT.Abs, bias=dt_col[0:16, :]).then_inc(ba_act, 1)
                act.wait_ge(ba_act, 2)
                A(picked[:, 1, :], picked[:, 0, :], ACT.Exp, scale=-1.0).then_inc(ba_act, 1)
                act.wait_ge(ba_act, 3)
                A(picked[:, 0, :], picked[:, 1, :], ACT.Ln, bias=1.0).then_inc(ba_act, 1)

            def gate_columns():
                act.wait_ge(ba_turned, 1)
                A(ba_t[:], bank[2][:, 0:P].rearrange("p (c r) -> p c r", r=16), ACT.Copy).then_inc(ba_act, 1)
                act.wait_ge(ba_act, 5)
                A(head_cols[:, 8:12, :], ba_t[:, 0:4, 8:16], ACT.Exp).then_inc(ba_act, 1)

            def z_out(h):
                act.wait_ge(dn_dve, all_done(DN_DVE, h))
                A(pre[:, 3, :], bank[0][:], ACT.Silu).then_inc(pre_ready, 1)

            def conv_start(h, j):
                act.wait_ge(taps_ready, h + 1)
                if not isinstance(h, int) or h > 0 or j > 0:
                    act.wait_ge(pre_ready, 4 * h + j)
                A(conv_acc[:], bank[(U_HEADS + j) % 2][:], ACT.Copy, scale=taps[:, TAPS - 1, j:j + 1]
                  ).then_inc(conv_first, 1)

            def conv_end(h, j):
                act.wait_ge(conv_tap, 9 * h + 3 * j + 3)
                if not isinstance(h, int):
                    if j < 2:
                        act.wait_ge(dn_dve, after(DN_DVE, h - 1, "q"))
                    else:
                        act.wait_ge(dn_pe, after(DN_PE, h - 1, "v_turn"))
                A(pre[:, j, :], conv_acc[:], ACT.Silu).then_inc(pre_ready, 1)

            def dn(gap, h):
                def pe(name):
                    act.wait_ge(dn_pe, after(DN_PE, h, name))

                def dve(name):
                    act.wait_ge(dn_dve, after(DN_DVE, h, name))

                def own(name):
                    act.wait_ge(dn_act, after(DN_ACT, h, name))

                if gap == 0:
                    act.wait_ge(pre_ready, 4 * h + 3)
                    A(sq[:, 0, :], pre[:, 1, :], ACT.Square).then_inc(dn_act, 1)
                    A(sq[:, 1, :], pre[:, 0, :], ACT.Square).then_inc(dn_act, 1)
                if gap == 1:
                    pe("k_squares")
                    A(rs[:, 0, :], bank[2][:], ACT.Ln, bias=EPS).then_inc(dn_act, 1)
                    own("k_log")
                    A(rs[:, 0, :], rs[:, 0, :], ACT.Exp, scale=-0.5).then_inc(dn_act, 1)
                    pe("q_squares")
                    A(rs[:, 1, :], bank[3][:], ACT.Ln, bias=EPS).then_inc(dn_act, 1)
                    own("q_log")
                    A(rs[:, 1, :], rs[:, 1, :], ACT.Exp, scale=-0.5, bias=-0.5 * math.log(P)).then_inc(dn_act, 1)
                if gap == 3:
                    dve("gaps")
                    A(decay[:], decay[:], ACT.Exp).then_inc(dn_act, 1)
                    dve("gap_end")
                    A(q_dec[:], bank[4][:], ACT.Exp).then_inc(dn_act, 1)
                    A(ends[:, 1, :], ends[:, 0, :], ACT.Exp).then_inc(dn_act, 1)
                if gap == 7:
                    pe("y_turn")
                    A(xi[:], bank[2][:], ACT.Copy).then_inc(dn_act, 1)
                for l in range(1, 7):
                    if gap == 6 + 2 * l:
                        pe(f"mx{l}")
                        A(mxs, bank[3][:], ACT.Copy).then_inc(dn_act, 1)
                for c in range(TB):
                    if gap == 20 + 3 * c:
                        pe(f"vn{c}")
                        A(v_new[:, c % 2, :], bank[6][:, c * P:(c + 1) * P], ACT.Copy).then_inc(dn_act, 1)
                if gap == 30:
                    pe("o3")
                    A(sq[:, 0, :], bank[3][:], ACT.Square).then_inc(dn_act, 1)
                if gap == 31:
                    pe("o_squares")
                    A(rs[:, 0, :], bank[5][:], ACT.Ln, scale=1.0 / P, bias=EPS).then_inc(dn_act, 1)
                    own("o_log")
                    A(rs[:, 0, :], rs[:, 0, :], ACT.Exp, scale=-0.5).then_inc(dn_act, 1)

            def att_out(n, u):
                if u == 5:
                    pass
                elif not isinstance(n, int) or n > 0:
                    reader = ("v_turn0", "v_turn1", "score3", "score3", "score7")[u]
                    act.wait_ge(at_pe, after(AT_PE, n - 1, reader))
                elif u < 2:
                    act.wait_ge(dn_dve, after(DN_DVE, DN_HEADS - 1, "q"))
                elif u == 2:
                    act.wait_ge(dn_pe, after(DN_PE, DN_HEADS - 1, "v_turn"))
                elif u == 3:
                    act.wait_ge(dn_dve, all_done(DN_DVE, DN_HEADS))
                A(pre[:, u, :], bank[(U_ATT + u) % 2][:], ACT.Copy).then_inc(att_pre_ready, 1)

            def att(gap, n):
                def pe(name):
                    act.wait_ge(at_pe, after(AT_PE, n, name))

                if gap == 0:
                    for e in range(2):
                        pe(f"v_turn{e}")
                        A(v_tok[:, :, e * P:(e + 1) * P], bank[2 + e][:].rearrange("p (b c) -> p b c", b=TB), ACT.Copy
                          ).then_inc(at_act, 1)
                for i, (m, qb) in enumerate(SC):
                    if gap == 2 + 2 * i:
                        act.wait_ge(at_dve, after(AT_DVE, n, f"max{i}"))
                        e = ex[:, m, ex_block(qb)]
                        A(e, e, ACT.Exp, bias=neg_max[:, i:i + 1], accum_out=row_sum[:, i:i + 1]).then_inc(at_act, 1)
                for k in range(TB):
                    if gap == 22 + 2 * k:
                        pe(f"p_turn{k}")
                        w = (TB - k) * P
                        A(p_t[:, PT_OFF[k]:PT_OFF[k] + w], bank[2 + k % 2][:, 0:w], ACT.Copy).then_inc(at_act, 1)
                if gap == 31:
                    for e in range(2):
                        pe(f"pv{e}")
                        A(att_sq[:, e, :], bank[4 + e][:], ACT.Square).then_inc(at_act, 1)
                if gap == 33:
                    pe("squares")
                    A(att_rs[:, 0, :], bank[2][:], ACT.Ln, scale=1.0 / (2 * P), bias=EPS).then_inc(at_act, 1)
                    act.wait_ge(at_act, after(AT_ACT, n, "log"))
                    A(att_rs[:, 1, :], att_rs[:, 0, :], ACT.Exp, scale=-0.5).then_inc(at_act, 1)

            def head_window(h, before):
                span = S_HEADS(h)
                for gap in range(8 * CHUNKS):
                    if gap % CHUNKS == 0:
                        high(span, gap // CHUNKS)
                    if before is None:
                        if gap == 0:
                            gates_beta()
                        if gap == 4:
                            gate_columns()
                    else:
                        if gap == 0:
                            z_out(before)
                        dn(gap, before)
                    for j in range(3):
                        if gap == 8 * (j + 1):
                            half_done(act, span, 2 * j + 1)
                            conv_start(h, j)
                        if gap == 8 * (j + 1) + 3:
                            conv_end(h, j)

            head_window(0, None)
            with act.Fori(1, DN_HEADS) as h:
                head_window(h, h - 1)

            def att_window(n, before):
                span = S_ATT(n)
                for gap in range(12 * CHUNKS):
                    if gap % CHUNKS == 0:
                        high(span, gap // CHUNKS)
                    if before is None:
                        if gap == 0:
                            z_out(DN_HEADS - 1)
                        if gap < 32:
                            dn(gap, DN_HEADS - 1)
                    else:
                        if gap == 0:
                            half_done(act, span, -1)
                            att_out(before, 5)
                        att(gap, before)
                    for u in range(5):
                        if gap == 8 * (u + 1) + 1:
                            half_done(act, span, 2 * u + 1)
                            att_out(n, u)

            att_window(0, None)
            with act.Fori(1, DA_HEADS) as n:
                att_window(n, n - 1)

            half_done(act, S_OUT0, -1)
            att_out(DA_HEADS - 1, 5)
            act.wait_ge(at_dve, all_done(AT_DVE, DA_HEADS - 1))
            for k in range(0, KT - 2, 2):
                A(h_high[:, k:k + 2, :], mix[:, k:k + 2, :], ACT.Copy).then_inc(mix_high, 1)
            act.wait_ge(mix_low, 7)
            for t in range(TB):
                act.dma_start(x1[:, t, :], x[0, t * P:(t + 1) * P, :]).then_inc(x_landed[t], 16)
            for gap in range(16 * CHUNKS):
                if gap % CHUNKS == 0:
                    high(S_OUT0, gap // CHUNKS)
                att(gap, DA_HEADS - 1)
                if gap == 35:
                    for e in range(2):
                        act.wait_ge(at_dve, after(AT_DVE, DA_HEADS - 1, f"o{e}"))
                        A(h_high[:, KT - 2 + e, :], att_o[:, e, :], ACT.Copy).then_inc(mix_high, 1)
            act.dma_start(w_row[:], ffn_norm_w[0:1, :].to_broadcast([P, D])).then_inc(row_landed, 16)
            with act.Fori(0, 4) as g:
                for j in range(4):
                    high(S_OUT1(g), j)
            act.wait_ge(out_added, 32)
            norm(1)

            def gate_out(n, fb):
                if not isinstance(n, int) or 4 * n + fb >= 2:
                    act.wait_ge(hid_ready, 4 * n + fb - 1)
                A(gate_act[:, fb % 2, :], bank[2 + 2 * (fb % 2)][:], ACT.Silu).then_inc(gate_ready, 1)

            def hidden_high(n, fb):
                act.wait_ge(hid_ready, 4 * n + fb + 1)
                A(hid_high[:, fb, :], hidden[:, fb % 2, :], ACT.Copy).then_inc(hid_high_ready, 1)

            for j in range(16):
                high(S_FF0, j)
                if j % 4 == 2:
                    half_done(act, S_FF0, j - 1)
                    gate_out(0, j // 4)
                if j % 4 == 0 and j > 0:
                    hidden_high(0, j // 4 - 1)
            with act.Fori(1, FF_GROUPS) as n:
                span = S_FF(n)
                for j in range(24):
                    high(span, j)
                    if j == 0:
                        hidden_high(n - 1, 3)
                    if j in (2, 14, 18, 22):
                        half_done(act, span, j - 1)
                        gate_out(n, (j - 10) // 4 if j > 2 else 0)
                    if j == 12:
                        half_done(act, span, 11)
                    if j in (12, 16, 20):
                        hidden_high(n, (j - 12) // 4)
            hidden_high(FF_GROUPS - 1, 3)
            for j in range(8):
                high(S_END, j)
            act.wait_ge(out_added, 32 + 16 * FF_GROUPS)
            act.dma_start(w_row[:], final_norm_w.rearrange("(a n) -> a n", a=1).to_broadcast([P, D])
                          ).then_inc(row_landed, 16)
            norm(2, turned=False)

        @block.vector
        def _(dve):
            V = nc.vector

            def low(span, j):
                if last_halves(span, j):
                    return
                s = span[0] + j + LEAD
                dve.wait_ge(w_high_ready, count(span, j + LEAD + 1))
                V.tensor_tensor(w_low[:, s % SLOTS, :], raw[:, (s // 2) % 2, (s % 2) * HALF:(s % 2 + 1) * HALF],
                                w_high[:, s % SLOTS, :].bitcast(F32), ALU.subtract).then_inc(w_low_ready, 1)

            V.memset(ones[:], 1.0).then_inc(dve_const, 1)
            V.memset(small[:], 0.0).then_inc(dve_const, 1)
            V.memset(state[:], 0.0).then_inc(dn_dve, 1)
            V.memset(resid[:], 0.0).then_inc(at_dve, 1)

            def norm(r, turned=True):
                def low_parts(t):
                    for g in range(4):
                        dve.wait_ge(norm_high, 16 * r + 4 * t + g + 1)
                        at = (slice(None), slice(4 * g, 4 * g + 4), slice(t * P, (t + 1) * P))
                        V.tensor_tensor(h_low[at], bank[2 + g][:].rearrange("p (k i) -> p k i", k=4),
                                        h_high[at].bitcast(F32), ALU.subtract).then_inc(norm_low, 1)

                dve.wait_ge(row_landed, 16 * (r + 1))
                for t in range(TB):
                    dve.wait_ge(norm_rstd, TB * r + t + 1)
                    if turned and t >= 2:
                        dve.wait_ge(norm_turned, 16 * r + 4 * (t - 1))
                    to = xn[:, t % 2, :] if turned else x1[:, t, :]
                    V.scalar_tensor_tensor(out=to, in0=x1[:, t, :], scalar=rstd[:, t:t + 1], in1=w_row[:],
                                           op0=ALU.mult, op1=ALU.mult).then_inc(norm_scaled, 1)
                    if turned and t > 0:
                        low_parts(t - 1)
                if turned:
                    low_parts(TB - 1)

            for j in range(-LEAD, 0):
                low((0, 0, 4), j)
            norm(0)

            dve.wait_ge(params_landed, PARAMS)
            for i in range(2):
                V.tensor_tensor(lam_v[:, 2 * i, :], lam_v[:, 2 * i, :], lam_v[:, 2 * i + 1, :], ALU.mult).then_inc(lam_step, 1)
                dve.wait_ge(lam_step, 2 * i + 1)
                V.tensor_reduce(lam_dot[:, i:i + 1], lam_v[:, 2 * i, :], AX.X, ALU.add).then_inc(lam_step, 1)
            dve.wait_ge(lam_act, 1)
            V.scalar_tensor_tensor(out=lam, in0=lam_exp[:, 0:1], scalar=LAM_INIT, in1=lam_exp[:, 1:2],
                                   op0=ALU.add, op1=ALU.subtract).then_inc(lam_step, 1)
            V.tensor_scalar(da_w[:], da_w[:], 1.0 - LAM_INIT, None, ALU.mult).then_inc(lam_step, 1)
            dve.wait_ge(param_turned, 1)
            V.tensor_copy(conv_t[:].rearrange("p t j h -> p (t j h)"), bank[7][:, 0:TAPS * 24]).then_inc(conv_ready, 1)
            low((0, 0, 4), 0)
            low((0, 0, 4), 1)

            def pick_taps(h):
                if isinstance(h, int):
                    dve.wait_ge(conv_ready, 1)
                else:
                    dve.wait_ge(conv_first, 3 * h)
                V.tensor_scalar(taps[:], conv_t[:, :, :, bass.ds(h, 1)].rearrange("p t j a -> p t (j a)"), 1.0, None,
                                ALU.mult).then_inc(taps_ready, 1)

            def gates_beta():
                steps = [0]

                def step(ins):
                    ins.then_inc(ba_dve, 1)
                    steps[0] += 1
                    dve.wait_ge(ba_dve, steps[0])

                half_done(dve, (0, 0, 4), 1)
                dve.wait_ge(ba_act, 2)
                step(V.tensor_scalar(gates[:], bank[0][0:16, :], dt_col[0:16, :], 0.0, ALU.add, ALU.max))
                step(V.tensor_scalar(betas[:], betas[:], 1.0, None, ALU.add))
                step(V.reciprocal(betas[:], betas[:]))
                dve.wait_ge(ba_act, 4)
                dve.wait_ge(lam_act, 2)
                step(V.tensor_tensor(picked[:, 0, :], gates[:], picked[:, 0, :], ALU.add))
                step(V.tensor_scalar(picked[:, 1, :], picked[:, 0, :], rate[0:16, :], -1.0, ALU.mult, ALU.mult))
                for c in range(TB):
                    at = slice(c * P, (c + 1) * P)
                    last = V.tensor_tensor_scan(gates[:, at], ones[0:16, :], picked[:, 1, at], 0.0, ALU.mult, ALU.add)
                step(last)
                assert steps[0] == 6

            def gate_columns():
                dve.wait_ge(ba_act, 6)
                V.tensor_copy(head_cols[:, 0:4, :], ba_t[:, 0:4, 8:16]).then_inc(ba_dve, 1)
                V.tensor_copy(head_cols[:, 4:8, :], ba_t[:, 4:8, 0:8]).then_inc(ba_dve, 1)
                V.scalar_tensor_tensor(out=head_cols[:, 8:12, :], in0=head_cols[:, 8:12, :], scalar=-1.0,
                                       in1=ba_t[:, 4:8, 0:8], op0=ALU.mult, op1=ALU.mult).then_inc(ba_dve, 1)

            def conv(h, j, k):
                if k == 1:
                    dve.wait_ge(conv_first, 3 * h + j + 1)
                else:
                    dve.wait_ge(conv_tap, 9 * h + 3 * j + k - 1)
                V.scalar_tensor_tensor(out=conv_acc[:, k:T], in0=bank[(U_HEADS + j) % 2][:, 0:T - k],
                                       scalar=taps[:, TAPS - 1 - k, j:j + 1], in1=conv_acc[:, k:T],
                                       op0=ALU.mult, op1=ALU.add).then_inc(conv_tap, 1)

            gate_col, beta_col, nbg_col = cols[:, 0:4], cols[:, 4:8], cols[:, 8:12]
            spread = lambda col: col.rearrange("p (c a) -> p c a", a=1).to_broadcast([P, TB, P])

            def dn(gap, h):
                def pe(name):
                    dve.wait_ge(dn_pe, after(DN_PE, h, name))

                def act(name):
                    dve.wait_ge(dn_act, after(DN_ACT, h, name))

                def own(name):
                    dve.wait_ge(dn_dve, after(DN_DVE, h, name))

                if gap == 0:
                    if isinstance(h, int):
                        pass
                    dve.wait_ge(ba_dve, 9)
                    row = ident[0:16, bass.ds(h + 8, 1)]
                    V.tensor_scalar(picked[:, 0, :], gates[:], row, None, ALU.mult).then_inc(dn_dve, 1)
                    V.tensor_scalar(picked[:, 1, :], betas[:], ident[0:16, bass.ds(h, 1)], None, ALU.mult).then_inc(dn_dve, 1)
                    V.tensor_scalar(cols[:], head_cols[:, :, bass.ds(h, 1)].rearrange("p r a -> p (r a)"), 1.0, None,
                                    ALU.mult).then_inc(dn_dve, 1)
                if gap == 2:
                    act("k_rstd")
                    V.tensor_tensor(kT[:], pre[:, 1, :], rs[:, 0, :], ALU.mult).then_inc(dn_dve, 1)
                    act("q_rstd")
                    V.tensor_tensor(qT[:], pre[:, 0, :], rs[:, 1, :], ALU.mult).then_inc(dn_dve, 1)
                if gap == 3:
                    pe("gate_rows")
                    own("columns")
                    for c in range(TB):
                        at = slice(c * P, (c + 1) * P)
                        last = V.tensor_scalar(decay[:, at], bank[4][:, at], gate_col[:, c:c + 1], 0.0,
                                               ALU.subtract, ALU.min)
                    last.then_inc(dn_dve, 1)
                    V.tensor_tensor(ends[:, 0, :], bank[4][:, P - 1:T:P], gate_col, ALU.subtract).then_inc(dn_dve, 1)
                if gap == 4:
                    act("decay")
                    V.tensor_tensor(by_chunk(decay[:]), by_chunk(decay[:]),
                                    incl[:].rearrange("p (c i) -> p c i", c=1).to_broadcast([P, TB, P]), ALU.mult
                                    ).then_inc(dn_dve, 1)
                    own("decay_mask")
                    pe("beta_rows")
                    V.tensor_tensor(m_t[:], decay[:], bank[5][:], ALU.mult).then_inc(dn_dve, 1)
                if gap == 5:
                    pe("kk")
                    own("decay_beta")
                    V.tensor_tensor(m_t[:], m_t[:], bank[2][:], ALU.mult).then_inc(dn_dve, 1)
                    pe("kq")
                    V.tensor_tensor(decay[:], decay[:], bank[3][:], ALU.mult).then_inc(dn_dve, 1)
                    pe("v_turn")
                    V.tensor_tensor(by_chunk(bv[:]), by_chunk(bank[6][:]), spread(beta_col), ALU.mult).then_inc(dn_dve, 1)
                if gap == 6:
                    pe("k_turn")
                    act("decay_end")
                    V.tensor_tensor(by_chunk(k_dec[:]), by_chunk(bank[4][:]), spread(ends[:, 1, :]), ALU.mult
                                    ).then_inc(dn_dve, 1)
                    V.tensor_copy(ends[:, 2, :], q_dec[:, P - 1:T:P]).then_inc(dn_dve, 1)
                    own("chunk_decay")
                    V.tensor_tensor(q_dec[:], q_dec[:], qT[:], ALU.mult).then_inc(dn_dve, 1)
                for l in range(1, 7):
                    if gap == 7 + 2 * l:
                        if l < 6:
                            pe(f"xmx{l}")
                            V.tensor_tensor(xi[:], xi[:], bank[4][:], ALU.subtract).then_inc(dn_dve, 1)
                        pe(f"xmx_turn{l}")
                        V.tensor_tensor(yi[:], yi[:], bank[5][:], ALU.subtract).then_inc(dn_dve, 1)
                for c in range(TB):
                    at = slice(c * P, (c + 1) * P)
                    if gap == 19 + 3 * c and c > 0:
                        pe(f"ks{c}")
                        V.scalar_tensor_tensor(out=resid[:], in0=bank[2][:, at], scalar=nbg_col[:, c:c + 1], in1=bv[:, at],
                                               op0=ALU.mult, op1=ALU.add).then_inc(dn_dve, 1)
                    if gap == 21 + 3 * c and c < TB - 1:
                        pe(f"kv{c}")
                        if c == 0:
                            V.tensor_copy(state[:], bank[4][:, at]).then_inc(dn_dve, 1)
                        else:
                            V.scalar_tensor_tensor(out=state[:], in0=state[:], scalar=ends[:, 2, c:c + 1],
                                                   in1=bank[4][:, at], op0=ALU.mult, op1=ALU.add).then_inc(dn_dve, 1)
                if gap == 31:
                    act("o_rstd")
                    V.scalar_tensor_tensor(out=rs[:, 1, :], in0=bank[3][:], scalar=dn_w[:, 0:1], in1=rs[:, 0, :],
                                           op0=ALU.mult, op1=ALU.mult).then_inc(dn_dve, 1)
                    own("o_scaled")
                    V.tensor_tensor(mix[:, bass.ds(h, 1), :].rearrange("p a n -> p (a n)"), rs[:, 1, :], pre[:, 3, :],
                                    ALU.mult).then_inc(dn_dve, 1)

            def att(gap, n):
                def act(name):
                    dve.wait_ge(at_act, after(AT_ACT, n, name))

                def own(name):
                    dve.wait_ge(at_dve, after(AT_DVE, n, name))

                if gap == 0:
                    dve.wait_ge(const_step, CONSTS)
                    dve.wait_ge(at_pe, after(AT_PE, n, "v_turn1"))
                    V.tensor_scalar(bias_h[:], base_bias[:], slopes[:, bass.ds(n, 1)], None, ALU.mult).then_inc(at_dve, 1)
                for i, (m, qb) in enumerate(SC):
                    if gap == 1 + 2 * i:
                        dve.wait_ge(at_pe, after(AT_PE, n, f"score{i}"))
                        own("bias")
                        e = ex[:, m, ex_block(qb)]
                        w = (qb + 1) * P
                        V.scalar_tensor_tensor(out=e, in0=bank[2 + i % 2][:, 0:w], scalar=float(P) ** -0.5,
                                               in1=bias_h[:, T - w:T], op0=ALU.mult, op1=ALU.add).then_inc(at_dve, 1)
                        own(f"score{i}")
                        V.tensor_reduce(neg_max[:, i:i + 1], e, AX.X, ALU.max, negate=True).then_inc(at_dve, 1)
                if gap == 18:
                    act("exp7")
                    V.reciprocal(inv_sum[:], row_sum[:]).then_inc(at_dve, 1)
                    own("rsum")
                    V.tensor_scalar(inv_sum[:, 4:8], inv_sum[:, 4:8], lam, None, ALU.mult).then_inc(at_dve, 1)
                    own("rsum_lam")
                for q in range(TB):
                    if gap == 18 + q // 2:
                        V.tensor_scalar(ex[:, 1, ex_block(q)], ex[:, 1, ex_block(q)], inv_sum[:, 4 + q:5 + q], None,
                                        ALU.mult).then_inc(at_dve, 1)
                        own(f"p_low{q}")
                        V.scalar_tensor_tensor(out=ex[:, 0, ex_block(q)], in0=ex[:, 0, ex_block(q)],
                                               scalar=inv_sum[:, q:q + 1], in1=ex[:, 1, ex_block(q)],
                                               op0=ALU.mult, op1=ALU.subtract).then_inc(at_dve, 1)
                if gap == 33:
                    act("rstd")
                    for e in range(2):
                        if isinstance(n, int):
                            to = att_o[:, e, :]
                        else:
                            to = mix[:, bass.ds(2 * n + DN_HEADS + e, 1), :].rearrange("p a n -> p (a n)")
                        V.scalar_tensor_tensor(out=to, in0=bank[4 + e][:], scalar=da_w[:, e:e + 1],
                                               in1=att_rs[:, 1, :], op0=ALU.mult, op1=ALU.mult).then_inc(at_dve, 1)

            def head_window(h, before):
                span = S_HEADS(h)
                for gap in range(8 * CHUNKS):
                    if gap == 0:
                        pick_taps(h)
                    if before is None:
                        if gap == 0:
                            gates_beta()
                        if gap == 4:
                            gate_columns()
                    else:
                        dn(gap, before)
                    if gap % CHUNKS == 1:
                        low(span, gap // CHUNKS)
                    for j in range(3):
                        for k in range(1, TAPS):
                            if gap == 8 * (j + 1) + k - 1:
                                conv(h, j, k)

            head_window(0, None)
            with dve.Fori(1, DN_HEADS) as h:
                head_window(h, h - 1)

            def att_window(n, before):
                span = S_ATT(n)
                for gap in range(12 * CHUNKS):
                    if before is None:
                        if gap < 32:
                            dn(gap, DN_HEADS - 1)
                    else:
                        att(gap, before)
                    if gap % CHUNKS == 1:
                        low(span, gap // CHUNKS)

            att_window(0, None)
            with dve.Fori(1, DA_HEADS) as n:
                att_window(n, n - 1)

            for k in range(0, KT - 2, 2):
                dve.wait_ge(mix_high, k // 2 + 1)
                V.tensor_tensor(h_low[:, k:k + 2, :], mix[:, k:k + 2, :], h_high[:, k:k + 2, :].bitcast(F32),
                                ALU.subtract).then_inc(mix_low, 1)

            def add_block(span, j, t, cols_of, x_loaded=False):
                if x_loaded:
                    dve.wait_ge(x_landed[t], 32)
                chunk_done(dve, span, j, t)
                at = x1[:, t, cols_of]
                V.tensor_tensor(at, at, bank[OUT_BANKS[t]][:], ALU.add).then_inc(out_added, 1)

            for gap in range(16 * CHUNKS):
                j = gap // CHUNKS
                if gap % CHUNKS == 0:
                    low(S_OUT0, j)
                att(gap, DA_HEADS - 1)
                if gap == 35:
                    for e in range(2):
                        dve.wait_ge(mix_high, 8 + e)
                        V.tensor_tensor(h_low[:, KT - 2 + e, :], att_o[:, e, :], h_high[:, KT - 2 + e, :].bitcast(F32),
                                        ALU.subtract).then_inc(mix_low, 1)
                if j % 4 == 3:
                    add_block(S_OUT0, j, gap % CHUNKS, slice(j // 4 * T, (j // 4 + 1) * T), x_loaded=True)
            with dve.Fori(0, 4) as g:
                for j in range(4):
                    low(S_OUT1(g), j)
                for t in range(TB):
                    add_block(S_OUT1(g), 3, t, bass.ds(g * T, T))
            norm(1)

            def product(n, fb):
                dve.wait_ge(gate_ready, 4 * n + fb + 1)
                V.tensor_tensor(hidden[:, fb % 2, :], gate_act[:, fb % 2, :], bank[3 + 2 * (fb % 2)][:], ALU.mult
                                ).then_inc(hid_ready, 1)

            def hidden_low(n, fb):
                dve.wait_ge(hid_high_ready, 4 * n + fb + 1)
                V.tensor_tensor(hid_low[:, fb, :], hidden[:, fb % 2, :], hid_high[:, fb, :].bitcast(F32), ALU.subtract
                                ).then_inc(hid_low_ready, 1)

            for j in range(16):
                low(S_FF0, j)
                if j % 4 == 0 and j > 0:
                    half_done(dve, S_FF0, j - 1)
                    product(0, j // 4 - 1)
                    hidden_low(0, j // 4 - 1)
            with dve.Fori(1, FF_GROUPS) as n:
                span = S_FF(n)
                for j in range(24):
                    if j == 0:
                        half_done(dve, span, -1)
                        product(n - 1, 3)
                        hidden_low(n - 1, 3)
                    low(span, j)
                    if j in (4, 16, 20):
                        half_done(dve, span, j - 1)
                        product(n, (j - 12) // 4 if j > 4 else 0)
                    if j in (12, 16, 20):
                        hidden_low(n, (j - 12) // 4)
                    if j in (5, 7, 9, 11):
                        for t in range(TB):
                            add_block(span, j, t, slice((j - 5) // 2 * T, (j - 3) // 2 * T))
            half_done(dve, S_END, -1)
            product(FF_GROUPS - 1, 3)
            hidden_low(FF_GROUPS - 1, 3)
            for j in range(8):
                low(S_END, j)
                if j % 2 == 1:
                    for t in range(TB):
                        add_block(S_END, j, t, slice(j // 2 * T, (j // 2 + 1) * T))
            norm(2, turned=False)

        @block.tensor
        def _(pe):
            M = nc.tensor.matmul

            def turn(out_ap, in_ap, n=P):
                return nc.tensor.transpose(out_ap, in_ap, ident[0:n, 0:n])

            def three(out_ap, stat, mov, start, stop):
                M(out_ap, stat[0], mov[0], start=start, stop=False, skip_group_check=True)
                M(out_ap, stat[0], mov[1], start=False, stop=False, skip_group_check=True)
                return M(out_ap, stat[1], mov[0], start=False, stop=stop, skip_group_check=True)

            def weights(slot, at):
                return w_high[:, slot, at], w_low[:, slot, at]

            def half_ready(span, j):
                pe.wait_ge(w_low_ready, count(span, j + 1))

            def column_chunk(span, j, c, b, part):
                slot = (span[0] + j) % SLOTS
                if c == 0:
                    half_ready(span, j)
                for kk in (2 * c, 2 * c + 1):
                    k = 8 * part + kk
                    last = three(bank[b][:], weights(slot, slice(kk * P, (kk + 1) * P)), (h_high[:, k, :], h_low[:, k, :]),
                                 k == 0, k == KT - 1)
                last.then_inc(chunks_done, 1)

            def row_chunk(span, j, t, acts, k0, start, stop):
                slot = (span[0] + j) % SLOTS
                if t == 0:
                    half_ready(span, j)
                for kk in range(2):
                    last = three(bank[OUT_BANKS[t]][:], tuple(a[:, k0 + kk, t * P:(t + 1) * P] for a in acts),
                                 weights(slot, slice(kk * T, (kk + 1) * T)), start and kk == 0, stop and kk == 1)
                last.then_inc(chunks_done, 1)

            pe.wait_ge(const_step, CONSTS)

            def norm(r):
                for t in range(TB):
                    pe.wait_ge(norm_scaled, TB * r + t + 1)
                    for g in range(4):
                        if t > 0:
                            pe.wait_ge(norm_low, 16 * r + 4 * (t - 1) + g + 1)
                        for k in range(4):
                            last = turn(bank[2 + g][:, k * P:(k + 1) * P], xn[:, t % 2, (4 * g + k) * P:(4 * g + k + 1) * P])
                        last.then_inc(norm_turned, 1)

            norm(0)
            pe.wait_ge(params_landed, PARAMS)
            turn(bank[7][:, 0:TAPS * 24], conv_rows[0:TAPS * 24, :], TAPS * 24).then_inc(param_turned, 1)
            pe.wait_ge(norm_low, 16)
            for j in range(2):
                for c in range(CHUNKS):
                    column_chunk((0, 0, 4), j, c, 0, j)

            def gates_turned():
                pe.wait_ge(ba_dve, 6)
                for i, rows in enumerate((gates, betas)):
                    for c in range(TB):
                        last = turn(bank[2][:, (4 * i + c) * 16:(4 * i + c + 1) * 16], rows[:, c * P:(c + 1) * P], 16)
                last.then_inc(ba_turned, 1)

            def dn(gap, h):
                def act(name):
                    pe.wait_ge(dn_act, after(DN_ACT, h, name))

                def dve(name):
                    pe.wait_ge(dn_dve, after(DN_DVE, h, name))

                def pool(name):
                    pe.wait_ge(dn_pool, after(DN_POOL, h, name))

                def chunks(b, stat, mov):
                    for c in range(TB):
                        at = slice(c * P, (c + 1) * P)
                        last = M(bank[b][:, at], stat[:, at], mov[:, at], start=True, stop=True)
                    last.then_inc(dn_pe, 1)

                def turns(b, src):
                    for c in range(TB):
                        last = turn(bank[b][:, c * P:(c + 1) * P], src[:, c * P:(c + 1) * P])
                    last.then_inc(dn_pe, 1)

                if gap == 1:
                    pe.wait_ge(dn_dve, all_done(DN_DVE, h))
                    act("k_square")
                    M(bank[2][:], ones[:], sq[:, 0, :], start=True, stop=True).then_inc(dn_pe, 1)
                    act("q_square")
                    M(bank[3][:], ones[:], sq[:, 1, :], start=True, stop=True).then_inc(dn_pe, 1)
                if gap == 2:
                    dve("gate_pick")
                    M(bank[4][:], ones[0:16, :], picked[:, 0, :], start=True, stop=True).then_inc(dn_pe, 1)
                    dve("beta_pick")
                    M(bank[5][:], ones[0:16, :], picked[:, 1, :], start=True, stop=True).then_inc(dn_pe, 1)
                if gap == 3:
                    pe.wait_ge(pre_ready, 4 * h + 3)
                    turns(6, pre[:, 2, :])
                if gap == 4:
                    dve("k")
                    chunks(2, kT[:], kT[:])
                    dve("q")
                    chunks(3, kT[:], qT[:])
                if gap == 5:
                    dve("gap_end")
                    act("decay_start")
                    turns(4, kT[:])
                if gap == 7:
                    pool("y0")
                    turns(2, yi[:])
                for l in range(1, 7):
                    if gap == 6 + 2 * l:
                        pool(f"level{l}")
                        if l == 1:
                            act("x0")
                            dve("a")
                        else:
                            dve(f"x{l - 1}")
                        chunks(3, level_m[:, l % 2, :], xi[:])
                    if gap == 7 + 2 * l:
                        act(f"mx{l}")
                        if l == 1:
                            dve("k_dec")
                        else:
                            dve(f"y{l - 1}")
                        if l < 6:
                            chunks(4, yi[:], mxs)
                        chunks(5, mxs, yi[:])
                for c in range(TB):
                    at = slice(c * P, (c + 1) * P)
                    if gap == 19 + 3 * c and c > 0:
                        dve(f"s{c - 1}")
                        M(bank[2][:, at], kT[:, at], state[:], start=True, stop=True).then_inc(dn_pe, 1)
                    if gap == 20 + 3 * c:
                        dve(f"r{c}" if c else "y6")
                        M(bank[6][:, at], yi[:, at], resid[:] if c else bv[:, at], start=True, stop=True).then_inc(dn_pe, 1)
                    if gap == 21 + 3 * c:
                        if c:
                            dve("q_dec")
                            M(bank[3][:, at], state[:], q_dec[:, at], start=True, stop=False)
                        act(f"vn{c}")
                        M(bank[3][:, at], v_new[:, c % 2, :], decay[:, at], start=(c == 0), stop=True).then_inc(dn_pe, 1)
                        if c < TB - 1:
                            M(bank[4][:, at], k_dec[:, at], v_new[:, c % 2, :], start=True, stop=True).then_inc(dn_pe, 1)
                if gap == 31:
                    act("o_square")
                    M(bank[5][:], ones[:], sq[:, 0, :], start=True, stop=True).then_inc(dn_pe, 1)

            def att(gap, n):
                def act(name):
                    pe.wait_ge(at_act, after(AT_ACT, n, name))

                def dve(name):
                    pe.wait_ge(at_dve, after(AT_DVE, n, name))

                if gap == 0:
                    pe.wait_ge(at_dve, all_done(AT_DVE, n))
                    pe.wait_ge(dn_dve, all_done(DN_DVE, DN_HEADS))
                    pe.wait_ge(att_pre_ready, 6 * n + 2)
                    for e in range(2):
                        for k in range(TB):
                            last = turn(bank[2 + e][:, k * P:(k + 1) * P], pre[:, e, k * P:(k + 1) * P])
                        last.then_inc(at_pe, 1)
                for i, (m, qb) in enumerate(SC):
                    if gap == 1 + 2 * i:
                        pe.wait_ge(att_pre_ready, 6 * n + (4 if m == 0 else 6))
                        if i < 2:
                            act(f"v{i}")
                        else:
                            dve(f"score{i - 2}")
                        w = (qb + 1) * P
                        M(bank[2 + i % 2][:, 0:w], pre[:, 2 + 2 * m, qb * P:(qb + 1) * P], pre[:, 3 + 2 * m, 0:w],
                          start=True, stop=True).then_inc(at_pe, 1)
                for k in range(TB):
                    if gap == 22 + 2 * k:
                        if k < 2:
                            dve("p3")
                        else:
                            act(f"p{k - 2}")
                        for q in range(k, TB):
                            at = ex_block(q).start + k * P
                            last = turn(bank[2 + k % 2][:, (q - k) * P:(q - k + 1) * P], ex[:, 0, at:at + P])
                        last.then_inc(at_pe, 1)
                if gap in (30, 31):
                    e = gap - 30
                    act("p3")
                    for k in range(TB):
                        w = (TB - k) * P
                        last = M(bank[4 + e][:, k * P:T], v_tok[:, k, e * P:(e + 1) * P], p_t[:, PT_OFF[k]:PT_OFF[k] + w],
                                 start=(k == 0), stop=(k == TB - 1), skip_group_check=True)
                    last.then_inc(at_pe, 1)
                if gap == 33:
                    act("square1")
                    M(bank[2][:], ones[:], att_sq[:, 0, :], start=True, stop=False)
                    M(bank[2][:], ones[:], att_sq[:, 1, :], start=False, stop=True).then_inc(at_pe, 1)

            def head_unit_ready(h, j):
                first = isinstance(h, int)
                if j == 0 and not first:
                    pe.wait_ge(conv_tap, 9 * h)
                if j == 1:
                    if first:
                        pe.wait_ge(ba_act, 2)
                        pe.wait_ge(ba_dve, 1)
                    else:
                        pe.wait_ge(pre_ready, 4 * h)
                if j >= 2:
                    pe.wait_ge(conv_tap, 9 * h + 3 * (j - 1))

            def head_window(h, before):
                span = S_HEADS(h)
                for gap in range(8 * CHUNKS):
                    j, c = divmod(gap, CHUNKS)
                    if gap % 8 == 0:
                        head_unit_ready(h, gap // 8)
                    column_chunk(span, j, c, (U_HEADS + j // 2) % 2, j % 2)
                    if before is None:
                        if gap == 12:
                            gates_turned()
                    else:
                        dn(gap, before)

            head_window(0, None)
            with pe.Fori(1, DN_HEADS) as h:
                head_window(h, h - 1)

            def att_window(n, before):
                span = S_ATT(n)
                for gap in range(12 * CHUNKS):
                    j, c = divmod(gap, CHUNKS)
                    if gap % 8 == 0:
                        u = gap // 8
                        if before is None and u < 2:
                            if u == 0:
                                pe.wait_ge(conv_tap, 9 * DN_HEADS)
                            else:
                                pe.wait_ge(pre_ready, 4 * DN_HEADS)
                        else:
                            pe.wait_ge(att_pre_ready, 6 * n + u - 1)
                    column_chunk(span, j, c, (U_ATT + j // 2) % 2, j % 2)
                    if before is None:
                        if gap < 32:
                            dn(gap, DN_HEADS - 1)
                    else:
                        att(gap, before)

            att_window(0, None)
            with pe.Fori(1, DA_HEADS) as n:
                att_window(n, n - 1)

            h_parts = (h_high, h_low)
            pe.wait_ge(att_pre_ready, 6 * DA_HEADS)
            for gap in range(16 * CHUNKS):
                j, t = divmod(gap, CHUNKS)
                if j < 4 and t == 0:
                    pe.wait_ge(mix_low, j + 1)
                if j % 4 == 0 and j > 0:
                    pe.wait_ge(out_added, j - 4 + t + 1)
                row_chunk(S_OUT0, j, t, h_parts, 2 * (j % 4), j % 4 == 0, j % 4 == 3)
                att(gap, DA_HEADS - 1)
            pe.wait_ge(mix_low, 9)
            with pe.Fori(0, 4) as g:
                for j in range(4):
                    for t in range(TB):
                        if j == 0:
                            pe.wait_ge(out_added, 4 * g + 12 + t + 1)
                        row_chunk(S_OUT1(g), j, t, h_parts, 8 + 2 * j, j == 0, j == 3)
            norm(1)
            pe.wait_ge(norm_low, 32)

            def pair(span, j0, n, fb):
                if not isinstance(n, int) or 4 * n + fb >= 2:
                    pe.wait_ge(hid_ready, 4 * n + fb - 1)
                for j in range(4):
                    for c in range(CHUNKS):
                        column_chunk(span, j0 + j, c, 2 + 2 * (fb % 2) + j // 2, j % 2)

            def down(span, j0, n, added):
                pe.wait_ge(hid_low_ready, 4 * n + 4)
                for j in range(8):
                    for t in range(TB):
                        if j % 2 == 0:
                            pe.wait_ge(out_added, added + 4 * (j // 2) - 4 + t + 1)
                        row_chunk(span, j0 + j, t, (hid_high, hid_low), 2 * (j % 2), j % 2 == 0, j % 2 == 1)

            for fb in range(4):
                pair(S_FF0, 4 * fb, 0, fb)
            with pe.Fori(1, FF_GROUPS) as n:
                pair(S_FF(n), 0, n, 0)
                down(S_FF(n), 4, n - 1, 16 * n + 16)
                for fb in range(1, 4):
                    pair(S_FF(n), 8 + 4 * fb, n, fb)
            down(S_END, 0, FF_GROUPS - 1, 32 + 16 * (FF_GROUPS - 1))
    return nc


_INS = ["x", "attn_norm_w", "w_in", "conv_w", "a_log", "dt_bias", "dn_norm_w", "lam_q1", "lam_k1", "lam_q2", "lam_k2",
        "da_norm_w", "w_out", "ffn_norm_w", "w_gate", "w_up", "w_down", "final_norm_w"]


def kernel(**inputs):
    import numpy as _np
    import concourse.bacc as _bacc
    from concourse import mybir as _mybir
    from concourse.bass_utils import run_bass_kernel_spmd as _run

    nc = _bacc.Bacc("TRN2", target_bir_lowering=False, num_devices=1)
    arrays, args = {}, []
    for name in _INS:
        a = _np.ascontiguousarray(inputs[name])
        arrays[f"in_{name}_dram"] = a
        args.append(nc.dram_tensor(f"in_{name}_dram", a.shape, _mybir.dt.from_np(a.dtype), kind="ExternalInput").ap())
    args.append(nc.dram_tensor("out_0_dram", (1, T, D), F32, kind="ExternalOutput").ap())
    build(nc, *args)
    r = _run(nc, [arrays], core_ids=[0])
    return r.results[0]["out_0_dram"]
```

```python
import math
from contextlib import ExitStack

import concourse.bass as bass
from concourse import mybir

F32 = mybir.dt.float32
F32R = mybir.dt.float32r
ACT = mybir.ActivationFunctionType
ALU = mybir.AluOpType
AX = mybir.AxisListType

P = 128
T = 512
D = 2048
TB = T // P
KT = D // P
DN_HEADS, DA_HEADS = 8, 4
TAPS = 4
D_FF = 5632
DN_WIDTH = DN_HEADS * P
OFF_Z = 3 * DN_WIDTH
OFF_B = OFF_Z + DN_WIDTH
OFF_Q = OFF_B + 2 * DN_HEADS
OFF_K = OFF_Q + DA_HEADS * 2 * P
OFF_V = OFF_K + DA_HEADS * 2 * P
EPS = 1e-6
LAM_INIT = 0.8 - 0.6 * math.exp(0.0)
FAR = -1e30

UNIT = 2048
HALF = UNIT // 2
SLOTS = 4
LEAD = 3
CHUNKS = 4
FF_GROUPS = D_FF // (4 * P)
U_HEADS = 1
U_ATT = U_HEADS + 4 * DN_HEADS
U_OUT = U_ATT + 6 * DA_HEADS
U_FF = U_OUT + 16
UNITS = U_FF + 12 * FF_GROUPS
HALVES = 2 * UNITS
EXP_WIDTH = P * TB * (TB + 1) // 2

DN_PE = (["gate_rows", "beta_rows", "v_turn", "kk", "kq", "k_turn"]
         + [f"{s}{l}" for l in range(1, 6) for s in ("mx", "xmx")] + ["xmx_turn5", "mx6", "xmx_turn6"]
         + ["vn0", "o0", "kv0"] + [f"{s}{c}" for c in (1, 2) for s in ("ks", "vn", "o", "kv")]
         + ["ks3", "vn3", "o3", "o_squares"])
DN_ACT = (["decay", "decay_start", "decay_end"]
          + [f"mx{l}" for l in range(1, 7)] + [f"vn{c}" for c in range(4)] + ["o_square", "o_log", "o_rstd"])
DN_DVE = (["k", "q", "columns", "gaps", "gap_end", "decay_mask", "decay_beta", "m", "a",
           "bv", "k_dec", "chunk_decay", "q_dec", "x0"]
          + [s for l in range(1, 6) for s in (f"x{l}", f"y{l}")] + ["y6"]
          + ["s0"] + [s for c in (1, 2) for s in (f"r{c}", f"s{c}")] + ["r3", "o_scaled", "o"])
DN_POOL = ["level0", "y0"] + [f"level{l}" for l in range(1, 6)]

SC = [(m, qb) for m in range(2) for qb in range(TB)]
AT_PE = (["v_turn0", "v_turn1"] + [f"score{i}" for i in range(8)] + [f"p_turn{k}" for k in range(TB)]
         + ["pv0", "pv1", "squares"])
AT_ACT = (["v0", "v1"] + [f"exp{i}" for i in range(8)] + [f"p{k}" for k in range(TB)]
          + ["square0", "square1", "log", "rstd"])
AT_DVE = (["bias"] + [s for i in range(8) for s in (f"score{i}", f"max{i}")] + ["rsum", "rsum_lam"]
          + [s for q in range(TB) for s in (f"p_low{q}", f"p{q}")] + ["o0", "o1"])


PT_OFF = [sum(TB - i for i in range(k)) * P for k in range(TB)]


def ex_block(qb):
    return slice(P * qb * (qb + 1) // 2, P * (qb + 1) * (qb + 2) // 2)


def after(steps, head, name):
    return head * len(steps) + steps.index(name) + 1 + FIRST[id(steps)]


CONSTS = 3 + 3 * 7 + 2 + DA_HEADS
FIRST = {id(DN_PE): 0, id(DN_ACT): 0, id(DN_DVE): 1, id(DN_POOL): 0, id(AT_PE): 0, id(AT_ACT): 0, id(AT_DVE): 1}


def all_done(steps, heads):
    return heads * len(steps) + FIRST[id(steps)]


def build(nc, x, attn_norm_w, w_in, conv_w, a_log, dt_bias, dn_norm_w, lam_q1, lam_k1, lam_q2, lam_k2,
          da_norm_w, w_out, ffn_norm_w, w_gate, w_up, w_down, final_norm_w, out):
    stack = ExitStack()

    def sb(name, shape, dt=F32, where=stack):
        return where.enter_context(nc.sbuf_tensor(name, shape, dt))

    def sem(name):
        return stack.enter_context(nc.semaphore(name))

    with stack:
        bank = [stack.enter_context(nc.psum_tensor(f"bank{i}", [P, 512], F32)) for i in range(8)]

        raw = sb("raw", [P, 2, UNIT])
        w_high = sb("w_high", [P, SLOTS, HALF], F32R)
        w_low = sb("w_low", [P, SLOTS, HALF], F32R)
        h_high = sb("h_high", [P, KT, T], F32R)
        h_low = sb("h_low", [P, KT, T], F32R)
        x1 = sb("x1", [P, TB, D])
        mix = x1[:].rearrange("p t (k n) -> p (t k) n", n=T)
        ident = sb("ident", [P, P])
        ones = sb("ones", [P, P])
        part_sq = sb("part_sq", [P, TB, 4])
        ones_r = sb("ones_r", [P, P], F32R)
        small = sb("small", [P, 64])
        conv_rows = sb("conv_rows", [P, P])
        conv_t = sb("conv_t", [P, TAPS, 3, DN_HEADS])
        dn_w = sb("dn_w", [P, 1])
        da_w = sb("da_w", [P, 2])
        lam_v = sb("lam_v", [P, 4, P])
        slopes = sb("slopes", [P, DA_HEADS])
        base_bias = sb("base_bias", [P, T])
        incl = sb("incl", [P, P])
        levels = sb("levels", [P, 7, P])
        sum_sq = small[:, 0:4]
        rstd_log = small[:, 4:8]
        rstd = small[:, 8:12]
        lam_dot = small[:, 12:14]
        lam_exp = small[:, 14:16]
        lam = small[:, 16:17]
        rate = small[:, 17:18]
        dt_col = small[:, 18:19]
        alog_col = small[:, 19:20]

        heads = ExitStack()
        stack.enter_context(heads)
        pre = sb("pre", [P, 6, T], where=heads)
        deltanet = ExitStack()
        heads.enter_context(deltanet)
        d = lambda name, shape: sb(name, shape, where=deltanet)
        conv_acc = d("conv_acc", [P, T])
        row_parts = sb("row_parts", [48, 2, T], F32R, where=deltanet)
        head_cols = d("head_cols", [P, 12, DN_HEADS])
        cols = d("cols", [P, 12])
        taps = d("taps", [P, TAPS, 3])
        ba_t = d("ba_t", [P, 8, 16])
        picked = sb("picked", [48, 2, T], F32R, where=deltanet)
        sq = d("sq", [P, 2, T])
        rs = d("rs", [P, 2, T])
        kT, qT = d("kT", [P, T]), d("qT", [P, T])
        decay = d("decay", [P, T])
        qk_high = sb("qk_high", [P, 2, T], F32R, where=deltanet)
        qk_low = sb("qk_low", [P, 2, T], F32R, where=deltanet)
        level_m, mxs = sq, rs[:, 1, :]
        k_tiles = lambda view, a: view[:, a:a + 2, :]
        qk_sq = k_tiles(mix, 8)
        q_dec, k_dec, bv, m_t = (mix[:, k, :] for k in range(10, 14))
        gates = mix[0:16, 14, :]
        betas = mix[0:16, 15, :]
        qk_rs = k_tiles(mix, 14)
        exps = rs[0:16]
        row_pick = small[0:48, 24:40]
        xi, yi = d("xi", [P, T]), d("yi", [P, T])
        state, resid = d("state", [P, P]), d("resid", [P, P])
        v_new = d("v_new", [P, 2, P])
        ends = d("ends", [P, 3, TB])
        deltanet.close()
        attention = ExitStack()
        heads.enter_context(attention)
        a = lambda name, shape: sb(name, shape, where=attention)
        v_tok = a("v_tok", [P, TB, 2 * P])
        ex = a("ex", [P, 2, EXP_WIDTH])
        p_t = a("p_t", [P, EXP_WIDTH])
        bias_h = a("bias_h", [P, T])
        att_sq = a("att_sq", [P, 2, T])
        att_rs = a("att_rs", [P, 2, T])
        att_o = a("att_o", [P, 2, T])
        neg_max = a("neg_max", [P, 8])
        row_sum = a("row_sum", [P, 8])
        inv_sum = a("inv_sum", [P, 8])
        attention.close()
        heads.close()
        norms = ExitStack()
        stack.enter_context(norms)
        w_row = sb("w_row", [P, D], where=norms)
        turning = ExitStack()
        norms.enter_context(turning)
        xn = sb("xn", [P, TB, D], where=turning)
        squares_out = sb("squares_out", [P, T], where=turning)
        diag = sb("diag", [P, TB, P], where=turning)
        turning.close()
        ffn = ExitStack()
        norms.enter_context(ffn)
        hid_high = sb("hid_high", [P, 4, T], F32R, where=ffn)
        hid_low = sb("hid_low", [P, 4, T], F32R, where=ffn)
        gate_act = sb("gate_act", [P, 2, T], where=ffn)
        hidden = sb("hidden", [P, 2, T], where=ffn)
        last_squares = sb("last_squares", [P, T], where=ffn)
        ffn.close()
        norms.close()

        raw_landed = [sem("raw_landed0"), sem("raw_landed1")]
        w_high_ready = sem("w_high_ready")
        w_low_ready = sem("w_low_ready")
        chunks_done = sem("chunks_done")
        x_landed = [sem(f"x_landed{t}") for t in range(TB)]
        row_landed = sem("row_landed")
        params_landed = sem("params_landed")
        const_step = sem("const_step")
        dve_const = sem("dve_const")
        norm_sq = sem("norm_sq")
        norm_log = sem("norm_log")
        norm_rstd = sem("norm_rstd")
        norm_sum = sem("norm_sum")
        norm_scaled = sem("norm_scaled")
        norm_diag = sem("norm_diag")
        out_scaled_act = sem("out_scaled_act")
        out_scaled = sem("out_scaled")
        norm_turned = sem("norm_turned")
        norm_high = sem("norm_high")
        norm_low = sem("norm_low")
        conv_first = sem("conv_first")
        conv_tap = sem("conv_tap")
        pre_ready = sem("pre_ready")
        att_pre_ready = sem("att_pre_ready")
        param_turned = sem("param_turned")
        conv_ready = sem("conv_ready")
        taps_ready = sem("taps_ready")
        lam_step = sem("lam_step")
        lam_act = sem("lam_act")
        ba_act = sem("ba_act")
        ba_dve = sem("ba_dve")
        ba_turned = sem("ba_turned")
        rows_clear = sem("rows_clear")
        parts_high = sem("parts_high")
        parts_low = sem("parts_low")
        rows_picked = sem("rows_picked")
        qk_sums = sem("qk_sums")
        qk_logs = sem("qk_logs")
        qk_rstds = sem("qk_rstds")
        qk_squared = sem("qk_squared")
        qk_high_ready = sem("qk_high_ready")
        qk_low_ready = sem("qk_low_ready")
        dn_pe, dn_act, dn_dve, dn_pool = sem("dn_pe"), sem("dn_act"), sem("dn_dve"), sem("dn_pool")
        at_pe, at_act, at_dve = sem("at_pe"), sem("at_act"), sem("at_dve")
        mix_high = sem("mix_high")
        mix_low = sem("mix_low")
        out_added = sem("out_added")
        gate_ready = sem("gate_ready")
        hid_ready = sem("hid_ready")
        hid_high_ready = sem("hid_high_ready")
        hid_low_ready = sem("hid_low_ready")
        stored = sem("stored")

        by_k = lambda w: w[0].rearrange("(k p) n -> p k n", p=P)
        in_v, gate_v, up_v = by_k(w_in), by_k(w_gate), by_k(w_up)
        out_v, down_v = by_k(w_out), by_k(w_down)

        def in_column(kind, head):
            return {"q": 0, "k": DN_WIDTH, "v": 2 * DN_WIDTH, "z": OFF_Z}[kind] + head * P

        def att_column(u, head):
            return (OFF_V, OFF_V + P, OFF_Q, OFF_K, OFF_Q + P, OFF_K + P)[u] + head * 2 * P

        OUT_BANKS = (0, 1, 6, 7)
        PAIR = (slice(0, 2), slice(2, 4))
        ADDED_END = 32 + 16 * (FF_GROUPS - 1)
        END_BANKS = (OUT_BANKS[0:2], OUT_BANKS[2:4])
        NORM_BANKS = ((2, 3, 4, 5), OUT_BANKS)

        block = stack.enter_context(nc.Block())

        def count(span, j, scale=1, plus=0):
            base, i, per = span
            return scale * (base + j) + plus + i * (per * scale)

        def last_halves(span, j):
            return isinstance(span[1], int) and count(span, j + LEAD) >= HALVES

        def half_done(eng, span, j):
            eng.wait_ge(chunks_done, count(span, j + 1, CHUNKS))

        def chunk_done(eng, span, j, c):
            eng.wait_ge(chunks_done, count(span, j, CHUNKS, c + 1))

        S_HEADS = lambda h: (2 * U_HEADS, h, 8)
        S_ATT = lambda n: (2 * U_ATT, n, 12)
        S_OUT0 = (2 * U_OUT, 0, 4)
        S_OUT1 = lambda g: (2 * U_OUT + 16, g, 4)
        S_OUT1_LAST = (2 * U_OUT + 28, 0, 4)
        S_FF0 = (2 * U_FF, 0, 24)
        S_FF = lambda n: (2 * U_FF + 16 - 24, n, 24)
        S_END = (HALVES - 8, 0, 8)
        PARAMS = 16 * 10
        by_chunk = lambda t: t.rearrange("p (c i) -> p c i", c=TB)

        @block.sync
        def _(sp):
            def load(u, slot, src, blocks=KT):
                if not isinstance(u, int) or u >= 2:
                    sp.wait_ge(w_low_ready, 2 * u - 2)
                sp.dma_start(raw[:, slot, :].rearrange("p (k n) -> p k n", k=blocks), src
                             ).then_inc(raw_landed[slot], 16)

            def columns(view, col):
                return view[:, :, bass.ds(col, P)]

            def load_head(h):
                for j, kind in enumerate("qkvz"):
                    load(4 * h + U_HEADS + j, (U_HEADS + j) % 2, columns(in_v, in_column(kind, h)))

            def load_attention(n):
                for j in range(6):
                    load(6 * n + U_ATT + j, (U_ATT + j) % 2, columns(in_v, att_column(j, n)))

            def load_out(g, half_k):
                for j in range(2):
                    load(2 * g + U_OUT + 8 * half_k + j, (U_OUT + j) % 2,
                         out_v[:, 8 * half_k + 4 * j:8 * half_k + 4 * j + 4, bass.ds(g * T, T)], 4)

            def load_pair(u, n, fb):
                load(u, U_FF % 2, columns(gate_v, n * (4 * P) + fb * P))
                load(u + 1, 1 - U_FF % 2, columns(up_v, n * (4 * P) + fb * P))

            def load_down(u, n):
                for c in range(4):
                    load(u + c, (U_FF + c) % 2, down_v[:, bass.ds(n * 4, 4), c * T:(c + 1) * T], 4)

            for t in range(TB):
                sp.dma_start(x1[:, t, :], x[0, t * P:(t + 1) * P, :]).then_inc(x_landed[t], 16)
                if t == 1:
                    sp.dma_start(w_row[:], attn_norm_w[0:1, :].to_broadcast([P, D])).then_inc(row_landed, 16)
            load(0, 0, columns(in_v, OFF_B))
            load_head(0)
            with sp.Fori(1, DN_HEADS) as h:
                load_head(h)
            with sp.Fori(0, DA_HEADS) as n:
                load_attention(n)
            for half_k in range(2):
                with sp.Fori(0, 4) as g:
                    load_out(g, half_k)
            for fb in range(4):
                load_pair(U_FF + 2 * fb, 0, fb)
            with sp.Fori(1, FF_GROUPS) as n:
                u = 12 * n + (U_FF + 8 - 12)
                load_pair(u, n, 0)
                load_down(u + 2, n - 1)
                for fb in range(1, 4):
                    load_pair(u + 4 + 2 * fb, n, fb)
            load_down(UNITS - 4, FF_GROUPS - 1)
            for t in range(TB):
                for i, scaled in enumerate((out_scaled_act, out_scaled)):
                    sp.wait_ge(scaled, t + 1)
                    at = slice(i * (D // 2), (i + 1) * (D // 2))
                    sp.dma_start(out[0, t * P:(t + 1) * P, at], x1[:, t, at]).then_inc(stored, 16)
            sp.wait_ge(stored, 2 * 16 * TB)

        @block.gpsimd
        def _(pool):
            steps = [0]

            def const(ins):
                ins.then_inc(const_step, 1)
                steps[0] += 1
                pool.wait_ge(const_step, steps[0])

            const(pool.memset(ident[:], 0.0))
            const(pool.affine_select(out=ident[:], in_=ident[:], compare_op=ALU.not_equal, fill=1.0, base=0,
                                     pattern=[[-1, P]], channel_multiplier=1))
            pool.wait_ge(dve_const, 1)
            const(pool.affine_select(out=incl[:], in_=ones[:], compare_op=ALU.is_ge, fill=0.0, base=0,
                                     pattern=[[1, P]], channel_multiplier=-1))
            for l in range(7):
                s = 1 << l
                odd = levels[:, l, :].rearrange("p (g b s) -> p g b s", b=2, s=s)[:, :, 1, :]
                src = ones[:].rearrange("p (g b s) -> p g b s", b=2, s=s)[:, :, 1, :]
                const(pool.memset(levels[:, l, :], 0.0))
                const(pool.affine_select(out=odd, in_=src, compare_op=ALU.is_ge, fill=0.0, base=0,
                                         pattern=[[-2 * s, P // (2 * s)], [0, s]], channel_multiplier=1))
                const(pool.affine_select(out=odd, in_=odd, compare_op=ALU.is_ge, fill=0.0, base=s - 1,
                                         pattern=[[2 * s, P // (2 * s)], [0, s]], channel_multiplier=-1))
            const(pool.iota(base_bias[:], pattern=[[1, T]], base=P - T, channel_multiplier=-1,
                            allow_small_or_imprecise_dtypes=True))
            const(pool.affine_select(out=base_bias[:], in_=base_bias[:], compare_op=ALU.is_ge, fill=FAR, base=T - P,
                                     pattern=[[-1, T]], channel_multiplier=1))
            for n in range(DA_HEADS):
                const(pool.memset(slopes[:, n:n + 1], 2.0 ** (-8.0 * (n + 1) / DA_HEADS)))
            assert steps[0] == CONSTS

            def mask(l):
                return levels[:, l:l + 1, :].to_broadcast([P, TB, P])

            def squares(h):
                pool.wait_ge(pre_ready, 4 * h + 2)
                if not isinstance(h, int):
                    pool.wait_ge(qk_sums, 2 * h)
                pool.tensor_tensor(qk_sq, pre[:, 0:2, :], pre[:, 0:2, :], ALU.mult).then_inc(qk_squared, 1)
                pool.wait_ge(qk_high_ready, h + 1)
                pool.tensor_tensor(qk_low[:], qk_sq, qk_high[:].bitcast(F32), ALU.subtract).then_inc(qk_low_ready, 1)

            def head_levels(h):
                pool.wait_ge(dn_dve, after(DN_DVE, h, "m"))
                pool.tensor_tensor(by_chunk(level_m[:, 0, :]), by_chunk(m_t), mask(0), ALU.mult).then_inc(dn_pool, 1)
                pool.wait_ge(dn_pool, after(DN_POOL, h, "level0"))
                pool.tensor_tensor(by_chunk(yi[:]), ident[:].rearrange("p (c i) -> p c i", c=1).to_broadcast([P, TB, P]),
                                   by_chunk(level_m[:, 0, :]), ALU.subtract).then_inc(dn_pool, 1)
                for l in range(1, 6):
                    if l >= 3:
                        pool.wait_ge(dn_pe, after(DN_PE, h, f"mx{l - 2}"))
                    if l == 2:
                        pool.wait_ge(dn_pool, after(DN_POOL, h, "y0"))
                    pool.tensor_tensor(by_chunk(level_m[:, l % 2, :]), by_chunk(m_t), mask(l), ALU.mult
                                       ).then_inc(dn_pool, 1)

            squares(0)
            with pool.Fori(1, DN_HEADS) as h:
                head_levels(h - 1)
                squares(h)
            head_levels(DN_HEADS - 1)

        @block.scalar
        def _(act):
            A = nc.scalar.activation

            def high(span, j, by_block=False):
                if last_halves(span, j):
                    return
                s = span[0] + j + LEAD
                act.wait_ge(raw_landed[(s // 2) % 2], 16 * (s // 4 + 1) + span[1] * (span[2] * 4))
                if by_block:
                    act.wait_ge(chunks_done, CHUNKS * span[0] + CHUNKS * 3 + (j + LEAD - SLOTS) + 1)
                elif not isinstance(span[1], int) or s >= SLOTS:
                    half_done(act, span, j + LEAD - SLOTS)
                A(w_high[:, s % SLOTS, :], raw[:, (s // 2) % 2, (s % 2) * HALF:(s % 2 + 1) * HALF], ACT.Copy
                  ).then_inc(w_high_ready, 1)

            def rstds(r, i, two):
                if r == 0:
                    act.wait_ge(norm_sq, 2 * i + 2)
                else:
                    act.wait_ge(norm_sum, 2 * (r - 1) + i + 1)
                if r > 0:
                    act.wait_ge(norm_diag, 4 * r)
                A(rstd_log[:, two], sum_sq[:, two], ACT.Ln, scale=1.0 / D, bias=EPS).then_inc(norm_log, 1)
                act.wait_ge(norm_log, 2 * r + i + 1)
                A(rstd[:, two], rstd_log[:, two], ACT.Exp, scale=-0.5).then_inc(norm_rstd, 1)

            def high_parts(r):
                for t in range(TB):
                    for g in range(4):
                        act.wait_ge(norm_turned, 16 * r + 4 * t + g + 1)
                        A(h_high[:, 4 * g:4 * g + 4, t * P:(t + 1) * P],
                          bank[NORM_BANKS[t % 2][g]][:].rearrange("p (k i) -> p k i", k=4), ACT.Copy).then_inc(norm_high, 1)

            def group_square(to, t, g, added, squared):
                act.wait_ge(out_added, added)
                act.wait_ge(norm_sq, squared)
                A(to[:], x1[:, t, bass.ds(g * T, T)], ACT.Square, accum_out=part_sq[:, t, bass.ds(g, 1)]
                  ).then_inc(norm_sq, 1)

            act.wait_ge(dve_const, 2)
            for pair in range(2):
                for t in (2 * pair, 2 * pair + 1):
                    act.wait_ge(x_landed[t], 16)
                    A(h_low[:, 4 * t:4 * t + 4, :].rearrange("p k n -> p (k n)"), x1[:, t, :], ACT.Square,
                      accum_out=sum_sq[:, t:t + 1]).then_inc(norm_sq, 1)
                rstds(0, pair, PAIR[pair])

            act.dma_start(conv_rows[0:TAPS * 24, :], conv_w[0].rearrange("t (b c) -> (t b) c", c=P)).then_inc(params_landed, 16)
            act.dma_start(dn_w[:], dn_norm_w[0].rearrange("(c a) -> c a", a=1)).then_inc(params_landed, 16)
            for e in range(2):
                act.dma_start(da_w[:, e:e + 1], da_norm_w[0, e * P:(e + 1) * P].rearrange("(c a) -> c a", a=1)
                              ).then_inc(params_landed, 16)
            for i, v in enumerate((lam_q1, lam_k1, lam_q2, lam_k2)):
                act.dma_start(lam_v[:, i, :], v[0:1, :].to_broadcast([P, P])).then_inc(params_landed, 16)
            act.dma_start(dt_col[8:16, :], dt_bias[0].rearrange("(c a) -> c a", a=1)).then_inc(params_landed, 16)
            act.dma_start(alog_col[8:16, :], a_log[0].rearrange("(c a) -> c a", a=1)).then_inc(params_landed, 16)
            high_parts(0)
            for j in range(-LEAD, 0):
                high((0, 0, 4), j)

            act.wait_ge(lam_step, 4)
            A(lam_exp, lam_dot, ACT.Exp).then_inc(lam_act, 1)
            act.wait_ge(params_landed, PARAMS)
            A(rate, alog_col, ACT.Exp).then_inc(lam_act, 1)
            high((0, 0, 4), 0)
            high((0, 0, 4), 1)

            def gates_beta():
                half_done(act, (0, 0, 4), 1)
                A(betas, bank[0][0:16, :], ACT.Exp, scale=-1.0).then_inc(ba_act, 1)
                A(exps[:, 0, :], bank[0][0:16, :], ACT.Abs, bias=dt_col[0:16, :]).then_inc(ba_act, 1)
                act.wait_ge(ba_act, 2)
                A(exps[:, 1, :], exps[:, 0, :], ACT.Exp, scale=-1.0).then_inc(ba_act, 1)
                act.wait_ge(ba_act, 3)
                A(exps[:, 0, :], exps[:, 1, :], ACT.Ln, bias=1.0).then_inc(ba_act, 1)

            def gate_columns():
                act.wait_ge(ba_dve, 6)
                for i, rows in enumerate((gates, betas)):
                    A(row_parts[0:16, i, :], rows, ACT.Copy).then_inc(parts_high, 1)
                act.wait_ge(ba_turned, 1)
                A(ba_t[:], bank[2][:, 0:P].rearrange("p (c r) -> p c r", r=16), ACT.Copy).then_inc(ba_act, 1)
                act.wait_ge(ba_act, 5)
                A(head_cols[:, 8:12, :], ba_t[:, 0:4, 8:16], ACT.Exp).then_inc(ba_act, 1)

            def z_out(h):
                act.wait_ge(dn_dve, all_done(DN_DVE, h))
                A(pre[:, 3, :], bank[0][:], ACT.Silu).then_inc(pre_ready, 1)

            def conv_start(h, j):
                act.wait_ge(taps_ready, h + 1)
                if not isinstance(h, int) or h > 0 or j > 0:
                    act.wait_ge(pre_ready, 4 * h + j)
                A(conv_acc[:], bank[(U_HEADS + j) % 2][:], ACT.Copy, scale=taps[:, TAPS - 1, j:j + 1]
                  ).then_inc(conv_first, 1)

            def conv_end(h, j):
                act.wait_ge(conv_tap, 9 * h + 3 * j + 3)
                if not isinstance(h, int):
                    if j < 2:
                        act.wait_ge(dn_dve, after(DN_DVE, h - 1, "q"))
                    else:
                        act.wait_ge(dn_pe, after(DN_PE, h - 1, "v_turn"))
                A(pre[:, j, :], conv_acc[:], ACT.Silu).then_inc(pre_ready, 1)

            def dn(gap, h):
                def pe(name):
                    act.wait_ge(dn_pe, after(DN_PE, h, name))

                def dve(name):
                    act.wait_ge(dn_dve, after(DN_DVE, h, name))

                def own(name):
                    act.wait_ge(dn_act, after(DN_ACT, h, name))

                if gap == 2:
                    dve("gaps")
                    A(decay[:], decay[:], ACT.Exp).then_inc(dn_act, 1)
                    dve("gap_end")
                    A(q_dec, bank[4][:], ACT.Exp).then_inc(dn_act, 1)
                    A(ends[:, 1, :], ends[:, 0, :], ACT.Exp).then_inc(dn_act, 1)
                for l in range(1, 7):
                    if gap == 5 + 2 * l:
                        pe(f"mx{l}")
                        if l < 6:
                            A(mxs, bank[3][:], ACT.Copy).then_inc(dn_act, 1)
                        else:
                            A(mxs[64:P, 0:T // 2], bank[3][0:64, 0:T // 2], ACT.Copy).then_inc(dn_act, 1)
                for c in range(TB):
                    if gap == 19 + 3 * c:
                        pe(f"vn{c}")
                        A(v_new[:, c % 2, :], bank[6][:, c * P:(c + 1) * P], ACT.Copy).then_inc(dn_act, 1)
                if gap == 29:
                    pe("o3")
                    A(sq[:, 0, :], bank[3][:], ACT.Square).then_inc(dn_act, 1)
            def norms_log(h, before):
                if before is not None:
                    act.wait_ge(dn_pe, after(DN_PE, before, "o_squares"))
                    A(rs[:, 0, :], bank[5][:], ACT.Ln, scale=1.0 / P, bias=EPS).then_inc(dn_act, 1)
                if h is not None:
                    if before is None:
                        act.wait_ge(ba_turned, 1)
                        act.wait_ge(parts_low, 2)
                    else:
                        act.wait_ge(dn_dve, after(DN_DVE, before, "q"))
                    for i, (part, b) in enumerate(((1, 2), (0, 6))):
                        act.wait_ge(qk_sums, 2 * h + i + 1)
                        A(qk_rs[:, part, :], bank[b][:], ACT.Ln, bias=EPS).then_inc(qk_logs, 1)

            def norms_exp(h, before):
                if before is not None:
                    act.wait_ge(dn_act, after(DN_ACT, before, "o_log"))
                    A(rs[:, 0, :], rs[:, 0, :], ACT.Exp, scale=-0.5).then_inc(dn_act, 1)
                if h is not None:
                    for i, part in enumerate((1, 0)):
                        act.wait_ge(qk_logs, 2 * h + i + 1)
                        A(qk_rs[:, part, :], qk_rs[:, part, :], ACT.Exp, scale=-0.5, bias=-0.5 * math.log(P) * i
                          ).then_inc(qk_rstds, 1)

            def att_out(n, u):
                if u == 5:
                    pass
                elif not isinstance(n, int) or n > 0:
                    reader = ("v_turn0", "v_turn1", "score3", "score3", "score7")[u]
                    act.wait_ge(at_pe, after(AT_PE, n - 1, reader))
                elif u < 2:
                    act.wait_ge(dn_dve, after(DN_DVE, DN_HEADS - 1, "q"))
                elif u == 2:
                    act.wait_ge(dn_pe, after(DN_PE, DN_HEADS - 1, "v_turn"))
                elif u == 3:
                    act.wait_ge(dn_dve, all_done(DN_DVE, DN_HEADS))
                A(pre[:, u, :], bank[(U_ATT + u) % 2][:], ACT.Copy).then_inc(att_pre_ready, 1)

            def att(gap, n):
                def pe(name):
                    act.wait_ge(at_pe, after(AT_PE, n, name))

                if gap == 0:
                    for e in range(2):
                        pe(f"v_turn{e}")
                        A(v_tok[:, :, e * P:(e + 1) * P], bank[2 + e][:].rearrange("p (b c) -> p b c", b=TB), ACT.Copy
                          ).then_inc(at_act, 1)
                for i, (m, qb) in enumerate(SC):
                    if gap == 2 + 2 * i:
                        act.wait_ge(at_dve, after(AT_DVE, n, f"max{i}"))
                        e = ex[:, m, ex_block(qb)]
                        A(e, e, ACT.Exp, bias=neg_max[:, i:i + 1], accum_out=row_sum[:, i:i + 1]).then_inc(at_act, 1)
                for k in range(TB):
                    if gap == 22 + 2 * k:
                        pe(f"p_turn{k}")
                        w = (TB - k) * P
                        A(p_t[:, PT_OFF[k]:PT_OFF[k] + w], bank[2 + k % 2][:, 0:w], ACT.Copy).then_inc(at_act, 1)
                if gap == 31:
                    for e in range(2):
                        pe(f"pv{e}")
                        A(att_sq[:, e, :], bank[4 + e][:], ACT.Square).then_inc(at_act, 1)
                if gap == 33:
                    pe("squares")
                    A(att_rs[:, 0, :], bank[2][:], ACT.Ln, scale=1.0 / (2 * P), bias=EPS).then_inc(at_act, 1)
                    act.wait_ge(at_act, after(AT_ACT, n, "log"))
                    A(att_rs[:, 1, :], att_rs[:, 0, :], ACT.Exp, scale=-0.5).then_inc(at_act, 1)

            def head_window(h, before):
                span = S_HEADS(h)
                for gap in range(8 * CHUNKS):
                    if gap % CHUNKS == 0:
                        high(span, gap // CHUNKS)
                    if before is None:
                        if gap == 0:
                            gates_beta()
                        if gap == 13:
                            gate_columns()
                    else:
                        dn(gap, before)
                        if gap == 3:
                            z_out(before)
                    for j in range(3):
                        if gap == 8 * (j + 1):
                            half_done(act, span, 2 * j + 1)
                            conv_start(h, j)
                        if gap == 8 * (j + 1) + 3:
                            conv_end(h, j)
                    if gap == 23:
                        act.wait_ge(qk_squared, h + 1)
                        A(qk_high[:], qk_sq, ACT.Copy).then_inc(qk_high_ready, 1)
                    if gap == 31:
                        norms_log(h, before)
                        norms_exp(h, before)

            head_window(0, None)
            with act.Fori(1, DN_HEADS) as h:
                head_window(h, h - 1)

            def att_window(n, before):
                span = S_ATT(n)
                for gap in range(12 * CHUNKS):
                    if gap % CHUNKS == 0:
                        high(span, gap // CHUNKS)
                    if before is None:
                        if gap < 32:
                            dn(gap, DN_HEADS - 1)
                        if gap == 3:
                            z_out(DN_HEADS - 1)
                        if gap == 31:
                            norms_log(None, DN_HEADS - 1)
                            norms_exp(None, DN_HEADS - 1)
                    else:
                        if gap == 0:
                            half_done(act, span, -1)
                            att_out(before, 5)
                        att(gap, before)
                    for u in range(5):
                        if gap == 8 * (u + 1) + 1:
                            half_done(act, span, 2 * u + 1)
                            att_out(n, u)

            att_window(0, None)
            with act.Fori(1, DA_HEADS) as n:
                att_window(n, n - 1)

            half_done(act, S_OUT0, -1)
            att_out(DA_HEADS - 1, 5)
            act.wait_ge(at_dve, all_done(AT_DVE, DA_HEADS - 1))
            def mix_split(k):
                A(h_high[:, k:k + 2, :], mix[:, k:k + 2, :], ACT.Copy).then_inc(mix_high, 1)

            mix_split(0)
            mix_split(2)
            for gap in range(16 * CHUNKS):
                if gap % CHUNKS == 0:
                    high(S_OUT0, gap // CHUNKS)
                att(gap, DA_HEADS - 1)
                if gap < 5:
                    mix_split(4 + 2 * gap)
                if gap == 6:
                    act.wait_ge(mix_low, 7)
                    for t in range(TB):
                        act.dma_start(x1[:, t, :], x[0, t * P:(t + 1) * P, :]).then_inc(x_landed[t], 16)
                if gap == 35:
                    for e in range(2):
                        act.wait_ge(at_dve, after(AT_DVE, DA_HEADS - 1, f"o{e}"))
                        A(h_high[:, KT - 2 + e, :], att_o[:, e, :], ACT.Copy).then_inc(mix_high, 1)
            act.wait_ge(at_dve, all_done(AT_DVE, DA_HEADS))
            act.dma_start(w_row[:], ffn_norm_w[0:1, :].to_broadcast([P, D])).then_inc(row_landed, 16)
            with act.Fori(0, 3) as g:
                for j in range(4):
                    high(S_OUT1(g), j)
                for t in range(TB):
                    group_square(squares_out, t, g, 4 * g + 16 + t + 1, TB + 4 * g + t)
            high(S_OUT1_LAST, 0)
            for t in range(TB):
                if t == 3:
                    for j in (1, 2):
                        high(S_OUT1_LAST, j, by_block=True)
                group_square(squares_out, t, 3, 28 + t + 1, TB + 12 + t)
                if t % 2 == 1:
                    rstds(1, t // 2, PAIR[t // 2])
            high(S_OUT1_LAST, 3, by_block=True)
            high_parts(1)

            def gate_out(n, fb):
                if not isinstance(n, int) or 4 * n + fb >= 2:
                    act.wait_ge(hid_ready, 4 * n + fb - 1)
                A(gate_act[:, fb % 2, :], bank[2 + 2 * (fb % 2)][:], ACT.Silu).then_inc(gate_ready, 1)

            def hidden_high(n, fb):
                act.wait_ge(hid_ready, 4 * n + fb + 1)
                A(hid_high[:, fb, :], hidden[:, fb % 2, :], ACT.Copy).then_inc(hid_high_ready, 1)

            act.wait_ge(norm_scaled, TB + 16)
            act.dma_start(w_row[:], final_norm_w.rearrange("(a n) -> a n", a=1).to_broadcast([P, D])
                          ).then_inc(row_landed, 16)
            for j in range(16):
                high(S_FF0, j)
                if j % 4 == 2:
                    half_done(act, S_FF0, j - 1)
                    gate_out(0, j // 4)
                if j % 4 == 0 and j > 0:
                    hidden_high(0, j // 4 - 1)
            with act.Fori(1, FF_GROUPS) as n:
                span = S_FF(n)
                for j in range(24):
                    high(span, j)
                    if j == 0:
                        hidden_high(n - 1, 3)
                    if j in (2, 14, 18, 22):
                        half_done(act, span, j - 1)
                        gate_out(n, (j - 10) // 4 if j > 2 else 0)
                    if j == 12:
                        half_done(act, span, 11)
                    if j in (12, 16, 20):
                        hidden_high(n, (j - 12) // 4)
            hidden_high(FF_GROUPS - 1, 3)
            for j in range(8):
                high(S_END, j)
                if j in (1, 3):
                    for t in range(TB):
                        group_square(last_squares, t, j // 2, ADDED_END + 4 * (j // 2) + t + 1,
                                     TB + 16 + 4 * (j // 2) + t)
            for t in range(TB):
                for c in (2, 3):
                    group_square(last_squares, t, c, ADDED_END + 8 + 2 * t + c - 1, TB + 16 + 8 + 2 * t + c - 2)
                rstds(2, t, slice(t, t + 1))
                act.wait_ge(norm_rstd, 4 + t + 1)
                act.wait_ge(norm_scaled, TB + 16 + 8)
                A(x1[:, t, 0:D // 2], x1[:, t, 0:D // 2], ACT.Copy, scale=rstd[:, t:t + 1]).then_inc(out_scaled_act, 1)

        @block.vector
        def _(dve):
            V = nc.vector

            def low(span, j):
                if last_halves(span, j):
                    return
                s = span[0] + j + LEAD
                dve.wait_ge(w_high_ready, count(span, j + LEAD + 1))
                V.tensor_tensor(w_low[:, s % SLOTS, :], raw[:, (s // 2) % 2, (s % 2) * HALF:(s % 2 + 1) * HALF],
                                w_high[:, s % SLOTS, :].bitcast(F32), ALU.subtract).then_inc(w_low_ready, 1)

            V.memset(ones[:], 1.0).then_inc(dve_const, 1)
            V.memset(small[:], 0.0).then_inc(dve_const, 1)
            dve.wait_ge(dve_const, 1)
            V.tensor_copy(ones_r[:], ones[:]).then_inc(dve_const, 1)
            V.memset(state[:], 0.0).then_inc(dn_dve, 1)
            V.memset(resid[:], 0.0).then_inc(at_dve, 1)

            def times_row(r, t, cols_of):
                V.tensor_tensor(xn[:, t, cols_of], x1[:, t, cols_of], w_row[:, cols_of], ALU.mult).then_inc(norm_scaled, 1)

            def diagonals(r, pair):
                dve.wait_ge(norm_rstd, 2 * r + pair + 1)
                for t in (2 * pair, 2 * pair + 1):
                    V.tensor_scalar(diag[:, t, :], ident[:], rstd[:, t:t + 1], None, ALU.mult).then_inc(norm_diag, 1)

            def sums(two, n):
                dve.wait_ge(norm_sq, n)
                V.tensor_reduce(sum_sq[:, two], part_sq[:, two, :], AX.X, ALU.add).then_inc(norm_sum, 1)

            def low_parts(r):
                for t in range(TB):
                    for g in range(4):
                        dve.wait_ge(norm_high, 16 * r + 4 * t + g + 1)
                        at = (slice(None), slice(4 * g, 4 * g + 4), slice(t * P, (t + 1) * P))
                        V.tensor_tensor(h_low[at], bank[NORM_BANKS[t % 2][g]][:].rearrange("p (k i) -> p k i", k=4),
                                        h_high[at].bitcast(F32), ALU.subtract).then_inc(norm_low, 1)

            dve.wait_ge(row_landed, 16)
            dve.wait_ge(const_step, 2)
            for pair in range(2):
                for t in (2 * pair, 2 * pair + 1):
                    dve.wait_ge(x_landed[t], 16)
                    times_row(0, t, slice(0, D))
                diagonals(0, pair)
            low_parts(0)
            for j in range(-LEAD, 0):
                low((0, 0, 4), j)

            dve.wait_ge(params_landed, PARAMS)
            for i in range(2):
                V.tensor_tensor(lam_v[:, 2 * i, :], lam_v[:, 2 * i, :], lam_v[:, 2 * i + 1, :], ALU.mult).then_inc(lam_step, 1)
                dve.wait_ge(lam_step, 2 * i + 1)
                V.tensor_reduce(lam_dot[:, i:i + 1], lam_v[:, 2 * i, :], AX.X, ALU.add).then_inc(lam_step, 1)
            dve.wait_ge(lam_act, 1)
            V.scalar_tensor_tensor(out=lam, in0=lam_exp[:, 0:1], scalar=LAM_INIT, in1=lam_exp[:, 1:2],
                                   op0=ALU.add, op1=ALU.subtract).then_inc(lam_step, 1)
            V.tensor_scalar(da_w[:], da_w[:], 1.0 - LAM_INIT, None, ALU.mult).then_inc(lam_step, 1)
            low((0, 0, 4), 0)
            low((0, 0, 4), 1)

            def pick_taps(h):
                if isinstance(h, int):
                    dve.wait_ge(conv_ready, 1)
                else:
                    dve.wait_ge(conv_first, 3 * h)
                V.tensor_scalar(taps[:], conv_t[:, :, :, bass.ds(h, 1)].rearrange("p t j a -> p t (j a)"), 1.0, None,
                                ALU.mult).then_inc(taps_ready, 1)

            def gates_beta():
                steps = [0]

                def step(ins):
                    ins.then_inc(ba_dve, 1)
                    steps[0] += 1
                    dve.wait_ge(ba_dve, steps[0])

                half_done(dve, (0, 0, 4), 1)
                V.memset(row_parts[:].bitcast(F32), 0.0).then_inc(rows_clear, 1)
                V.tensor_copy(row_pick[0:16, :], ident[0:16, 0:16]).then_inc(rows_clear, 1)
                V.tensor_copy(row_pick[32:48, :], ident[32:48, 32:48]).then_inc(rows_clear, 1)
                dve.wait_ge(rows_clear, 3)
                dve.wait_ge(ba_act, 2)
                step(V.tensor_scalar(gates, bank[0][0:16, :], dt_col[0:16, :], 0.0, ALU.add, ALU.max))
                step(V.tensor_scalar(betas, betas, 1.0, None, ALU.add))
                step(V.reciprocal(betas, betas))
                dve.wait_ge(ba_act, 4)
                dve.wait_ge(lam_act, 2)
                step(V.tensor_tensor(exps[:, 0, :], gates, exps[:, 0, :], ALU.add))
                step(V.tensor_scalar(exps[:, 1, :], exps[:, 0, :], rate[0:16, :], -1.0, ALU.mult, ALU.mult))
                for c in range(TB):
                    at = slice(c * P, (c + 1) * P)
                    last = V.tensor_tensor_scan(gates[:, at], ones[0:16, :], exps[:, 1, at], 0.0, ALU.mult, ALU.add)
                step(last)
                assert steps[0] == 6

            def gate_columns():
                for i, rows in enumerate((gates, betas)):
                    dve.wait_ge(parts_high, i + 1)
                    V.tensor_tensor(row_parts[32:48, i, :], rows, row_parts[0:16, i, :].bitcast(F32), ALU.subtract
                                    ).then_inc(parts_low, 1)
                dve.wait_ge(ba_act, 6)
                V.tensor_copy(head_cols[:, 0:4, :], ba_t[:, 0:4, 8:16]).then_inc(ba_dve, 1)
                V.tensor_copy(head_cols[:, 4:8, :], ba_t[:, 4:8, 0:8]).then_inc(ba_dve, 1)
                V.scalar_tensor_tensor(out=head_cols[:, 8:12, :], in0=head_cols[:, 8:12, :], scalar=-1.0,
                                       in1=ba_t[:, 4:8, 0:8], op0=ALU.mult, op1=ALU.mult).then_inc(ba_dve, 1)

            def conv(h, j, k):
                if k == 1:
                    dve.wait_ge(conv_first, 3 * h + j + 1)
                else:
                    dve.wait_ge(conv_tap, 9 * h + 3 * j + k - 1)
                V.scalar_tensor_tensor(out=conv_acc[:, k:T], in0=bank[(U_HEADS + j) % 2][:, 0:T - k],
                                       scalar=taps[:, TAPS - 1 - k, j:j + 1], in1=conv_acc[:, k:T],
                                       op0=ALU.mult, op1=ALU.add).then_inc(conv_tap, 1)

            def pick_rows(h, before):
                if before is None:
                    dve.wait_ge(ba_dve, 9)
                    dve.wait_ge(parts_low, 2)
                else:
                    dve.wait_ge(dn_pe, after(DN_PE, before, "beta_rows"))
                for i, row in enumerate((h + DN_HEADS, h)):
                    V.tensor_scalar(picked[:, i, :], row_parts[:, i, :].bitcast(F32), row_pick[:, bass.ds(row, 1)],
                                    None, ALU.mult).then_inc(rows_picked, 1)

            gate_col, beta_col, nbg_col = cols[:, 0:4], cols[:, 4:8], cols[:, 8:12]
            spread = lambda col: col.rearrange("p (c a) -> p c a", a=1).to_broadcast([P, TB, P])

            def dn(gap, h):
                def pe(name):
                    dve.wait_ge(dn_pe, after(DN_PE, h, name))

                def act(name):
                    dve.wait_ge(dn_act, after(DN_ACT, h, name))

                def own(name):
                    dve.wait_ge(dn_dve, after(DN_DVE, h, name))

                if gap == 0:
                    dve.wait_ge(qk_rstds, 2 * h + 1)
                    V.tensor_tensor(kT[:], pre[:, 1, :], qk_rs[:, 1, :], ALU.mult).then_inc(dn_dve, 1)
                    dve.wait_ge(qk_rstds, 2 * h + 2)
                    V.tensor_tensor(qT[:], pre[:, 0, :], qk_rs[:, 0, :], ALU.mult).then_inc(dn_dve, 1)
                    V.tensor_scalar(cols[:], head_cols[:, :, bass.ds(h, 1)].rearrange("p r a -> p (r a)"), 1.0, None,
                                    ALU.mult).then_inc(dn_dve, 1)
                if gap == 1:
                    pe("gate_rows")
                    own("columns")
                    for c in range(TB):
                        at = slice(c * P, (c + 1) * P)
                        last = V.tensor_scalar(decay[:, at], bank[4][:, at], gate_col[:, c:c + 1], 0.0,
                                               ALU.subtract, ALU.min)
                    last.then_inc(dn_dve, 1)
                    V.tensor_tensor(ends[:, 0, :], bank[4][:, P - 1:T:P], gate_col, ALU.subtract).then_inc(dn_dve, 1)
                if gap == 2:
                    act("decay")
                    V.tensor_tensor(by_chunk(decay[:]), by_chunk(decay[:]),
                                    incl[:].rearrange("p (c i) -> p c i", c=1).to_broadcast([P, TB, P]), ALU.mult
                                    ).then_inc(dn_dve, 1)
                    own("decay_mask")
                    pe("beta_rows")
                    V.tensor_tensor(m_t, decay[:], bank[5][:], ALU.mult).then_inc(dn_dve, 1)
                if gap == 3:
                    pe("kk")
                    own("decay_beta")
                    V.tensor_tensor(m_t, m_t, bank[2][:], ALU.mult).then_inc(dn_dve, 1)
                    pe("kq")
                    V.tensor_tensor(decay[:], decay[:], bank[3][:], ALU.mult).then_inc(dn_dve, 1)
                    pe("v_turn")
                    V.tensor_tensor(by_chunk(bv), by_chunk(bank[6][:]), spread(beta_col), ALU.mult).then_inc(dn_dve, 1)
                if gap == 4:
                    pe("k_turn")
                    act("decay_end")
                    V.tensor_tensor(by_chunk(k_dec), by_chunk(bank[4][:]), spread(ends[:, 1, :]), ALU.mult
                                    ).then_inc(dn_dve, 1)
                    V.tensor_copy(ends[:, 2, :], q_dec[:, P - 1:T:P]).then_inc(dn_dve, 1)
                    own("chunk_decay")
                    V.tensor_tensor(q_dec, q_dec, qT[:], ALU.mult).then_inc(dn_dve, 1)
                if gap == 5:
                    dve.wait_ge(dn_pool, after(DN_POOL, h, "y0"))
                    V.transpose(xi[:], yi[:]).then_inc(dn_dve, 1)
                for l in range(1, 7):
                    if gap == 6 + 2 * l:
                        if l < 6:
                            pe(f"xmx{l}")
                            V.tensor_tensor(xi[:], xi[:], bank[4][:], ALU.subtract).then_inc(dn_dve, 1)
                        if l < 5:
                            own(f"x{l}")
                            V.transpose(yi[:], xi[:]).then_inc(dn_dve, 1)
                        else:
                            pe(f"xmx_turn{l}")
                            if l == 5:
                                to, turned = yi[:], bank[5][:]
                            else:
                                to = by_chunk(yi[0:64, :])[:, :, 64:P]
                                turned = by_chunk(bank[5][0:64, 0:T // 2])
                            V.tensor_tensor(to, to, turned, ALU.subtract).then_inc(dn_dve, 1)
                for c in range(TB):
                    at = slice(c * P, (c + 1) * P)
                    if gap == 18 + 3 * c and c > 0:
                        pe(f"ks{c}")
                        V.scalar_tensor_tensor(out=resid[:], in0=bank[2][:, at], scalar=nbg_col[:, c:c + 1], in1=bv[:, at],
                                               op0=ALU.mult, op1=ALU.add).then_inc(dn_dve, 1)
                    if gap == 20 + 3 * c and c < TB - 1:
                        pe(f"kv{c}")
                        if c == 0:
                            V.tensor_copy(state[:], bank[4][:, at]).then_inc(dn_dve, 1)
                        else:
                            V.scalar_tensor_tensor(out=state[:], in0=state[:], scalar=ends[:, 2, c:c + 1],
                                                   in1=bank[4][:, at], op0=ALU.mult, op1=ALU.add).then_inc(dn_dve, 1)
                if gap == 31:
                    act("o_rstd")
                    V.scalar_tensor_tensor(out=rs[:, 1, :], in0=bank[3][:], scalar=dn_w[:, 0:1], in1=rs[:, 0, :],
                                           op0=ALU.mult, op1=ALU.mult).then_inc(dn_dve, 1)
                    own("o_scaled")
                    V.tensor_tensor(mix[:, bass.ds(h, 1), :].rearrange("p a n -> p (a n)"), rs[:, 1, :], pre[:, 3, :],
                                    ALU.mult).then_inc(dn_dve, 1)

            def att(gap, n):
                def act(name):
                    dve.wait_ge(at_act, after(AT_ACT, n, name))

                def own(name):
                    dve.wait_ge(at_dve, after(AT_DVE, n, name))

                if gap == 0:
                    dve.wait_ge(const_step, CONSTS)
                    dve.wait_ge(at_pe, after(AT_PE, n, "v_turn1"))
                    V.tensor_scalar(bias_h[:], base_bias[:], slopes[:, bass.ds(n, 1)], None, ALU.mult).then_inc(at_dve, 1)
                for i, (m, qb) in enumerate(SC):
                    if gap == 1 + 2 * i:
                        dve.wait_ge(at_pe, after(AT_PE, n, f"score{i}"))
                        own("bias")
                        e = ex[:, m, ex_block(qb)]
                        w = (qb + 1) * P
                        V.scalar_tensor_tensor(out=e, in0=bank[2 + i % 2][:, 0:w], scalar=float(P) ** -0.5,
                                               in1=bias_h[:, T - w:T], op0=ALU.mult, op1=ALU.add).then_inc(at_dve, 1)
                        own(f"score{i}")
                        V.tensor_reduce(neg_max[:, i:i + 1], e, AX.X, ALU.max, negate=True).then_inc(at_dve, 1)
                if gap == 18:
                    act("exp7")
                    V.reciprocal(inv_sum[:], row_sum[:]).then_inc(at_dve, 1)
                    own("rsum")
                    V.tensor_scalar(inv_sum[:, 4:8], inv_sum[:, 4:8], lam, None, ALU.mult).then_inc(at_dve, 1)
                    own("rsum_lam")
                for q in range(TB):
                    if gap == 18 + q // 2:
                        V.tensor_scalar(ex[:, 1, ex_block(q)], ex[:, 1, ex_block(q)], inv_sum[:, 4 + q:5 + q], None,
                                        ALU.mult).then_inc(at_dve, 1)
                        own(f"p_low{q}")
                        V.scalar_tensor_tensor(out=ex[:, 0, ex_block(q)], in0=ex[:, 0, ex_block(q)],
                                               scalar=inv_sum[:, q:q + 1], in1=ex[:, 1, ex_block(q)],
                                               op0=ALU.mult, op1=ALU.subtract).then_inc(at_dve, 1)
                if gap == 33:
                    act("rstd")
                    for e in range(2):
                        if isinstance(n, int):
                            to = att_o[:, e, :]
                        else:
                            to = mix[:, bass.ds(2 * n + DN_HEADS + e, 1), :].rearrange("p a n -> p (a n)")
                        V.scalar_tensor_tensor(out=to, in0=bank[4 + e][:], scalar=da_w[:, e:e + 1],
                                               in1=att_rs[:, 1, :], op0=ALU.mult, op1=ALU.mult).then_inc(at_dve, 1)

            def head_window(h, before):
                span = S_HEADS(h)
                for gap in range(8 * CHUNKS):
                    if gap == 6 and before is None:
                        dve.wait_ge(param_turned, 1)
                        V.tensor_copy(conv_t[:].rearrange("p t j h -> p (t j h)"), bank[7][:, 0:TAPS * 24]
                                      ).then_inc(conv_ready, 1)
                    if gap == 6:
                        pick_taps(h)
                    if gap == 24:
                        pick_rows(h, before)
                    if before is None:
                        if gap == 0:
                            gates_beta()
                        if gap == 13:
                            gate_columns()
                    else:
                        dn(gap, before)
                    if gap % CHUNKS == 1:
                        low(span, gap // CHUNKS)
                    for j in range(3):
                        for k in range(1, TAPS):
                            if gap == 8 * (j + 1) + k - 1:
                                conv(h, j, k)

            head_window(0, None)
            with dve.Fori(1, DN_HEADS) as h:
                head_window(h, h - 1)

            def att_window(n, before):
                span = S_ATT(n)
                for gap in range(12 * CHUNKS):
                    if before is None:
                        if gap < 32:
                            dn(gap, DN_HEADS - 1)
                    else:
                        att(gap, before)
                    if gap % CHUNKS == 1:
                        low(span, gap // CHUNKS)

            att_window(0, None)
            with dve.Fori(1, DA_HEADS) as n:
                att_window(n, n - 1)

            def mix_split(k):
                dve.wait_ge(mix_high, k // 2 + 1)
                V.tensor_tensor(h_low[:, k:k + 2, :], mix[:, k:k + 2, :], h_high[:, k:k + 2, :].bitcast(F32),
                                ALU.subtract).then_inc(mix_low, 1)

            mix_split(0)
            mix_split(2)

            def add_block(span, j, t, cols_of, x_loaded=False, c=None, b=None):
                if x_loaded:
                    dve.wait_ge(x_landed[t], 32)
                chunk_done(dve, span, j, t if c is None else c)
                at = x1[:, t, cols_of]
                V.tensor_tensor(at, at, bank[OUT_BANKS[t] if b is None else b][:], ALU.add).then_inc(out_added, 1)

            for gap in range(16 * CHUNKS):
                j = gap // CHUNKS
                if gap % CHUNKS == 0:
                    low(S_OUT0, j)
                att(gap, DA_HEADS - 1)
                if gap < 5:
                    mix_split(4 + 2 * gap)
                if gap == 35:
                    for e in range(2):
                        dve.wait_ge(mix_high, 8 + e)
                        V.tensor_tensor(h_low[:, KT - 2 + e, :], att_o[:, e, :], h_high[:, KT - 2 + e, :].bitcast(F32),
                                        ALU.subtract).then_inc(mix_low, 1)
                if j % 4 == 3:
                    add_block(S_OUT0, j, gap % CHUNKS, slice(j // 4 * T, (j // 4 + 1) * T), x_loaded=True)
            def out_times_row(g, t):
                dve.wait_ge(row_landed, 32)
                dve.wait_ge(out_added, 4 * g + 16 + t + 1)
                times_row(1, t, bass.ds(g * T, T))

            with dve.Fori(0, 3) as g:
                for j in range(4):
                    low(S_OUT1(g), j)
                for t in range(TB):
                    add_block(S_OUT1(g), 3, t, bass.ds(g * T, T))
                for t in range(TB):
                    out_times_row(g, t)
            low(S_OUT1_LAST, 0)
            for t in range(TB):
                if t == 3:
                    for j in (1, 2):
                        low(S_OUT1_LAST, j)
                add_block(S_OUT1_LAST, t, t, slice(D - T, D), c=3)
                out_times_row(3, t)
                if t % 2 == 1:
                    sums(PAIR[t // 2], TB + 12 + t + 1)
                    diagonals(1, t // 2)
            low(S_OUT1_LAST, 3)
            low_parts(1)

            def product(n, fb):
                dve.wait_ge(gate_ready, 4 * n + fb + 1)
                V.tensor_tensor(hidden[:, fb % 2, :], gate_act[:, fb % 2, :], bank[3 + 2 * (fb % 2)][:], ALU.mult
                                ).then_inc(hid_ready, 1)

            def hidden_low(n, fb):
                dve.wait_ge(hid_high_ready, 4 * n + fb + 1)
                V.tensor_tensor(hid_low[:, fb, :], hidden[:, fb % 2, :], hid_high[:, fb, :].bitcast(F32), ALU.subtract
                                ).then_inc(hid_low_ready, 1)

            for j in range(16):
                low(S_FF0, j)
                if j % 4 == 0 and j > 0:
                    half_done(dve, S_FF0, j - 1)
                    product(0, j // 4 - 1)
                    hidden_low(0, j // 4 - 1)
            with dve.Fori(1, FF_GROUPS) as n:
                span = S_FF(n)
                for j in range(24):
                    if j == 0:
                        half_done(dve, span, -1)
                        product(n - 1, 3)
                        hidden_low(n - 1, 3)
                    low(span, j)
                    if j in (4, 16, 20):
                        half_done(dve, span, j - 1)
                        product(n, (j - 12) // 4 if j > 4 else 0)
                    if j in (12, 16, 20):
                        hidden_low(n, (j - 12) // 4)
                    if j in (5, 7, 9, 11):
                        for t in range(TB):
                            add_block(span, j, t, slice((j - 5) // 2 * T, (j - 3) // 2 * T))
            half_done(dve, S_END, -1)
            product(FF_GROUPS - 1, 3)
            hidden_low(FF_GROUPS - 1, 3)
            for j in range(8):
                low(S_END, j)
                if j in (1, 3):
                    for t in range(TB):
                        add_block(S_END, j, t, slice(j // 2 * T, (j // 2 + 1) * T))
                if j in (2, 4):
                    dve.wait_ge(row_landed, 48)
                    c = j // 2 - 1
                    for t in range(TB):
                        dve.wait_ge(norm_sq, TB + 16 + 4 * c + t + 1)
                        at = slice(c * T, (c + 1) * T)
                        V.tensor_tensor(x1[:, t, at], x1[:, t, at], w_row[:, at], ALU.mult).then_inc(norm_scaled, 1)

            def scale_block(t):
                dve.wait_ge(norm_rstd, 4 + t + 1)
                at = slice(D // 2, D)
                V.scalar_tensor_tensor(out=x1[:, t, at], in0=x1[:, t, at], scalar=rstd[:, t:t + 1], in1=w_row[:, at],
                                       op0=ALU.mult, op1=ALU.mult).then_inc(out_scaled, 1)

            for t in range(TB):
                add_block(S_END, 4 + t, t, slice(2 * T, 3 * T), c=1, b=END_BANKS[t % 2][0])
                if t > 0:
                    scale_block(t - 1)
                add_block(S_END, 4 + t, t, slice(3 * T, D), c=3, b=END_BANKS[t % 2][1])
                sums(slice(t, t + 1), TB + 16 + 8 + 2 * t + 2)
            scale_block(TB - 1)

        @block.tensor
        def _(pe):
            M = nc.tensor.matmul

            def turn(out_ap, in_ap, n=P):
                return nc.tensor.transpose(out_ap, in_ap, ident[0:n, 0:n])

            def three(out_ap, stat, mov, start, stop):
                M(out_ap, stat[0], mov[0], start=start, stop=False, skip_group_check=True)
                M(out_ap, stat[0], mov[1], start=False, stop=False, skip_group_check=True)
                return M(out_ap, stat[1], mov[0], start=False, stop=stop, skip_group_check=True)

            def weights(slot, at):
                return w_high[:, slot, at], w_low[:, slot, at]

            def half_ready(span, j):
                pe.wait_ge(w_low_ready, count(span, j + 1))

            def column_chunk(span, j, c, b, part):
                slot = (span[0] + j) % SLOTS
                if c == 0:
                    half_ready(span, j)
                for kk in (2 * c, 2 * c + 1):
                    k = 8 * part + kk
                    last = three(bank[b][:], weights(slot, slice(kk * P, (kk + 1) * P)), (h_high[:, k, :], h_low[:, k, :]),
                                 k == 0, k == KT - 1)
                last.then_inc(chunks_done, 1)

            def row_chunk(span, j, t, acts, k0, start, stop, b=None):
                slot = (span[0] + j) % SLOTS
                if t == 0:
                    half_ready(span, j)
                for kk in range(2):
                    last = three(bank[OUT_BANKS[t] if b is None else b][:], tuple(a[:, k0 + kk, t * P:(t + 1) * P] for a in acts),
                                 weights(slot, slice(kk * T, (kk + 1) * T)), start and kk == 0, stop and kk == 1)
                last.then_inc(chunks_done, 1)

            pe.wait_ge(const_step, CONSTS)
            pe.wait_ge(dve_const, 3)

            def norm(r, scaled):
                for t in range(TB):
                    pe.wait_ge(norm_scaled, scaled + t + 1)
                    pe.wait_ge(norm_diag, TB * r + t + 1)
                    for g in range(4):
                        b = NORM_BANKS[t % 2][g]
                        if r == 1 and t == 1 and g == 0:
                            pe.wait_ge(out_added, 32)
                        if t >= 2:
                            pe.wait_ge(norm_low, 16 * r + 4 * (t - 2) + g + 1)
                        for k in range(4):
                            at = slice((4 * g + k) * P, (4 * g + k + 1) * P)
                            last = M(bank[b][:, k * P:(k + 1) * P], xn[:, t, at], diag[:, t, :], start=True, stop=True)
                        last.then_inc(norm_turned, 1)

            norm(0, 0)
            pe.wait_ge(norm_low, 16)
            for j in range(2):
                for c in range(CHUNKS):
                    column_chunk((0, 0, 4), j, c, 0, j)

            def gates_turned():
                pe.wait_ge(ba_dve, 6)
                for i, rows in enumerate((gates, betas)):
                    for c in range(TB):
                        last = turn(bank[2][:, (4 * i + c) * 16:(4 * i + c + 1) * 16], rows[:, c * P:(c + 1) * P], 16)
                last.then_inc(ba_turned, 1)

            def qk_norms(h, before):
                pe.wait_ge(qk_low_ready, h + 1)
                if before is not None:
                    pe.wait_ge(dn_dve, after(DN_DVE, before, "r3"))
                    pe.wait_ge(dn_act, after(DN_ACT, before, "vn3"))
                for i, b in ((1, 2), (0, 6)):
                    M(bank[b][:], ones_r[:], qk_high[:, i, :], start=True, stop=False)
                    M(bank[b][:], ones_r[:], qk_low[:, i, :], start=False, stop=True).then_inc(qk_sums, 1)

            def dn(gap, h):
                def act(name):
                    pe.wait_ge(dn_act, after(DN_ACT, h, name))

                def dve(name):
                    pe.wait_ge(dn_dve, after(DN_DVE, h, name))

                def pool(name):
                    pe.wait_ge(dn_pool, after(DN_POOL, h, name))

                def chunks(b, stat, mov):
                    for c in range(TB):
                        at = slice(c * P, (c + 1) * P)
                        last = M(bank[b][:, at], stat[:, at], mov[:, at], start=True, stop=True)
                    last.then_inc(dn_pe, 1)

                def halves(b, stat, mov):
                    for c in range(TB):
                        last = M(bank[b][0:64, c * 64:(c + 1) * 64], stat(c), mov(c), start=True, stop=True)
                    last.then_inc(dn_pe, 1)

                def turns(b, src):
                    for c in range(TB):
                        last = turn(bank[b][:, c * P:(c + 1) * P], src[:, c * P:(c + 1) * P])
                    last.then_inc(dn_pe, 1)

                if gap == 0:
                    pe.wait_ge(rows_picked, 2 * h + 1)
                    M(bank[4][:], ones_r[0:48, :], picked[:, 0, :], start=True, stop=True).then_inc(dn_pe, 1)
                if gap == 1:
                    pe.wait_ge(qk_logs, 2 * h + 2)
                    pe.wait_ge(rows_picked, 2 * h + 2)
                    M(bank[5][:], ones_r[0:48, :], picked[:, 1, :], start=True, stop=True).then_inc(dn_pe, 1)
                    pe.wait_ge(pre_ready, 4 * h + 3)
                    turns(6, pre[:, 2, :])
                if gap == 3:
                    dve("k")
                    chunks(2, kT[:], kT[:])
                    dve("q")
                    chunks(3, kT[:], qT[:])
                if gap == 4:
                    dve("gap_end")
                    act("decay_start")
                    turns(4, kT[:])
                for l in range(1, 7):
                    if gap == 5 + 2 * l:
                        if l < 6:
                            pool(f"level{l}")
                        if l == 1:
                            dve("x0")
                        else:
                            dve(f"x{l - 1}")
                        if l < 6:
                            chunks(3, level_m[:, l % 2, :], xi[:])
                        else:
                            halves(3, lambda c: m_t[:, c * P + 64:(c + 1) * P], lambda c: xi[:, c * P:c * P + 64])
                    if gap == 6 + 2 * l:
                        act(f"mx{l}")
                        if l == 1:
                            dve("k_dec")
                        else:
                            dve(f"y{l - 1}")
                        if l < 6:
                            chunks(4, yi[:], mxs)
                        if l == 5:
                            chunks(5, mxs, yi[:])
                        if l == 6:
                            halves(5, lambda c: mxs[:, c * 64:(c + 1) * 64], lambda c: yi[:, c * P + 64:(c + 1) * P])
                for c in range(TB):
                    at = slice(c * P, (c + 1) * P)
                    if gap == 18 + 3 * c and c > 0:
                        dve(f"s{c - 1}")
                        M(bank[2][:, at], kT[:, at], state[:], start=True, stop=True).then_inc(dn_pe, 1)
                    if gap == 19 + 3 * c:
                        dve(f"r{c}" if c else "y6")
                        M(bank[6][:, at], yi[:, at], resid[:] if c else bv[:, at], start=True, stop=True).then_inc(dn_pe, 1)
                    if gap == 20 + 3 * c:
                        if c:
                            dve("q_dec")
                            M(bank[3][:, at], state[:], q_dec[:, at], start=True, stop=False)
                        act(f"vn{c}")
                        M(bank[3][:, at], v_new[:, c % 2, :], decay[:, at], start=(c == 0), stop=True).then_inc(dn_pe, 1)
                        if c < TB - 1:
                            M(bank[4][:, at], k_dec[:, at], v_new[:, c % 2, :], start=True, stop=True).then_inc(dn_pe, 1)
                if gap == 30:
                    act("o_square")
                    M(bank[5][:], ones[:], sq[:, 0, :], start=True, stop=True).then_inc(dn_pe, 1)

            def att(gap, n):
                def act(name):
                    pe.wait_ge(at_act, after(AT_ACT, n, name))

                def dve(name):
                    pe.wait_ge(at_dve, after(AT_DVE, n, name))

                if gap == 0:
                    pe.wait_ge(at_dve, all_done(AT_DVE, n))
                    pe.wait_ge(dn_dve, all_done(DN_DVE, DN_HEADS))
                    pe.wait_ge(att_pre_ready, 6 * n + 2)
                    for e in range(2):
                        for k in range(TB):
                            last = turn(bank[2 + e][:, k * P:(k + 1) * P], pre[:, e, k * P:(k + 1) * P])
                        last.then_inc(at_pe, 1)
                for i, (m, qb) in enumerate(SC):
                    if gap == 1 + 2 * i:
                        pe.wait_ge(att_pre_ready, 6 * n + (4 if m == 0 else 6))
                        if i < 2:
                            act(f"v{i}")
                        else:
                            dve(f"score{i - 2}")
                        w = (qb + 1) * P
                        M(bank[2 + i % 2][:, 0:w], pre[:, 2 + 2 * m, qb * P:(qb + 1) * P], pre[:, 3 + 2 * m, 0:w],
                          start=True, stop=True).then_inc(at_pe, 1)
                for k in range(TB):
                    if gap == 22 + 2 * k:
                        if k < 2:
                            dve("p3")
                        else:
                            act(f"p{k - 2}")
                        for q in range(k, TB):
                            at = ex_block(q).start + k * P
                            last = turn(bank[2 + k % 2][:, (q - k) * P:(q - k + 1) * P], ex[:, 0, at:at + P])
                        last.then_inc(at_pe, 1)
                if gap in (30, 31):
                    e = gap - 30
                    act("p3")
                    for k in range(TB):
                        w = (TB - k) * P
                        last = M(bank[4 + e][:, k * P:T], v_tok[:, k, e * P:(e + 1) * P], p_t[:, PT_OFF[k]:PT_OFF[k] + w],
                                 start=(k == 0), stop=(k == TB - 1), skip_group_check=True)
                    last.then_inc(at_pe, 1)
                if gap == 33:
                    act("square1")
                    M(bank[2][:], ones[:], att_sq[:, 0, :], start=True, stop=False)
                    M(bank[2][:], ones[:], att_sq[:, 1, :], start=False, stop=True).then_inc(at_pe, 1)

            def head_unit_ready(h, j):
                first = isinstance(h, int)
                if j == 0 and not first:
                    pe.wait_ge(conv_tap, 9 * h)
                if j == 1:
                    if first:
                        pe.wait_ge(ba_act, 2)
                        pe.wait_ge(ba_dve, 1)
                    else:
                        pe.wait_ge(pre_ready, 4 * h)
                if j >= 2:
                    pe.wait_ge(conv_tap, 9 * h + 3 * (j - 1))

            def head_window(h, before):
                span = S_HEADS(h)
                for gap in range(8 * CHUNKS):
                    j, c = divmod(gap, CHUNKS)
                    if gap % 8 == 0:
                        head_unit_ready(h, gap // 8)
                    column_chunk(span, j, c, (U_HEADS + j // 2) % 2, j % 2)
                    if before is None:
                        if gap == 2:
                            pe.wait_ge(params_landed, PARAMS)
                            turn(bank[7][:, 0:TAPS * 24], conv_rows[0:TAPS * 24, :], TAPS * 24).then_inc(param_turned, 1)
                        if gap == 12:
                            gates_turned()
                    else:
                        dn(gap, before)
                    if gap == 30:
                        qk_norms(h, before)

            head_window(0, None)
            with pe.Fori(1, DN_HEADS) as h:
                head_window(h, h - 1)

            def att_window(n, before):
                span = S_ATT(n)
                for gap in range(12 * CHUNKS):
                    j, c = divmod(gap, CHUNKS)
                    if gap % 8 == 0:
                        u = gap // 8
                        if before is None and u < 2:
                            if u == 0:
                                pe.wait_ge(conv_tap, 9 * DN_HEADS)
                            else:
                                pe.wait_ge(pre_ready, 4 * DN_HEADS)
                        else:
                            pe.wait_ge(att_pre_ready, 6 * n + u - 1)
                    column_chunk(span, j, c, (U_ATT + j // 2) % 2, j % 2)
                    if before is None:
                        if gap < 32:
                            dn(gap, DN_HEADS - 1)
                    else:
                        att(gap, before)

            att_window(0, None)
            with pe.Fori(1, DA_HEADS) as n:
                att_window(n, n - 1)

            h_parts = (h_high, h_low)
            pe.wait_ge(att_pre_ready, 6 * DA_HEADS)
            for gap in range(16 * CHUNKS):
                j, t = divmod(gap, CHUNKS)
                if j < 4 and t == 0:
                    pe.wait_ge(mix_low, j + 1)
                if j % 4 == 0 and j > 0:
                    pe.wait_ge(out_added, j - 4 + t + 1)
                if gap == 0:
                    att(gap, DA_HEADS - 1)
                row_chunk(S_OUT0, j, t, h_parts, 2 * (j % 4), j % 4 == 0, j % 4 == 3)
                if gap > 0:
                    att(gap, DA_HEADS - 1)
            pe.wait_ge(mix_low, 9)
            with pe.Fori(0, 3) as g:
                for j in range(4):
                    for t in range(TB):
                        if j == 0:
                            pe.wait_ge(out_added, 4 * g + 12 + t + 1)
                        row_chunk(S_OUT1(g), j, t, h_parts, 8 + 2 * j, j == 0, j == 3)
            for t in range(TB):
                pe.wait_ge(out_added, 24 + t + 1)
                for j in range(4):
                    row_chunk(S_OUT1_LAST, j, t, h_parts, 8 + 2 * j, j == 0, j == 3)
            norm(1, TB + 12)
            pe.wait_ge(norm_low, 32)

            def pair(span, j0, n, fb):
                if not isinstance(n, int) or 4 * n + fb >= 2:
                    pe.wait_ge(hid_ready, 4 * n + fb - 1)
                for j in range(4):
                    for c in range(CHUNKS):
                        column_chunk(span, j0 + j, c, 2 + 2 * (fb % 2) + j // 2, j % 2)

            def down(span, j0, n, added, halves=8):
                pe.wait_ge(hid_low_ready, 4 * n + 4)
                for j in range(halves):
                    for t in range(TB):
                        if j % 2 == 0:
                            pe.wait_ge(out_added, added + 4 * (j // 2) - 4 + t + 1)
                        row_chunk(span, j0 + j, t, (hid_high, hid_low), 2 * (j % 2), j % 2 == 0, j % 2 == 1)

            for fb in range(4):
                pair(S_FF0, 4 * fb, 0, fb)
            with pe.Fori(1, FF_GROUPS) as n:
                pair(S_FF(n), 0, n, 0)
                down(S_FF(n), 4, n - 1, 16 * n + 16)
                for fb in range(1, 4):
                    pair(S_FF(n), 8 + 4 * fb, n, fb)
            down(S_END, 0, FF_GROUPS - 1, ADDED_END, halves=4)
            for t in range(TB):
                pe.wait_ge(out_added, ADDED_END + (4 + 2, 8, 8 + 2, 8 + 4)[t])
                for j in range(4, 8):
                    row_chunk(S_END, j, t, (hid_high, hid_low), 2 * (j % 2), j % 2 == 0, j % 2 == 1,
                              b=END_BANKS[t % 2][j // 2 - 2])
    return nc


_INS = ["x", "attn_norm_w", "w_in", "conv_w", "a_log", "dt_bias", "dn_norm_w", "lam_q1", "lam_k1", "lam_q2", "lam_k2",
        "da_norm_w", "w_out", "ffn_norm_w", "w_gate", "w_up", "w_down", "final_norm_w"]


def kernel(**inputs):
    import numpy as _np
    import concourse.bacc as _bacc
    from concourse import mybir as _mybir
    from concourse.bass_utils import run_bass_kernel_spmd as _run

    nc = _bacc.Bacc("TRN2", target_bir_lowering=False, num_devices=1)
    arrays, args = {}, []
    for name in _INS:
        a = _np.ascontiguousarray(inputs[name])
        arrays[f"in_{name}_dram"] = a
        args.append(nc.dram_tensor(f"in_{name}_dram", a.shape, _mybir.dt.from_np(a.dtype), kind="ExternalInput").ap())
    args.append(nc.dram_tensor("out_0_dram", (1, T, D), F32, kind="ExternalOutput").ap())
    build(nc, *args)
    r = _run(nc, [arrays], core_ids=[0])
    return r.results[0]["out_0_dram"]
```

```python
import math
from contextlib import ExitStack

import concourse.bass as bass
from concourse import mybir

F32 = mybir.dt.float32
F32R = mybir.dt.float32r
ACT = mybir.ActivationFunctionType
ALU = mybir.AluOpType
AX = mybir.AxisListType

P = 128
T = 512
D = 2048
TB = T // P
KT = D // P
DN_HEADS, DA_HEADS = 8, 4
TAPS = 4
D_FF = 5632
DN_WIDTH = DN_HEADS * P
OFF_Z = 3 * DN_WIDTH
OFF_B = OFF_Z + DN_WIDTH
OFF_Q = OFF_B + 2 * DN_HEADS
OFF_K = OFF_Q + DA_HEADS * 2 * P
OFF_V = OFF_K + DA_HEADS * 2 * P
EPS = 1e-6
LAM_INIT = 0.8 - 0.6 * math.exp(0.0)
FAR = -1e30

UNIT = 2048
HALF = UNIT // 2
SLOTS = 4
LEAD = 3
CHUNKS = 4
FF_GROUPS = D_FF // (4 * P)
U_HEADS = 1
U_ATT = U_HEADS + 4 * DN_HEADS
U_OUT = U_ATT + 6 * DA_HEADS
U_FF = U_OUT + 16
UNITS = U_FF + 12 * FF_GROUPS
HALVES = 2 * UNITS
EXP_WIDTH = P * TB * (TB + 1) // 2

DN_PE = (["gate_rows", "beta_rows", "v_turn", "kk", "kq", "k_turn"]
         + [f"{s}{l}" for l in range(1, 6) for s in ("mx", "xmx")] + ["xmx_turn5", "mx6", "xmx_turn6"]
         + ["vn0", "o0", "kv0"] + [f"{s}{c}" for c in (1, 2) for s in ("ks", "vn", "o", "kv")]
         + ["ks3", "vn3", "o3", "o_squares"])
DN_ACT = (["decay", "decay_start", "decay_end"]
          + [f"mx{l}" for l in range(1, 7)] + [f"vn{c}" for c in range(4)] + ["o_square", "o_high", "o_log", "o_rstd"])
DN_DVE = (["k", "q", "columns", "gaps", "gap_end", "decay_mask", "decay_beta", "m", "m_diag", "level0",
           "y0", "x0", "a", "bv", "k_dec", "chunk_decay", "q_dec"]
          + [s for l in range(1, 5) for s in (f"x{l}", f"y{l}")] + ["y_full", "x5", "y5", "y6"]
          + ["s0"] + [s for c in (1, 2) for s in (f"r{c}", f"s{c}")] + ["r3", "o_low", "o_scaled", "o"])
DN_POOL = ["m_diag", "level1", "y_clear"] + [f"level{l}" for l in range(2, 6)]

SC = [(m, qb) for m in range(2) for qb in range(TB)]
AT_PE = ([f"score{i}" for i in range(8)] + [f"p_turn{k}" for k in range(TB)]
         + ["pv0", "pv1", "squares"])
AT_ACT = (["v0", "v1"] + [f"exp{i}" for i in range(8)] + [f"p{k}" for k in range(TB)]
          + ["square0", "square1", "log", "rstd"])
AT_DVE = (["bias"] + [s for i in range(8) for s in (f"score{i}", f"max{i}")] + ["rsum", "rsum_lam"]
          + [s for q in range(TB) for s in (f"p_low{q}", f"p{q}")] + ["o0", "o1"])


PT_OFF = [sum(TB - i for i in range(k)) * P for k in range(TB)]


def ex_block(qb):
    return slice(P * qb * (qb + 1) // 2, P * (qb + 1) * (qb + 2) // 2)


def after(steps, head, name):
    return head * len(steps) + steps.index(name) + 1 + FIRST[id(steps)]


CONSTS = 3 + 3 * 6 + 2 + 2 + 3 * 4 + 1 + DA_HEADS
FIRST = {id(DN_PE): 0, id(DN_ACT): 0, id(DN_DVE): 1, id(DN_POOL): 0, id(AT_PE): 0, id(AT_ACT): 0, id(AT_DVE): 1}


def all_done(steps, heads):
    return heads * len(steps) + FIRST[id(steps)]


def build(nc, x, attn_norm_w, w_in, conv_w, a_log, dt_bias, dn_norm_w, lam_q1, lam_k1, lam_q2, lam_k2,
          da_norm_w, w_out, ffn_norm_w, w_gate, w_up, w_down, final_norm_w, out):
    stack = ExitStack()

    def sb(name, shape, dt=F32, where=stack):
        return where.enter_context(nc.sbuf_tensor(name, shape, dt))

    def sem(name):
        return stack.enter_context(nc.semaphore(name))

    with stack:
        bank = [stack.enter_context(nc.psum_tensor(f"bank{i}", [P, 512], F32)) for i in range(8)]

        packed = lambda t: t.rearrange("p (c i) -> p c i", i=64)
        by_chunk = lambda t: t.rearrange("p (c i) -> p c i", c=TB)

        raw = sb("raw", [P, 2, UNIT])
        w_high = sb("w_high", [P, SLOTS, HALF], F32R)
        w_low = sb("w_low", [P, SLOTS, HALF], F32R)
        h_high = sb("h_high", [P, KT, T], F32R)
        h_low = sb("h_low", [P, KT, T], F32R)
        x1 = sb("x1", [P, TB, D])
        mix = x1[:].rearrange("p t (k n) -> p (t k) n", n=T)
        ident = sb("ident", [P, P])
        ones = sb("ones", [P, P])
        part_sq = sb("part_sq", [P, TB, 4])
        ones_r = sb("ones_r", [P, P], F32R)
        small = sb("small", [P, 64])
        conv_rows = sb("conv_rows", [P, P])
        conv_t = sb("conv_t", [P, TAPS, 3, DN_HEADS])
        dn_w = sb("dn_w", [P, 1])
        da_w = sb("da_w", [P, 2])
        slopes = sb("slopes", [P, DA_HEADS])
        base_bias = sb("base_bias", [P, T])
        incl = sb("incl", [P, P])
        levels = sb("levels", [P, 6, 64])
        ident_q = sb("ident_q", [P, 64])
        sum_sq = small[:, 0:4]
        rstd_log = small[:, 4:8]
        rstd = small[:, 8:12]
        lam_dot = small[:, 12:14]
        lam_exp = small[:, 14:16]
        lam = small[:, 16:17]
        rate = small[:, 17:18]
        dt_col = small[:, 18:19]
        alog_col = small[:, 19:20]

        heads = ExitStack()
        stack.enter_context(heads)
        pre = sb("pre", [P, 6, T], where=heads)
        deltanet = ExitStack()
        heads.enter_context(deltanet)
        d = lambda name, shape: sb(name, shape, where=deltanet)
        conv_acc = d("conv_acc", [P, T])
        row_parts = sb("row_parts", [48, 2, T], F32R, where=deltanet)
        head_cols = d("head_cols", [P, 12, DN_HEADS])
        cols = d("cols", [P, 12])
        taps = d("taps", [P, TAPS, 3])
        ba_t = d("ba_t", [P, 8, 16])
        picked = sb("picked", [48, 2, T], F32R, where=deltanet)
        sq = d("sq", [P, 2, T])
        rs = d("rs", [P, 2, T])
        o_high = sb("o_high", [P, T], F32R, where=deltanet)
        o_low = sb("o_low", [P, T], F32R, where=deltanet)
        kT, qT = d("kT", [P, T]), d("qT", [P, T])
        decay = d("decay", [P, T])
        qk_high = sb("qk_high", [P, 2, T], F32R, where=deltanet)
        qk_low = sb("qk_low", [P, 2, T], F32R, where=deltanet)
        level_m, mxs = sq, rs[:, 1, :]
        m_q, m_p = level_m[:, 0, T // 2:T], level_m[:, 1, T // 2:T]
        y_q = rs[:, 1, T // 2:T]
        x_q, mx_p = d("x_q", [P, T // 2]), d("mx_p", [P, T // 2])
        x64 = d("x64", [P, TB, 64])
        k_tiles = lambda view, a: view[:, a:a + 2, :]
        qk_sq = k_tiles(mix, 8)
        q_dec, k_dec, bv, m_t = (mix[:, k, :] for k in range(10, 14))
        gates = mix[0:16, 14, :]
        betas = mix[0:16, 15, :]
        qk_rs = k_tiles(mix, 14)
        exps = rs[0:16]
        ba_sum, ba_low = sq[0:16, 0, :], sq[0:16, 1, :]
        row_pick = small[0:48, 24:40]
        yi = d("yi", [P, T])
        lam_v = by_chunk(yi[:])
        state, resid = d("state", [P, P]), d("resid", [P, P])
        v_new = d("v_new", [P, 2, P])
        ends = d("ends", [P, 3, TB])
        deltanet.close()
        attention = ExitStack()
        heads.enter_context(attention)
        a = lambda name, shape: sb(name, shape, where=attention)
        v_tok = a("v_tok", [P, TB, 2 * P])
        ex = a("ex", [P, 2, EXP_WIDTH])
        p_t = a("p_t", [P, EXP_WIDTH])
        bias_h = a("bias_h", [P, T])
        att_sum_high = sb("att_sum_high", [P, T], F32R, where=attention)
        att_sum_low = sb("att_sum_low", [P, T], F32R, where=attention)
        att_sq = a("att_sq", [P, 2, T])
        att_rs = a("att_rs", [P, 2, T])
        att_o = a("att_o", [P, 2, T])
        neg_max = a("neg_max", [P, 8])
        row_sum = a("row_sum", [P, 8])
        inv_sum = a("inv_sum", [P, 8])
        attention.close()
        heads.close()
        norms = ExitStack()
        stack.enter_context(norms)
        w_row = sb("w_row", [P, D], where=norms)
        turning = ExitStack()
        norms.enter_context(turning)
        xn = sb("xn", [P, TB, D], where=turning)
        squares_out = sb("squares_out", [P, T], where=turning)
        diag = sb("diag", [P, TB, P], where=turning)
        turning.close()
        ffn = ExitStack()
        norms.enter_context(ffn)
        hid_high = sb("hid_high", [P, 4, T], F32R, where=ffn)
        hid_low = sb("hid_low", [P, 4, T], F32R, where=ffn)
        gate_act = sb("gate_act", [P, 2, T], where=ffn)
        hidden = sb("hidden", [P, 2, T], where=ffn)
        last_squares = sb("last_squares", [P, T], where=ffn)
        ffn.close()
        norms.close()

        raw_landed = [sem("raw_landed0"), sem("raw_landed1")]
        w_high_ready = sem("w_high_ready")
        w_low_ready = sem("w_low_ready")
        chunks_done = sem("chunks_done")
        x_landed = [sem(f"x_landed{t}") for t in range(TB)]
        row_landed = sem("row_landed")
        params_landed = sem("params_landed")
        const_step = sem("const_step")
        dve_const = sem("dve_const")
        norm_sq = sem("norm_sq")
        norm_log = sem("norm_log")
        norm_rstd = sem("norm_rstd")
        norm_sum = sem("norm_sum")
        norm_scaled = sem("norm_scaled")
        norm_scaled2 = sem("norm_scaled2")
        norm_diag = sem("norm_diag")
        out_scaled_act = sem("out_scaled_act")
        out_scaled = sem("out_scaled")
        norm_turned = sem("norm_turned")
        norm_high = sem("norm_high")
        norm_low = sem("norm_low")
        conv_first = sem("conv_first")
        conv_tap = sem("conv_tap")
        pre_ready = sem("pre_ready")
        att_pre_ready = sem("att_pre_ready")
        param_turned = sem("param_turned")
        conv_ready = sem("conv_ready")
        taps_ready = sem("taps_ready")
        lam_step = sem("lam_step")
        lam_act = sem("lam_act")
        ba_summed = sem("ba_summed")
        ba_act = sem("ba_act")
        ba_dve = sem("ba_dve")
        ba_turned = sem("ba_turned")
        rows_clear = sem("rows_clear")
        parts_high = sem("parts_high")
        parts_low = sem("parts_low")
        rows_picked = sem("rows_picked")
        qk_sums = sem("qk_sums")
        qk_logs = sem("qk_logs")
        qk_rstds = sem("qk_rstds")
        qk_squared = sem("qk_squared")
        qk_high_ready = sem("qk_high_ready")
        qk_low_ready = sem("qk_low_ready")
        dn_pe, dn_act, dn_dve, dn_pool = sem("dn_pe"), sem("dn_act"), sem("dn_dve"), sem("dn_pool")
        at_pe, at_act, at_dve = sem("at_pe"), sem("at_act"), sem("at_dve")
        att_summed = sem("att_summed")
        att_sum_high_ready = sem("att_sum_high_ready")
        att_sum_low_ready = sem("att_sum_low_ready")
        mix_high = sem("mix_high")
        mix_low = sem("mix_low")
        out_added = sem("out_added")
        gate_ready = sem("gate_ready")
        hid_ready = sem("hid_ready")
        hid_high_ready = sem("hid_high_ready")
        hid_low_ready = sem("hid_low_ready")
        stored = sem("stored")

        def first_columns(view, start, n):
            return view.rearrange("p (k n) -> p k n", n=P)[:, :, start:start + n]

        by_k = lambda w: w[0].rearrange("(k p) n -> p k n", p=P)
        in_v, gate_v, up_v = by_k(w_in), by_k(w_gate), by_k(w_up)
        out_v, down_v = by_k(w_out), by_k(w_down)

        def in_column(kind, head):
            return {"q": 0, "k": DN_WIDTH, "v": 2 * DN_WIDTH, "z": OFF_Z}[kind] + head * P

        def att_column(u, head):
            return (None, None, OFF_Q, OFF_K, OFF_Q + P, OFF_K + P)[u] + head * 2 * P

        OUT_BANKS = (1, 7, 6, 0)
        ATT_BANKS = (1, 7, 0, 7, 1, 0)
        PAIR = (slice(0, 2), slice(2, 4))
        ADDED_END = 32 + 16 * (FF_GROUPS - 1)
        END_BLOCKS = ((0, 2), (2, 3), (3, 4))
        END_BANKS = (OUT_BANKS[0:2], OUT_BANKS[2:4])
        NORM_BANKS = ((2, 3, 4, 5), (0, 1, 6, 7))

        block = stack.enter_context(nc.Block())

        def count(span, j, scale=1, plus=0):
            base, i, per = span
            return scale * (base + j) + plus + i * (per * scale)

        def last_halves(span, j):
            return isinstance(span[1], int) and count(span, j + LEAD) >= HALVES

        def half_done(eng, span, j):
            eng.wait_ge(chunks_done, count(span, j + 1, CHUNKS))

        def chunk_done(eng, span, j, c):
            eng.wait_ge(chunks_done, count(span, j, CHUNKS, c + 1))

        S_HEADS = lambda h: (2 * U_HEADS, h, 8)
        S_ATT = lambda n: (2 * U_ATT, n, 12)
        S_OUT0 = (2 * U_OUT, 0, 4)
        S_OUT1 = lambda g: (2 * U_OUT + 16, g, 4)
        S_OUT1_LAST = (2 * U_OUT + 28, 0, 4)
        S_FF0 = (2 * U_FF, 0, 24)
        S_FF = lambda n: (2 * U_FF + 16 - 24, n, 24)
        S_END = (HALVES - 8, 0, 8)
        PARAMS = 16 * 10

        @block.sync
        def _(sp):
            def load(u, slot, src, blocks=KT):
                if not isinstance(u, int) or u >= 2:
                    sp.wait_ge(w_low_ready, 2 * u - 2)
                sp.dma_start(raw[:, slot, :].rearrange("p (k n) -> p k n", k=blocks), src
                             ).then_inc(raw_landed[slot], 16)

            def columns(view, col):
                return view[:, :, bass.ds(col, P)]

            def load_head(h, kinds="qkvz"):
                for kind in kinds:
                    j = "qkvz".index(kind)
                    load(4 * h + U_HEADS + j, (U_HEADS + j) % 2, columns(in_v, in_column(kind, h)))

            def load_attention(n):
                for j in range(6):
                    if j < 2:
                        load(6 * n + U_ATT + j, (U_ATT + j) % 2,
                             in_v[:, 8 * j:8 * j + 8, bass.ds(OFF_V + n * (2 * P), 2 * P)], KT // 2)
                    else:
                        load(6 * n + U_ATT + j, (U_ATT + j) % 2, columns(in_v, att_column(j, n)))

            def load_out(g, half_k):
                for j in range(2):
                    load(2 * g + U_OUT + 8 * half_k + j, (U_OUT + j) % 2,
                         out_v[:, 8 * half_k + 4 * j:8 * half_k + 4 * j + 4, bass.ds(g * T, T)], 4)

            def load_pair(u, n, fb):
                load(u, U_FF % 2, columns(gate_v, n * (4 * P) + fb * P))
                load(u + 1, 1 - U_FF % 2, columns(up_v, n * (4 * P) + fb * P))

            def load_down(u, n):
                for c in range(4):
                    load(u + c, (U_FF + c) % 2, down_v[:, bass.ds(n * 4, 4), c * T:(c + 1) * T], 4)

            for t in range(TB):
                sp.dma_start(x1[:, t, :], x[0, t * P:(t + 1) * P, :]).then_inc(x_landed[t], 16)
                if t == 1:
                    sp.dma_start(w_row[:], attn_norm_w[0:1, :].to_broadcast([P, D])).then_inc(row_landed, 16)
            load(0, 0, columns(in_v, OFF_B))
            sp.wait_ge(const_step, CONSTS)
            load_head(0, "q")
            sp.wait_ge(dve_const, 2)
            sp.wait_ge(norm_turned, 4 * TB)
            sp.dma_start(conv_rows[0:TAPS * 24, :], conv_w[0].rearrange("t (b c) -> (t b) c", c=P)).then_inc(params_landed, 16)
            sp.dma_start(dn_w[:], dn_norm_w[0].rearrange("(c a) -> c a", a=1)).then_inc(params_landed, 16)
            for e in range(2):
                sp.dma_start(da_w[:, e:e + 1], da_norm_w[0, e * P:(e + 1) * P].rearrange("(c a) -> c a", a=1)
                              ).then_inc(params_landed, 16)
            for i, v in enumerate((lam_q1, lam_k1, lam_q2, lam_k2)):
                sp.dma_start(lam_v[:, i, :], v[0:1, :].to_broadcast([P, P])).then_inc(params_landed, 16)
            sp.dma_start(dt_col[8:16, :], dt_bias[0].rearrange("(c a) -> c a", a=1)).then_inc(params_landed, 16)
            sp.dma_start(alog_col[8:16, :], a_log[0].rearrange("(c a) -> c a", a=1)).then_inc(params_landed, 16)
            load_head(0, "kvz")
            with sp.Fori(1, DN_HEADS) as h:
                load_head(h)
            with sp.Fori(0, DA_HEADS) as n:
                load_attention(n)
            for half_k in range(2):
                with sp.Fori(0, 4) as g:
                    load_out(g, half_k)
            for fb in range(4):
                load_pair(U_FF + 2 * fb, 0, fb)
            with sp.Fori(1, FF_GROUPS) as n:
                u = 12 * n + (U_FF + 8 - 12)
                load_pair(u, n, 0)
                load_down(u + 2, n - 1)
                for fb in range(1, 4):
                    load_pair(u + 4 + 2 * fb, n, fb)
            load_down(UNITS - 4, FF_GROUPS - 1)
            for t in range(TB):
                for i, scaled in enumerate((out_scaled_act, out_scaled)):
                    sp.wait_ge(scaled, t + 1)
                    at = slice(i * (D // 2), (i + 1) * (D // 2))
                    sp.dma_start(out[0, t * P:(t + 1) * P, at], x1[:, t, at]).then_inc(stored, 16)
            sp.wait_ge(stored, 2 * 16 * TB)

        @block.gpsimd
        def _(pool):
            steps = [0]

            def const(ins):
                ins.then_inc(const_step, 1)
                steps[0] += 1
                pool.wait_ge(const_step, steps[0])

            const(pool.memset(ident[:], 0.0))
            const(pool.affine_select(out=ident[:], in_=ident[:], compare_op=ALU.not_equal, fill=1.0, base=0,
                                     pattern=[[-1, P]], channel_multiplier=1))
            pool.wait_ge(dve_const, 1)
            const(pool.affine_select(out=incl[:], in_=ones[:], compare_op=ALU.is_ge, fill=0.0, base=0,
                                     pattern=[[1, P]], channel_multiplier=-1))
            full = raw[:, 1, 0:6 * P].rearrange("p (l i) -> p l i", l=6)
            for l in range(6):
                s = 1 << l
                odd = full[:, l, :].rearrange("p (g b s) -> p g b s", b=2, s=s)[:, :, 1, :]
                src = ones[:].rearrange("p (g b s) -> p g b s", b=2, s=s)[:, :, 1, :]
                const(pool.memset(full[:, l, :], 0.0))
                const(pool.affine_select(out=odd, in_=src, compare_op=ALU.is_ge, fill=0.0, base=0,
                                         pattern=[[-2 * s, P // (2 * s)], [0, s]], channel_multiplier=1))
                const(pool.affine_select(out=odd, in_=odd, compare_op=ALU.is_ge, fill=0.0, base=s - 1,
                                         pattern=[[2 * s, P // (2 * s)], [0, s]], channel_multiplier=-1))
            const(pool.iota(base_bias[:], pattern=[[1, T]], base=P - T, channel_multiplier=-1,
                            allow_small_or_imprecise_dtypes=True))
            const(pool.affine_select(out=base_bias[:], in_=base_bias[:], compare_op=ALU.is_ge, fill=FAR, base=T - P,
                                     pattern=[[-1, T]], channel_multiplier=1))
            for n in range(DA_HEADS):
                const(pool.memset(slopes[:, n:n + 1], 2.0 ** (-8.0 * (n + 1) / DA_HEADS)))
            pool.wait_ge(x_landed[2], 16)
            pool.wait_ge(row_landed, 16)
            pool.tensor_tensor(xn[:, 2, :], x1[:, 2, :], w_row[:], ALU.mult).then_inc(norm_scaled2, 1)

            const(pool.memset(levels[:], 0.0))
            const(pool.memset(ident_q[:], 0.0))
            for b in range(4):
                rows, block, q, p = slice(32 * b, 32 * b + 32), slice(32 * b, 32 * b + 32), 32 * (b // 2), 32 * (b % 2)
                const(pool.tensor_copy(levels[rows, 0, q:q + 32], full[rows, 0, block]))
                const(pool.tensor_copy(levels[rows, 1:5, p:p + 32], full[rows, 1:5, block]))
                const(pool.tensor_copy(ident_q[rows, q:q + 32], ident[rows, block]))
            const(pool.tensor_copy(levels[:, 5, :].rearrange("p (g s) -> p g s", s=32),
                                   full[:, 5, :].rearrange("p (g b s) -> p g b s", b=2, s=32)[:, :, 1, :]))
            assert steps[0] == CONSTS

            def mask(l):
                return levels[:, l:l + 1, :].to_broadcast([P, TB, 64])

            def squares(h):
                pool.wait_ge(pre_ready, 4 * h + 2)
                if not isinstance(h, int):
                    pool.wait_ge(qk_sums, 2 * h)
                pool.tensor_tensor(qk_sq, pre[:, 0:2, :], pre[:, 0:2, :], ALU.mult).then_inc(qk_squared, 1)
                pool.wait_ge(qk_high_ready, h + 1)
                pool.tensor_tensor(qk_low[:], qk_sq, qk_high[:].bitcast(F32), ALU.subtract).then_inc(qk_low_ready, 1)

            def head_levels(h):
                pool.wait_ge(dn_dve, after(DN_DVE, h, "m"))
                for b in range(4):
                    last = pool.tensor_tensor(packed(m_p)[32 * b:32 * b + 32, :, 32 * (b % 2):32 * (b % 2) + 32],
                                              by_chunk(m_t)[32 * b:32 * b + 32, :, 32 * b:32 * b + 32],
                                              ones[32 * b:32 * b + 32, :].rearrange("p (c i) -> p c i", c=TB), ALU.mult)
                last.then_inc(dn_pool, 1)
                pool.wait_ge(dn_pool, after(DN_POOL, h, "m_diag"))
                for l in range(1, 6):
                    if l >= 3:
                        pool.wait_ge(dn_pe, after(DN_PE, h, f"mx{l - 2}"))
                    if l == 2:
                        pool.memset(yi[:], 0.0).then_inc(dn_pool, 1)
                        pool.wait_ge(dn_dve, after(DN_DVE, h, "y0"))
                    if l < 5:
                        pool.tensor_tensor(packed(level_m[:, l % 2, 0:T // 2]), packed(m_p), mask(l), ALU.mult
                                           ).then_inc(dn_pool, 1)
                    else:
                        split = lambda view: view.rearrange("p c (g s) -> p c g s", s=32)
                        odd = by_chunk(m_t).rearrange("p c (g b s) -> p c g b s", b=2, s=32)[:, :, :, 1, :]
                        pool.tensor_tensor(split(packed(level_m[:, 1, 0:T // 2])), odd, split(mask(5)), ALU.mult
                                           ).then_inc(dn_pool, 1)

            squares(0)
            with pool.Fori(1, DN_HEADS) as h:
                head_levels(h - 1)
                squares(h)
            head_levels(DN_HEADS - 1)
            with pool.Fori(0, DA_HEADS) as n:
                pool.wait_ge(at_act, after(AT_ACT, n, "square1"))
                pool.tensor_tensor(att_sq[:, 0, :], att_sq[:, 0, :], att_sq[:, 1, :], ALU.add).then_inc(att_summed, 1)
                pool.wait_ge(att_sum_high_ready, n + 1)
                pool.tensor_tensor(att_sum_low[:], att_sq[:, 0, :], att_sum_high[:].bitcast(F32), ALU.subtract
                                   ).then_inc(att_sum_low_ready, 1)

        @block.scalar
        def _(act):
            A = nc.scalar.activation

            def high(span, j, by_block=False):
                if last_halves(span, j):
                    return
                s = span[0] + j + LEAD
                act.wait_ge(raw_landed[(s // 2) % 2], 16 * (s // 4 + 1) + span[1] * (span[2] * 4))
                if by_block:
                    act.wait_ge(chunks_done, CHUNKS * span[0] + CHUNKS * 3 + (j + LEAD - SLOTS) + 1)
                elif not isinstance(span[1], int) or s >= SLOTS:
                    half_done(act, span, j + LEAD - SLOTS)
                A(w_high[:, s % SLOTS, :], raw[:, (s // 2) % 2, (s % 2) * HALF:(s % 2 + 1) * HALF], ACT.Copy
                  ).then_inc(w_high_ready, 1)

            def rstds(r, i, two):
                if r == 0:
                    act.wait_ge(norm_sq, 2 * i + 2)
                else:
                    act.wait_ge(norm_sum, 2 * (r - 1) + i + 1)
                if r > 0:
                    act.wait_ge(norm_diag, 4 * r)
                A(rstd_log[:, two], sum_sq[:, two], ACT.Ln, scale=1.0 / D, bias=EPS).then_inc(norm_log, 1)
                act.wait_ge(norm_log, 2 * r + i + 1)
                A(rstd[:, two], rstd_log[:, two], ACT.Exp, scale=-0.5).then_inc(norm_rstd, 1)

            def high_parts(r, t, groups=range(4)):
                for g in groups:
                    act.wait_ge(norm_turned, 16 * r + 4 * t + g + 1)
                    A(h_high[:, 4 * g:4 * g + 4, t * P:(t + 1) * P],
                      bank[NORM_BANKS[t % 2][g]][:].rearrange("p (k i) -> p k i", k=4), ACT.Copy).then_inc(norm_high, 1)

            def group_square(to, t, g, added, squared):
                act.wait_ge(out_added, added)
                act.wait_ge(norm_sq, squared)
                A(to[:], x1[:, t, bass.ds(g * T, T)], ACT.Square, accum_out=part_sq[:, t, bass.ds(g, 1)]
                  ).then_inc(norm_sq, 1)

            act.wait_ge(dve_const, 2)
            for pair in range(2):
                for t in (2 * pair, 2 * pair + 1):
                    if t == 3:
                        high_parts(0, 0, range(2))
                    act.wait_ge(x_landed[t], 16)
                    A(h_low[:, 4 * t:4 * t + 4, :].rearrange("p k n -> p (k n)"), x1[:, t, :], ACT.Square,
                      accum_out=sum_sq[:, t:t + 1]).then_inc(norm_sq, 1)
                rstds(0, pair, PAIR[pair])

            high_parts(0, 0, range(2, 4))
            high_parts(0, 1)
            for s in range(2):
                act.wait_ge(raw_landed[0], 16)
                A(first_columns(w_high[:, s, :], 0, 48), first_columns(raw[:, 0, s * HALF:(s + 1) * HALF], 0, 48), ACT.Copy
                  ).then_inc(w_high_ready, 1)
            high_parts(0, 2)
            high_parts(0, 3)
            high((0, 0, 4), -1)

            act.wait_ge(lam_step, 4)
            A(lam_exp, lam_dot, ACT.Exp).then_inc(lam_act, 1)
            act.wait_ge(params_landed, PARAMS)
            A(rate, alog_col, ACT.Exp).then_inc(lam_act, 1)
            high((0, 0, 4), 0)
            high((0, 0, 4), 1)

            def gates_beta():
                act.wait_ge(ba_summed, 1)
                A(betas, ba_sum, ACT.Exp, scale=-1.0).then_inc(ba_act, 1)
                A(exps[:, 0, :], ba_sum, ACT.Abs, bias=dt_col[0:16, :]).then_inc(ba_act, 1)
                act.wait_ge(ba_act, 2)
                A(exps[:, 1, :], exps[:, 0, :], ACT.Exp, scale=-1.0).then_inc(ba_act, 1)
                act.wait_ge(ba_act, 3)
                A(exps[:, 0, :], exps[:, 1, :], ACT.Ln, bias=1.0).then_inc(ba_act, 1)

            def gate_columns():
                act.wait_ge(ba_dve, 6)
                for i, rows in enumerate((gates, betas)):
                    A(row_parts[0:16, i, :], rows, ACT.Copy).then_inc(parts_high, 1)
                act.wait_ge(ba_turned, 1)
                A(ba_t[:], bank[2][:, 0:P].rearrange("p (c r) -> p c r", r=16), ACT.Copy).then_inc(ba_act, 1)
                act.wait_ge(ba_act, 5)
                A(head_cols[:, 8:12, :], ba_t[:, 0:4, 8:16], ACT.Exp).then_inc(ba_act, 1)

            def z_out(h):
                act.wait_ge(dn_dve, all_done(DN_DVE, h))
                A(pre[:, 3, :], bank[0][:], ACT.Silu).then_inc(pre_ready, 1)

            def conv_start(h, j):
                act.wait_ge(taps_ready, h + 1)
                if not isinstance(h, int) or h > 0 or j > 0:
                    act.wait_ge(pre_ready, 4 * h + j)
                A(conv_acc[:], bank[(U_HEADS + j) % 2][:], ACT.Copy, scale=taps[:, TAPS - 1, j:j + 1]
                  ).then_inc(conv_first, 1)

            def conv_end(h, j):
                act.wait_ge(conv_tap, 9 * h + 3 * j + 3)
                if not isinstance(h, int):
                    if j < 2:
                        act.wait_ge(dn_dve, after(DN_DVE, h - 1, "q"))
                    else:
                        act.wait_ge(dn_pe, after(DN_PE, h - 1, "v_turn"))
                A(pre[:, j, :], conv_acc[:], ACT.Silu).then_inc(pre_ready, 1)

            def dn(gap, h):
                def pe(name):
                    act.wait_ge(dn_pe, after(DN_PE, h, name))

                def dve(name):
                    act.wait_ge(dn_dve, after(DN_DVE, h, name))

                def own(name):
                    act.wait_ge(dn_act, after(DN_ACT, h, name))

                if gap == 2:
                    dve("gaps")
                    A(decay[:], decay[:], ACT.Exp).then_inc(dn_act, 1)
                    dve("gap_end")
                    A(q_dec, bank[4][:], ACT.Exp).then_inc(dn_act, 1)
                    A(ends[:, 1, :], ends[:, 0, :], ACT.Exp).then_inc(dn_act, 1)
                for l in range(1, 7):
                    if gap == 5 + 2 * l:
                        pe(f"mx{l}")
                        if l < 5:
                            for b in range(4):
                                q, p = divmod(b, 2)
                                last = A(packed(mx_p[32 * b:32 * b + 32, :])[:, :, 32 * p:32 * p + 32],
                                         packed(bank[2][32 * p:32 * p + 32, 0:T // 2])[:, :, 32 * q:32 * q + 32], ACT.Copy)
                            last.then_inc(dn_act, 1)
                        elif l == 5:
                            A(mxs[32:64, 0:T // 2], bank[2][0:32, 0:T // 2], ACT.Copy)
                            A(mxs[96:P, 0:T // 2], bank[2][32:64, 0:T // 2], ACT.Copy).then_inc(dn_act, 1)
                        else:
                            A(mxs[64:P, 0:T // 2], bank[2][0:64, 0:T // 2], ACT.Copy).then_inc(dn_act, 1)
                for c in range(TB):
                    if gap == 19 + 3 * c:
                        pe(f"vn{c}")
                        A(v_new[:, c % 2, :], bank[6][:, c * P:(c + 1) * P], ACT.Copy).then_inc(dn_act, 1)
                if gap == 29:
                    pe("o3")
                    A(sq[:, 0, :], bank[3][:], ACT.Square).then_inc(dn_act, 1)
                    own("o_square")
                    A(o_high[:], sq[:, 0, :], ACT.Copy).then_inc(dn_act, 1)

            def norms_log(h, before):
                if before is not None:
                    act.wait_ge(dn_pe, after(DN_PE, before, "o_squares"))
                    A(rs[:, 0, :], bank[5][:], ACT.Ln, scale=1.0 / P, bias=EPS).then_inc(dn_act, 1)
                if h is not None:
                    if before is None:
                        act.wait_ge(ba_turned, 1)
                        act.wait_ge(parts_low, 2)
                    else:
                        act.wait_ge(dn_dve, after(DN_DVE, before, "q"))
                    for i, (part, b) in enumerate(((1, 2), (0, 6))):
                        act.wait_ge(qk_sums, 2 * h + i + 1)
                        A(qk_rs[:, part, :], bank[b][:], ACT.Ln, bias=EPS).then_inc(qk_logs, 1)

            def norms_exp(h, before):
                if before is not None:
                    act.wait_ge(dn_act, after(DN_ACT, before, "o_log"))
                    A(rs[:, 0, :], rs[:, 0, :], ACT.Exp, scale=-0.5).then_inc(dn_act, 1)
                if h is not None:
                    for i, part in enumerate((1, 0)):
                        act.wait_ge(qk_logs, 2 * h + i + 1)
                        A(qk_rs[:, part, :], qk_rs[:, part, :], ACT.Exp, scale=-0.5, bias=-0.5 * math.log(P) * i
                          ).then_inc(qk_rstds, 1)

            def att_out(n, u):
                if not isinstance(n, int) or n > 0:
                    if u < 2:
                        act.wait_ge(at_act, after(AT_ACT, n - 1, f"v{u}"))
                    elif u < 5:
                        act.wait_ge(at_pe, after(AT_PE, n - 1, ("score3", "score3", "score7")[u - 2]))
                elif u < 2:
                    act.wait_ge(dn_dve, after(DN_DVE, DN_HEADS - 1, "q"))
                elif u == 2:
                    act.wait_ge(dn_pe, after(DN_PE, DN_HEADS - 1, "v_turn"))
                elif u == 3:
                    act.wait_ge(dn_dve, all_done(DN_DVE, DN_HEADS))
                A(pre[:, u, :], bank[ATT_BANKS[u]][:], ACT.Copy).then_inc(att_pre_ready, 1)

            def att(gap, n):
                def pe(name):
                    act.wait_ge(at_pe, after(AT_PE, n, name))

                if gap == 0:
                    act.wait_ge(at_dve, all_done(AT_DVE, n))
                    act.wait_ge(dn_dve, all_done(DN_DVE, DN_HEADS))
                    act.wait_ge(att_pre_ready, 6 * n + 2)
                    for e in range(2):
                        A(v_tok[:, 2 * e:2 * e + 2, :].rearrange("p b c -> p (b c)"), pre[:, e, :], ACT.Copy
                          ).then_inc(at_act, 1)
                for i, (m, qb) in enumerate(SC):
                    if gap == 2 + 2 * i:
                        act.wait_ge(at_dve, after(AT_DVE, n, f"max{i}"))
                        e = ex[:, m, ex_block(qb)]
                        A(e, e, ACT.Exp, bias=neg_max[:, i:i + 1], accum_out=row_sum[:, i:i + 1]).then_inc(at_act, 1)
                for k in range(TB):
                    if gap == 22 + 2 * k:
                        pe(f"p_turn{k}")
                        w = (TB - k) * P
                        A(p_t[:, PT_OFF[k]:PT_OFF[k] + w], bank[2 + k % 2][:, 0:w], ACT.Copy).then_inc(at_act, 1)
                if gap == 31:
                    for e in range(2):
                        pe(f"pv{e}")
                        A(att_sq[:, e, :], bank[4 + e][:], ACT.Square).then_inc(at_act, 1)
                if gap == 32:
                    act.wait_ge(att_summed, n + 1)
                    A(att_sum_high[:], att_sq[:, 0, :], ACT.Copy).then_inc(att_sum_high_ready, 1)
                if gap == 35:
                    pe("squares")
                    A(att_rs[:, 0, :], bank[2][:], ACT.Ln, scale=1.0 / (2 * P), bias=EPS).then_inc(at_act, 1)
                    act.wait_ge(at_act, after(AT_ACT, n, "log"))
                    A(att_rs[:, 1, :], att_rs[:, 0, :], ACT.Exp, scale=-0.5).then_inc(at_act, 1)

            def head_window(h, before):
                span = S_HEADS(h)
                for gap in range(8 * CHUNKS):
                    if gap % CHUNKS == 0:
                        high(span, gap // CHUNKS)
                    if before is None:
                        if gap == 0:
                            gates_beta()
                        if gap == 13:
                            gate_columns()
                    else:
                        dn(gap, before)
                        if gap == 3:
                            z_out(before)
                    for j in range(3):
                        if gap == 8 * (j + 1):
                            half_done(act, span, 2 * j + 1)
                            conv_start(h, j)
                        if gap == 8 * (j + 1) + 5:
                            conv_end(h, j)
                    if gap == 25:
                        act.wait_ge(qk_squared, h + 1)
                        A(qk_high[:], qk_sq, ACT.Copy).then_inc(qk_high_ready, 1)
                    if gap == 31:
                        norms_log(h, before)
                        norms_exp(h, before)

            head_window(0, None)
            with act.Fori(1, DN_HEADS) as h:
                head_window(h, h - 1)

            def att_window(n, before):
                span = S_ATT(n)
                for gap in range(12 * CHUNKS):
                    if gap % CHUNKS == 0:
                        high(span, gap // CHUNKS)
                    if before is None:
                        if gap < 32:
                            dn(gap, DN_HEADS - 1)
                        if gap == 3:
                            z_out(DN_HEADS - 1)
                        if gap == 31:
                            norms_log(None, DN_HEADS - 1)
                            norms_exp(None, DN_HEADS - 1)
                    else:
                        if gap == 0:
                            half_done(act, span, -1)
                            att_out(before, 5)
                        att(gap, before)
                    for u in range(5):
                        if gap == max(8 * (u + 1), 16) + 1:
                            half_done(act, span, max(2 * u + 1, 3))
                            att_out(n, u)

            att_window(0, None)
            with act.Fori(1, DA_HEADS) as n:
                att_window(n, n - 1)

            def mix_split(k):
                A(h_high[:, k:k + 2, :], mix[:, k:k + 2, :], ACT.Copy).then_inc(mix_high, 1)

            half_done(act, S_OUT0, -2)
            act.wait_ge(at_dve, all_done(AT_DVE, DA_HEADS - 1))
            mix_split(0)
            mix_split(2)
            half_done(act, S_OUT0, -1)
            att_out(DA_HEADS - 1, 5)
            for gap in range(16 * CHUNKS):
                if gap % CHUNKS == 0:
                    high(S_OUT0, gap // CHUNKS)
                att(gap, DA_HEADS - 1)
                if gap < 5:
                    mix_split(4 + 2 * gap)
                if gap == 6:
                    act.wait_ge(mix_low, 7)
                    for t in range(TB):
                        act.dma_start(x1[:, t, :], x[0, t * P:(t + 1) * P, :]).then_inc(x_landed[t], 16)
                if gap == 36:
                    for e in range(2):
                        act.wait_ge(at_dve, after(AT_DVE, DA_HEADS - 1, f"o{e}"))
                        A(h_high[:, KT - 2 + e, :], att_o[:, e, :], ACT.Copy).then_inc(mix_high, 1)
            act.wait_ge(at_dve, all_done(AT_DVE, DA_HEADS))
            act.dma_start(w_row[:], ffn_norm_w[0:1, :].to_broadcast([P, D])).then_inc(row_landed, 16)
            with act.Fori(0, 3) as g:
                for j in range(4):
                    high(S_OUT1(g), j)
                for t in range(TB):
                    group_square(squares_out, t, g, 4 * g + 16 + t + 1, TB + 4 * g + t)
            high(S_OUT1_LAST, 0)
            for t in range(TB):
                if t == 3:
                    for j in (1, 2):
                        high(S_OUT1_LAST, j, by_block=True)
                group_square(squares_out, t, 3, 28 + t + 1, TB + 12 + t)
                if t % 2 == 1:
                    rstds(1, t // 2, PAIR[t // 2])
            high(S_OUT1_LAST, 3, by_block=True)
            for t in range(TB):
                high_parts(1, t)

            def gate_out(n, fb):
                if not isinstance(n, int) or 4 * n + fb >= 2:
                    act.wait_ge(hid_ready, 4 * n + fb - 1)
                A(gate_act[:, fb % 2, :], bank[2 + 2 * (fb % 2)][:], ACT.Silu).then_inc(gate_ready, 1)

            def hidden_high(n, fb):
                act.wait_ge(hid_ready, 4 * n + fb + 1)
                A(hid_high[:, fb, :], hidden[:, fb % 2, :], ACT.Copy).then_inc(hid_high_ready, 1)

            act.wait_ge(norm_scaled, TB - 1 + 16)
            act.dma_start(w_row[:], final_norm_w.rearrange("(a n) -> a n", a=1).to_broadcast([P, D])
                          ).then_inc(row_landed, 16)
            for j in range(16):
                high(S_FF0, j)
                if j % 4 == 2:
                    half_done(act, S_FF0, j - 1)
                    gate_out(0, j // 4)
                if j % 4 == 0 and j > 0:
                    hidden_high(0, j // 4 - 1)
            with act.Fori(1, FF_GROUPS) as n:
                span = S_FF(n)
                for j in range(24):
                    high(span, j)
                    if j == 0:
                        hidden_high(n - 1, 3)
                    if j in (2, 14, 18, 22):
                        half_done(act, span, j - 1)
                        gate_out(n, (j - 10) // 4 if j > 2 else 0)
                    if j == 12:
                        half_done(act, span, 11)
                    if j in (12, 16, 20):
                        hidden_high(n, (j - 12) // 4)
            hidden_high(FF_GROUPS - 1, 3)
            for j in range(8):
                high(S_END, j)
                if j in (1, 3):
                    for t in range(TB):
                        group_square(last_squares, t, j // 2, ADDED_END + 4 * (j // 2) + t + 1,
                                     TB + 16 + 4 * (j // 2) + t)
            for i, (t0, t1) in enumerate(END_BLOCKS):
                for t in range(t0, t1):
                    for c in (2, 3):
                        group_square(last_squares, t, c, ADDED_END + 8 + 2 * t + c - 1, TB + 16 + 8 + 2 * t + c - 2)
                rstds(2, i, slice(t0, t1))
                act.wait_ge(norm_rstd, 4 + i + 1)
                act.wait_ge(norm_scaled, TB - 1 + 16 + 8)
                for t in range(t0, t1):
                    A(x1[:, t, 0:D // 2], x1[:, t, 0:D // 2], ACT.Copy, scale=rstd[:, t:t + 1]).then_inc(out_scaled_act, 1)

        @block.vector
        def _(dve):
            V = nc.vector

            def low(span, j):
                if last_halves(span, j):
                    return
                s = span[0] + j + LEAD
                dve.wait_ge(w_high_ready, count(span, j + LEAD + 1))
                V.tensor_tensor(w_low[:, s % SLOTS, :], raw[:, (s // 2) % 2, (s % 2) * HALF:(s % 2 + 1) * HALF],
                                w_high[:, s % SLOTS, :].bitcast(F32), ALU.subtract).then_inc(w_low_ready, 1)

            V.memset(ones[:], 1.0).then_inc(dve_const, 1)
            V.memset(small[:], 0.0).then_inc(dve_const, 1)
            dve.wait_ge(dve_const, 1)
            V.tensor_copy(ones_r[:], ones[:]).then_inc(dve_const, 1)
            V.memset(state[:], 0.0).then_inc(dn_dve, 1)
            V.memset(resid[:], 0.0).then_inc(at_dve, 1)

            def times_row(r, t, cols_of):
                V.tensor_tensor(xn[:, t, cols_of], x1[:, t, cols_of], w_row[:, cols_of], ALU.mult).then_inc(norm_scaled, 1)

            def diagonals(r, pair):
                dve.wait_ge(norm_rstd, 2 * r + pair + 1)
                for t in (2 * pair, 2 * pair + 1):
                    V.tensor_scalar(diag[:, t, :], ident[:], rstd[:, t:t + 1], None, ALU.mult).then_inc(norm_diag, 1)

            def sums(two, n):
                dve.wait_ge(norm_sq, n)
                V.tensor_reduce(sum_sq[:, two], part_sq[:, two, :], AX.X, ALU.add).then_inc(norm_sum, 1)

            def low_parts(r, t, groups=range(4)):
                for g in groups:
                    dve.wait_ge(norm_high, 16 * r + 4 * t + g + 1)
                    at = (slice(None), slice(4 * g, 4 * g + 4), slice(t * P, (t + 1) * P))
                    V.tensor_tensor(h_low[at], bank[NORM_BANKS[t % 2][g]][:].rearrange("p (k i) -> p k i", k=4),
                                    h_high[at].bitcast(F32), ALU.subtract).then_inc(norm_low, 1)

            dve.wait_ge(row_landed, 16)
            dve.wait_ge(const_step, 2)
            for t in (0, 1, 3):
                dve.wait_ge(x_landed[t], 16)
                times_row(0, t, slice(0, D))
                if t == 0:
                    diagonals(0, 0)
            low_parts(0, 0, range(2))
            diagonals(0, 1)
            low_parts(0, 0, range(2, 4))
            low_parts(0, 1)
            for s in range(2):
                dve.wait_ge(w_high_ready, s + 1)
                V.tensor_tensor(first_columns(w_high[:, s, :], 32, 16), first_columns(raw[:, 0, s * HALF:(s + 1) * HALF], 0, 16),
                                first_columns(w_high[:, s, :], 0, 16).bitcast(F32), ALU.subtract).then_inc(w_low_ready, 1)
            low_parts(0, 2)
            low_parts(0, 3)
            low((0, 0, 4), -1)

            dve.wait_ge(params_landed, PARAMS)
            for i in range(2):
                V.tensor_tensor(lam_v[:, 2 * i, :], lam_v[:, 2 * i, :], lam_v[:, 2 * i + 1, :], ALU.mult).then_inc(lam_step, 1)
                dve.wait_ge(lam_step, 2 * i + 1)
                V.tensor_reduce(lam_dot[:, i:i + 1], lam_v[:, 2 * i, :], AX.X, ALU.add).then_inc(lam_step, 1)
            dve.wait_ge(lam_act, 1)
            V.scalar_tensor_tensor(out=lam, in0=lam_exp[:, 0:1], scalar=LAM_INIT, in1=lam_exp[:, 1:2],
                                   op0=ALU.add, op1=ALU.subtract).then_inc(lam_step, 1)
            V.tensor_scalar(da_w[:], da_w[:], 1.0 - LAM_INIT, None, ALU.mult).then_inc(lam_step, 1)
            low((0, 0, 4), 0)
            low((0, 0, 4), 1)

            def pick_taps(h):
                if isinstance(h, int):
                    dve.wait_ge(conv_ready, 1)
                else:
                    dve.wait_ge(conv_first, 3 * h)
                V.tensor_scalar(taps[:], conv_t[:, :, :, bass.ds(h, 1)].rearrange("p t j a -> p t (j a)"), 1.0, None,
                                ALU.mult).then_inc(taps_ready, 1)

            def gates_beta():
                steps = [0]

                def step(ins):
                    ins.then_inc(ba_dve, 1)
                    steps[0] += 1
                    dve.wait_ge(ba_dve, steps[0])

                half_done(dve, (0, 0, 4), 1)
                V.memset(row_parts[:].bitcast(F32), 0.0).then_inc(rows_clear, 1)
                V.tensor_copy(row_pick[0:16, :], ident[0:16, 0:16]).then_inc(rows_clear, 1)
                V.tensor_copy(row_pick[32:48, :], ident[32:48, 32:48]).then_inc(rows_clear, 1)
                dve.wait_ge(rows_clear, 3)
                V.tensor_copy(ba_low, bank[0][32:48, :]).then_inc(rows_clear, 1)
                dve.wait_ge(rows_clear, 4)
                V.tensor_tensor(ba_sum, bank[0][0:16, :], ba_low, ALU.add).then_inc(ba_summed, 1)
                dve.wait_ge(ba_summed, 1)
                step(V.tensor_scalar(gates, ba_sum, dt_col[0:16, :], 0.0, ALU.add, ALU.max))
                dve.wait_ge(ba_act, 1)
                step(V.tensor_scalar(betas, betas, 1.0, None, ALU.add))
                step(V.reciprocal(betas, betas))
                dve.wait_ge(ba_act, 4)
                dve.wait_ge(lam_act, 2)
                step(V.tensor_tensor(exps[:, 0, :], gates, exps[:, 0, :], ALU.add))
                step(V.tensor_scalar(exps[:, 1, :], exps[:, 0, :], rate[0:16, :], -1.0, ALU.mult, ALU.mult))
                for c in range(TB):
                    at = slice(c * P, (c + 1) * P)
                    last = V.tensor_tensor_scan(gates[:, at], ones[0:16, :], exps[:, 1, at], 0.0, ALU.mult, ALU.add)
                step(last)
                assert steps[0] == 6

            def gate_columns():
                dve.wait_ge(ba_dve, 6)
                dve.wait_ge(ba_act, 4)
                for array in (sq, rs, mx_p, x64):
                    V.memset(array[:], 0.0)
                for i, rows in enumerate((gates, betas)):
                    dve.wait_ge(parts_high, i + 1)
                    V.tensor_tensor(row_parts[32:48, i, :], rows, row_parts[0:16, i, :].bitcast(F32), ALU.subtract
                                    ).then_inc(parts_low, 1)
                dve.wait_ge(ba_act, 6)
                V.tensor_copy(head_cols[:, 0:4, :], ba_t[:, 0:4, 8:16]).then_inc(ba_dve, 1)
                V.tensor_copy(head_cols[:, 4:8, :], ba_t[:, 4:8, 0:8]).then_inc(ba_dve, 1)
                V.scalar_tensor_tensor(out=head_cols[:, 8:12, :], in0=head_cols[:, 8:12, :], scalar=-1.0,
                                       in1=ba_t[:, 4:8, 0:8], op0=ALU.mult, op1=ALU.mult).then_inc(ba_dve, 1)

            def conv(h, j, k):
                if k == 1:
                    dve.wait_ge(conv_first, 3 * h + j + 1)
                else:
                    dve.wait_ge(conv_tap, 9 * h + 3 * j + k - 1)
                V.scalar_tensor_tensor(out=conv_acc[:, k:T], in0=bank[(U_HEADS + j) % 2][:, 0:T - k],
                                       scalar=taps[:, TAPS - 1 - k, j:j + 1], in1=conv_acc[:, k:T],
                                       op0=ALU.mult, op1=ALU.add).then_inc(conv_tap, 1)

            def pick_rows(h, before):
                if before is None:
                    dve.wait_ge(ba_dve, 9)
                    dve.wait_ge(parts_low, 2)
                else:
                    dve.wait_ge(dn_pe, after(DN_PE, before, "beta_rows"))
                for i, row in enumerate((h + DN_HEADS, h)):
                    V.tensor_scalar(picked[:, i, :], row_parts[:, i, :].bitcast(F32), row_pick[:, bass.ds(row, 1)],
                                    None, ALU.mult).then_inc(rows_picked, 1)

            gate_col, beta_col, nbg_col = cols[:, 0:4], cols[:, 4:8], cols[:, 8:12]
            spread = lambda col: col.rearrange("p (c a) -> p c a", a=1).to_broadcast([P, TB, P])

            def dn(gap, h):
                def pe(name):
                    dve.wait_ge(dn_pe, after(DN_PE, h, name))

                def act(name):
                    dve.wait_ge(dn_act, after(DN_ACT, h, name))

                def own(name):
                    dve.wait_ge(dn_dve, after(DN_DVE, h, name))

                if gap == 0:
                    dve.wait_ge(qk_rstds, 2 * h + 1)
                    V.tensor_tensor(kT[:], pre[:, 1, :], qk_rs[:, 1, :], ALU.mult).then_inc(dn_dve, 1)
                    dve.wait_ge(qk_rstds, 2 * h + 2)
                    V.tensor_tensor(qT[:], pre[:, 0, :], qk_rs[:, 0, :], ALU.mult).then_inc(dn_dve, 1)
                    V.tensor_scalar(cols[:], head_cols[:, :, bass.ds(h, 1)].rearrange("p r a -> p (r a)"), 1.0, None,
                                    ALU.mult).then_inc(dn_dve, 1)
                if gap == 1:
                    pe("gate_rows")
                    own("columns")
                    for c in range(TB):
                        at = slice(c * P, (c + 1) * P)
                        last = V.tensor_scalar(decay[:, at], bank[4][:, at], gate_col[:, c:c + 1], 0.0,
                                               ALU.subtract, ALU.min)
                    last.then_inc(dn_dve, 1)
                    V.tensor_tensor(ends[:, 0, :], bank[4][:, P - 1:T:P], gate_col, ALU.subtract).then_inc(dn_dve, 1)
                if gap == 2:
                    act("decay")
                    V.tensor_tensor(by_chunk(decay[:]), by_chunk(decay[:]),
                                    incl[:].rearrange("p (c i) -> p c i", c=1).to_broadcast([P, TB, P]), ALU.mult
                                    ).then_inc(dn_dve, 1)
                    own("decay_mask")
                    pe("beta_rows")
                    V.tensor_tensor(m_t, decay[:], bank[5][:], ALU.mult).then_inc(dn_dve, 1)
                if gap == 3:
                    pe("kk")
                    own("decay_beta")
                    V.tensor_tensor(m_t, m_t, bank[2][:], ALU.mult).then_inc(dn_dve, 1)
                    own("m")
                    for b in range(4):
                        last = V.tensor_copy(packed(m_q)[32 * b:32 * b + 32, :, 32 * (b // 2):32 * (b // 2) + 32],
                                             by_chunk(m_t)[32 * b:32 * b + 32, :, 32 * b:32 * b + 32])
                    last.then_inc(dn_dve, 1)
                    own("m_diag")
                    V.tensor_tensor(packed(level_m[:, 0, 0:T // 2]), packed(m_q), levels[:, 0:1, :].to_broadcast([P, TB, 64]),
                                    ALU.mult).then_inc(dn_dve, 1)
                    own("level0")
                    V.tensor_tensor(packed(y_q), ident_q[:].rearrange("p (c i) -> p c i", c=1).to_broadcast([P, TB, 64]),
                                    packed(level_m[:, 0, 0:T // 2]), ALU.subtract).then_inc(dn_dve, 1)
                    own("y0")
                    V.transpose(x_q[:], y_q).then_inc(dn_dve, 1)
                    pe("kq")
                    V.tensor_tensor(decay[:], decay[:], bank[3][:], ALU.mult).then_inc(dn_dve, 1)
                    pe("v_turn")
                    V.tensor_tensor(by_chunk(bv), by_chunk(bank[6][:]), spread(beta_col), ALU.mult).then_inc(dn_dve, 1)
                if gap == 4:
                    pe("k_turn")
                    act("decay_end")
                    V.tensor_tensor(by_chunk(k_dec), by_chunk(bank[4][:]), spread(ends[:, 1, :]), ALU.mult
                                    ).then_inc(dn_dve, 1)
                    V.tensor_copy(ends[:, 2, :], q_dec[:, P - 1:T:P]).then_inc(dn_dve, 1)
                    own("chunk_decay")
                    V.tensor_tensor(q_dec, q_dec, qT[:], ALU.mult).then_inc(dn_dve, 1)
                for l in range(1, 7):
                    if gap == 6 + 2 * l:
                        if l < 5:
                            pe(f"xmx{l}")
                            for b in range(4):
                                q, p = divmod(b, 2)
                                to = packed(x_q[32 * b:32 * b + 32, :])[:, :, 32 * q:32 * q + 32]
                                last = V.tensor_tensor(to, to, packed(bank[4][32 * q:32 * q + 32, 0:T // 2]
                                                                      )[:, :, 32 * p:32 * p + 32], ALU.subtract)
                            last.then_inc(dn_dve, 1)
                            own(f"x{l}")
                            V.transpose(y_q, x_q[:]).then_inc(dn_dve, 1)
                        if l == 4:
                            own("y4")
                            dve.wait_ge(dn_pool, after(DN_POOL, h, "y_clear"))
                            for b in range(4):
                                V.tensor_copy(by_chunk(yi[32 * b:32 * b + 32, :])[:, :, 32 * b:32 * b + 32],
                                              packed(y_q[32 * b:32 * b + 32, :])[:, :, 32 * (b // 2):32 * (b // 2) + 32])
                            for b in range(2):
                                last = V.tensor_copy(x64[32 * b:32 * b + 32, :, 32 * b:32 * b + 32],
                                                     packed(x_q[32 * b:32 * b + 32, :])[:, :, 0:32])
                            last.then_inc(dn_dve, 1)
                            own("y_full")
                        if l == 5:
                            pe("xmx5")
                            V.tensor_scalar(x64[32:64, :, 0:32], by_chunk(bank[4][0:32, 0:P]), -1.0, None, ALU.mult
                                            ).then_inc(dn_dve, 1)
                        if l > 4:
                            pe(f"xmx_turn{l}")
                            if l == 5:
                                joined = [(by_chunk(yi[64 * i:64 * i + 32, :])[:, :, 64 * i + 32:64 * i + 64],
                                           by_chunk(bank[5][32 * i:32 * i + 32, 0:T // 2])[:, :, 32 * i:32 * i + 32])
                                          for i in range(2)]
                            else:
                                joined = [(by_chunk(yi[0:64, :])[:, :, 64:P], by_chunk(bank[5][0:64, 0:T // 2]))]
                            for to, turned in joined:
                                last = V.tensor_tensor(to, to, turned, ALU.subtract)
                            last.then_inc(dn_dve, 1)
                for c in range(TB):
                    at = slice(c * P, (c + 1) * P)
                    if gap == 18 + 3 * c and c > 0:
                        pe(f"ks{c}")
                        V.scalar_tensor_tensor(out=resid[:], in0=bank[2][:, at], scalar=nbg_col[:, c:c + 1], in1=bv[:, at],
                                               op0=ALU.mult, op1=ALU.add).then_inc(dn_dve, 1)
                    if gap == 20 + 3 * c and c < TB - 1:
                        pe(f"kv{c}")
                        if c == 0:
                            V.tensor_copy(state[:], bank[4][:, at]).then_inc(dn_dve, 1)
                        else:
                            V.scalar_tensor_tensor(out=state[:], in0=state[:], scalar=ends[:, 2, c:c + 1],
                                                   in1=bank[4][:, at], op0=ALU.mult, op1=ALU.add).then_inc(dn_dve, 1)
                if gap == 30:
                    act("o_high")
                    V.tensor_tensor(o_low[:], sq[:, 0, :], o_high[:].bitcast(F32), ALU.subtract).then_inc(dn_dve, 1)
                if gap == 31:
                    act("o_rstd")
                    V.scalar_tensor_tensor(out=rs[:, 1, :], in0=bank[3][:], scalar=dn_w[:, 0:1], in1=rs[:, 0, :],
                                           op0=ALU.mult, op1=ALU.mult).then_inc(dn_dve, 1)
                    own("o_scaled")
                    V.tensor_tensor(mix[:, bass.ds(h, 1), :].rearrange("p a n -> p (a n)"), rs[:, 1, :], pre[:, 3, :],
                                    ALU.mult).then_inc(dn_dve, 1)

            def att(gap, n):
                def act(name):
                    dve.wait_ge(at_act, after(AT_ACT, n, name))

                def own(name):
                    dve.wait_ge(at_dve, after(AT_DVE, n, name))

                if gap == 0:
                    dve.wait_ge(const_step, CONSTS)
                    V.tensor_scalar(bias_h[:], base_bias[:], slopes[:, bass.ds(n, 1)], None, ALU.mult).then_inc(at_dve, 1)
                for i, (m, qb) in enumerate(SC):
                    if gap == 1 + 2 * i:
                        dve.wait_ge(at_pe, after(AT_PE, n, f"score{i}"))
                        own("bias")
                        e = ex[:, m, ex_block(qb)]
                        w = (qb + 1) * P
                        V.scalar_tensor_tensor(out=e, in0=bank[2 + i % 2][:, 0:w], scalar=float(P) ** -0.5,
                                               in1=bias_h[:, T - w:T], op0=ALU.mult, op1=ALU.add).then_inc(at_dve, 1)
                        own(f"score{i}")
                        V.tensor_reduce(neg_max[:, i:i + 1], e, AX.X, ALU.max, negate=True).then_inc(at_dve, 1)
                if gap == 18:
                    act("exp7")
                    V.reciprocal(inv_sum[:], row_sum[:]).then_inc(at_dve, 1)
                    own("rsum")
                    V.tensor_scalar(inv_sum[:, 4:8], inv_sum[:, 4:8], lam, None, ALU.mult).then_inc(at_dve, 1)
                    own("rsum_lam")
                for q in range(TB):
                    if gap == 18 + q // 2:
                        V.tensor_scalar(ex[:, 1, ex_block(q)], ex[:, 1, ex_block(q)], inv_sum[:, 4 + q:5 + q], None,
                                        ALU.mult).then_inc(at_dve, 1)
                        own(f"p_low{q}")
                        V.scalar_tensor_tensor(out=ex[:, 0, ex_block(q)], in0=ex[:, 0, ex_block(q)],
                                               scalar=inv_sum[:, q:q + 1], in1=ex[:, 1, ex_block(q)],
                                               op0=ALU.mult, op1=ALU.subtract).then_inc(at_dve, 1)
                if gap == 35:
                    act("rstd")
                    for e in range(2):
                        if isinstance(n, int):
                            to = att_o[:, e, :]
                        else:
                            to = mix[:, bass.ds(2 * n + DN_HEADS + e, 1), :].rearrange("p a n -> p (a n)")
                        V.scalar_tensor_tensor(out=to, in0=bank[4 + e][:], scalar=da_w[:, e:e + 1],
                                               in1=att_rs[:, 1, :], op0=ALU.mult, op1=ALU.mult).then_inc(at_dve, 1)

            def head_window(h, before):
                span = S_HEADS(h)
                for gap in range(8 * CHUNKS):
                    if gap == 6 and before is None:
                        dve.wait_ge(param_turned, 1)
                        V.tensor_copy(conv_t[:].rearrange("p t j h -> p (t j h)"), bank[7][:, 0:TAPS * 24]
                                      ).then_inc(conv_ready, 1)
                    if gap == 6:
                        pick_taps(h)
                    if gap == 24:
                        pick_rows(h, before)
                    if before is None:
                        if gap == 0:
                            gates_beta()
                        if gap == 13:
                            gate_columns()
                    else:
                        dn(gap, before)
                    if gap % CHUNKS == 1:
                        low(span, gap // CHUNKS)
                    for j in range(3):
                        for k in range(1, TAPS):
                            if gap == 8 * (j + 1) + (0, 3, 4)[k - 1]:
                                conv(h, j, k)

            head_window(0, None)
            with dve.Fori(1, DN_HEADS) as h:
                head_window(h, h - 1)

            def att_window(n, before):
                span = S_ATT(n)
                for gap in range(12 * CHUNKS):
                    if before is None:
                        if gap < 32:
                            dn(gap, DN_HEADS - 1)
                    else:
                        att(gap, before)
                    if gap % CHUNKS == 1:
                        low(span, gap // CHUNKS)

            att_window(0, None)
            with dve.Fori(1, DA_HEADS) as n:
                att_window(n, n - 1)

            def mix_split(k):
                dve.wait_ge(mix_high, k // 2 + 1)
                V.tensor_tensor(h_low[:, k:k + 2, :], mix[:, k:k + 2, :], h_high[:, k:k + 2, :].bitcast(F32),
                                ALU.subtract).then_inc(mix_low, 1)

            mix_split(0)
            mix_split(2)

            def add_block(span, j, t, cols_of, x_loaded=False, c=None, b=None):
                if x_loaded:
                    dve.wait_ge(x_landed[t], 32)
                chunk_done(dve, span, j, t if c is None else c)
                at = x1[:, t, cols_of]
                V.tensor_tensor(at, at, bank[OUT_BANKS[t] if b is None else b][:], ALU.add).then_inc(out_added, 1)

            for gap in range(16 * CHUNKS):
                j = gap // CHUNKS
                if gap % CHUNKS == 0:
                    low(S_OUT0, j)
                att(gap, DA_HEADS - 1)
                if gap < 5:
                    mix_split(4 + 2 * gap)
                if gap == 36:
                    for e in range(2):
                        dve.wait_ge(mix_high, 8 + e)
                        V.tensor_tensor(h_low[:, KT - 2 + e, :], att_o[:, e, :], h_high[:, KT - 2 + e, :].bitcast(F32),
                                        ALU.subtract).then_inc(mix_low, 1)
                if j % 4 == 3:
                    add_block(S_OUT0, j, gap % CHUNKS, slice(j // 4 * T, (j // 4 + 1) * T), x_loaded=True)
            def out_times_row(g, t):
                dve.wait_ge(row_landed, 32)
                dve.wait_ge(out_added, 4 * g + 16 + t + 1)
                times_row(1, t, bass.ds(g * T, T))

            with dve.Fori(0, 3) as g:
                for j in range(4):
                    low(S_OUT1(g), j)
                for t in range(TB):
                    add_block(S_OUT1(g), 3, t, bass.ds(g * T, T))
                for t in range(TB):
                    out_times_row(g, t)
            low(S_OUT1_LAST, 0)
            for t in range(TB):
                if t == 3:
                    for j in (1, 2):
                        low(S_OUT1_LAST, j)
                add_block(S_OUT1_LAST, t, t, slice(D - T, D), c=3)
                out_times_row(3, t)
                if t % 2 == 1:
                    sums(PAIR[t // 2], TB + 12 + t + 1)
                    diagonals(1, t // 2)
            low(S_OUT1_LAST, 3)
            for t in range(TB):
                low_parts(1, t)

            def product(n, fb):
                dve.wait_ge(gate_ready, 4 * n + fb + 1)
                V.tensor_tensor(hidden[:, fb % 2, :], gate_act[:, fb % 2, :], bank[3 + 2 * (fb % 2)][:], ALU.mult
                                ).then_inc(hid_ready, 1)

            def hidden_low(n, fb):
                dve.wait_ge(hid_high_ready, 4 * n + fb + 1)
                V.tensor_tensor(hid_low[:, fb, :], hidden[:, fb % 2, :], hid_high[:, fb, :].bitcast(F32), ALU.subtract
                                ).then_inc(hid_low_ready, 1)

            for j in range(16):
                low(S_FF0, j)
                if j % 4 == 0 and j > 0:
                    half_done(dve, S_FF0, j - 1)
                    product(0, j // 4 - 1)
                    hidden_low(0, j // 4 - 1)
            with dve.Fori(1, FF_GROUPS) as n:
                span = S_FF(n)
                for j in range(24):
                    if j == 0:
                        half_done(dve, span, -1)
                        product(n - 1, 3)
                        hidden_low(n - 1, 3)
                    low(span, j)
                    if j in (4, 16, 20):
                        half_done(dve, span, j - 1)
                        product(n, (j - 12) // 4 if j > 4 else 0)
                    if j in (12, 16, 20):
                        hidden_low(n, (j - 12) // 4)
                    if j in (5, 7, 9, 11):
                        for t in range(TB):
                            add_block(span, j, t, slice((j - 5) // 2 * T, (j - 3) // 2 * T))
            half_done(dve, S_END, -1)
            product(FF_GROUPS - 1, 3)
            hidden_low(FF_GROUPS - 1, 3)
            for j in range(8):
                low(S_END, j)
                if j in (1, 3):
                    for t in range(TB):
                        add_block(S_END, j, t, slice(j // 2 * T, (j // 2 + 1) * T))
                if j in (2, 4):
                    dve.wait_ge(row_landed, 48)
                    c = j // 2 - 1
                    for t in range(TB):
                        dve.wait_ge(norm_sq, TB + 16 + 4 * c + t + 1)
                        at = slice(c * T, (c + 1) * T)
                        V.tensor_tensor(x1[:, t, at], x1[:, t, at], w_row[:, at], ALU.mult).then_inc(norm_scaled, 1)

            def scale_block(i, t):
                dve.wait_ge(norm_rstd, 4 + i + 1)
                at = slice(D // 2, D)
                V.scalar_tensor_tensor(out=x1[:, t, at], in0=x1[:, t, at], scalar=rstd[:, t:t + 1], in1=w_row[:, at],
                                       op0=ALU.mult, op1=ALU.mult).then_inc(out_scaled, 1)

            def end_add(t, c):
                add_block(S_END, 4 + t, t, slice(c * T, (c + 1) * T), c=2 * c - 3, b=END_BANKS[t % 2][c - 2])

            for t in (0, 1):
                end_add(t, 2)
                end_add(t, 3)
            sums(slice(0, 2), TB + 16 + 8 + 4)
            end_add(2, 2)
            scale_block(0, 0)
            end_add(2, 3)
            sums(slice(2, 3), TB + 16 + 8 + 6)
            scale_block(0, 1)
            end_add(3, 2)
            scale_block(1, 2)
            end_add(3, 3)
            sums(slice(3, 4), TB + 16 + 8 + 8)
            scale_block(2, 3)

        @block.tensor
        def _(pe):
            M = nc.tensor.matmul

            def turn(out_ap, in_ap, n=P):
                return nc.tensor.transpose(out_ap, in_ap, ident[0:n, 0:n])

            def three(out_ap, stat, mov, start, stop):
                M(out_ap, stat[0], mov[0], start=start, stop=False, skip_group_check=True)
                M(out_ap, stat[0], mov[1], start=False, stop=False, skip_group_check=True)
                return M(out_ap, stat[1], mov[0], start=False, stop=stop, skip_group_check=True)

            def weights(slot, at):
                return w_high[:, slot, at], w_low[:, slot, at]

            def half_ready(span, j):
                pe.wait_ge(w_low_ready, count(span, j + 1))

            def column_chunk(span, j, c, b, part):
                slot = (span[0] + j) % SLOTS
                if c == 0:
                    half_ready(span, j)
                for kk in (2 * c, 2 * c + 1):
                    k = 8 * part + kk
                    last = three(bank[b][:], weights(slot, slice(kk * P, (kk + 1) * P)), (h_high[:, k, :], h_low[:, k, :]),
                                 k == 0, k == KT - 1)
                last.then_inc(chunks_done, 1)

            def value_chunk(span, j, c):
                slot = (span[0] + j) % SLOTS
                if c == 0:
                    half_ready(span, j)
                k = CHUNKS * j + c
                for t in range(TB):
                    at = slice(t % 2 * 2 * P, (t % 2 + 1) * 2 * P)
                    last = three(bank[ATT_BANKS[t // 2]][:, at], tuple(h[:, k, t * P:(t + 1) * P] for h in (h_high, h_low)),
                                 weights(slot, slice(c * 2 * P, (c + 1) * 2 * P)), k == 0 and t % 2 == 0, k == KT - 1)
                last.then_inc(chunks_done, 1)

            def row_chunk(span, j, t, acts, k0, start, stop, b=None):
                slot = (span[0] + j) % SLOTS
                if t == 0:
                    half_ready(span, j)
                for kk in range(2):
                    last = three(bank[OUT_BANKS[t] if b is None else b][:], tuple(a[:, k0 + kk, t * P:(t + 1) * P] for a in acts),
                                 weights(slot, slice(kk * T, (kk + 1) * T)), start and kk == 0, stop and kk == 1)
                last.then_inc(chunks_done, 1)

            pe.wait_ge(const_step, 2)
            pe.wait_ge(dve_const, 3)

            def norm(r, scaled):
                for t in range(TB):
                    if r == 0 and t == 2:
                        pe.wait_ge(norm_scaled2, 1)
                    else:
                        pe.wait_ge(norm_scaled, scaled + t + (0 if r == 0 and t == 3 else 1))
                    pe.wait_ge(norm_diag, TB * r + t + 1)
                    for g in range(4):
                        b = NORM_BANKS[t % 2][g]
                        if r == 1 and t == 1 and g == 0:
                            pe.wait_ge(out_added, 32)
                        if t >= 2:
                            pe.wait_ge(norm_low, 16 * r + 4 * (t - 2) + g + 1)
                        for k in range(4):
                            at = slice((4 * g + k) * P, (4 * g + k + 1) * P)
                            last = M(bank[b][:, k * P:(k + 1) * P], xn[:, t, at], diag[:, t, :], start=True, stop=True)
                        last.then_inc(norm_turned, 1)

            norm(0, 0)
            def turned_ready(r, j, c):
                if c % 2 == 0:
                    pe.wait_ge(norm_low, 16 * r + 12 + 2 * j + c // 2 + 1)

            for j in range(2):
                for c in range(CHUNKS):
                    turned_ready(0, j, c)
                    if c == 0:
                        half_ready((0, 0, 4), j)
                    for kk in (2 * c, 2 * c + 1):
                        k = 8 * j + kk
                        M(bank[0][0:48, :], w_high[:, j, kk * P:kk * P + 48], h_high[:, k, :], start=k == 0, stop=False,
                          skip_group_check=True)
                        last = M(bank[0][0:16, :], w_high[:, j, kk * P:kk * P + 16], h_low[:, k, :], start=False,
                                 stop=k == KT - 1, skip_group_check=True)
                    last.then_inc(chunks_done, 1)

            pe.wait_ge(const_step, CONSTS)

            def gates_turned():
                pe.wait_ge(ba_dve, 6)
                for i, rows in enumerate((gates, betas)):
                    for c in range(TB):
                        last = turn(bank[2][:, (4 * i + c) * 16:(4 * i + c + 1) * 16], rows[:, c * P:(c + 1) * P], 16)
                last.then_inc(ba_turned, 1)

            def qk_norms(h, before):
                pe.wait_ge(qk_low_ready, h + 1)
                if before is not None:
                    pe.wait_ge(dn_dve, after(DN_DVE, before, "r3"))
                    pe.wait_ge(dn_act, after(DN_ACT, before, "vn3"))
                for i, b in ((1, 2), (0, 6)):
                    M(bank[b][:], ones_r[:], qk_high[:, i, :], start=True, stop=False)
                    M(bank[b][:], ones_r[:], qk_low[:, i, :], start=False, stop=True).then_inc(qk_sums, 1)

            def dn(gap, h):
                def act(name):
                    pe.wait_ge(dn_act, after(DN_ACT, h, name))

                def dve(name):
                    pe.wait_ge(dn_dve, after(DN_DVE, h, name))

                def pool(name):
                    pe.wait_ge(dn_pool, after(DN_POOL, h, name))

                def chunks(b, stat, mov):
                    for c in range(TB):
                        at = slice(c * P, (c + 1) * P)
                        last = M(bank[b][:, at], stat[:, at], mov[:, at], start=True, stop=True)
                    last.then_inc(dn_pe, 1)

                def odd32(view, c):
                    return view[:, c * P:(c + 1) * P].rearrange("p (g b s) -> p g b s", b=2, s=32)[:, :, 1, :]

                def halves(b, stat, mov):
                    for c in range(TB):
                        last = M(bank[b][0:64, c * 64:(c + 1) * 64], stat(c), mov(c), start=True, stop=True)
                    last.then_inc(dn_pe, 1)

                def turns(b, src):
                    for c in range(TB):
                        last = turn(bank[b][:, c * P:(c + 1) * P], src[:, c * P:(c + 1) * P])
                    last.then_inc(dn_pe, 1)

                if gap == 0:
                    pe.wait_ge(rows_picked, 2 * h + 1)
                    M(bank[4][:], ones_r[0:48, :], picked[:, 0, :], start=True, stop=True).then_inc(dn_pe, 1)
                if gap == 1:
                    pe.wait_ge(qk_logs, 2 * h + 2)
                    pe.wait_ge(rows_picked, 2 * h + 2)
                    M(bank[5][:], ones_r[0:48, :], picked[:, 1, :], start=True, stop=True).then_inc(dn_pe, 1)
                    pe.wait_ge(pre_ready, 4 * h + 3)
                    turns(6, pre[:, 2, :])
                if gap == 3:
                    dve("k")
                    chunks(2, kT[:], kT[:])
                    dve("q")
                    chunks(3, kT[:], qT[:])
                if gap == 4:
                    dve("gap_end")
                    act("decay_start")
                    turns(4, kT[:])
                for l in range(1, 7):
                    if gap == 5 + 2 * l:
                        if l < 6:
                            pool(f"level{l}")
                        if l == 1:
                            dve("x0")
                        else:
                            dve(f"x{l - 1}")
                        if l < 5:
                            halves(2, lambda c: level_m[:, l % 2, c * 64:(c + 1) * 64], lambda c: x_q[:, c * 64:(c + 1) * 64])
                        elif l == 5:
                            halves(2, lambda c: level_m[:, 1, c * 64:(c + 1) * 64], lambda c: x_q[:, c * 64:(c + 1) * 64])
                        else:
                            halves(2, lambda c: m_t[:, c * P + 64:(c + 1) * P], lambda c: x64[:, c, :])
                    if gap == 6 + 2 * l:
                        act(f"mx{l}")
                        if l == 1:
                            dve("k_dec")
                        else:
                            dve("y_full" if l == 5 else f"y{l - 1}")
                        if l < 5:
                            halves(4, lambda c: y_q[:, c * 64:(c + 1) * 64], lambda c: mx_p[:, c * 64:(c + 1) * 64])
                        if l == 5:
                            for c in range(TB):
                                last = M(bank[4][0:32, c * 32:(c + 1) * 32], yi[:, c * P + 32:c * P + 64],
                                         mxs[:, c * 64:c * 64 + 32], start=True, stop=True)
                            last.then_inc(dn_pe, 1)
                            halves(5, lambda c: mxs[:, c * 64:(c + 1) * 64], lambda c: odd32(yi, c))
                        if l == 6:
                            halves(5, lambda c: mxs[:, c * 64:(c + 1) * 64], lambda c: yi[:, c * P + 64:(c + 1) * P])
                for c in range(TB):
                    at = slice(c * P, (c + 1) * P)
                    if gap == 18 + 3 * c and c > 0:
                        dve(f"s{c - 1}")
                        M(bank[2][:, at], kT[:, at], state[:], start=True, stop=True).then_inc(dn_pe, 1)
                    if gap == 19 + 3 * c:
                        dve(f"r{c}" if c else "y6")
                        M(bank[6][:, at], yi[:, at], resid[:] if c else bv[:, at], start=True, stop=True).then_inc(dn_pe, 1)
                    if gap == 20 + 3 * c:
                        if c:
                            dve("q_dec")
                            M(bank[3][:, at], state[:], q_dec[:, at], start=True, stop=False)
                        act(f"vn{c}")
                        M(bank[3][:, at], v_new[:, c % 2, :], decay[:, at], start=(c == 0), stop=True).then_inc(dn_pe, 1)
                        if c < TB - 1:
                            M(bank[4][:, at], k_dec[:, at], v_new[:, c % 2, :], start=True, stop=True).then_inc(dn_pe, 1)
                if gap == 31:
                    dve("o_low")
                    M(bank[5][:], ones_r[:], o_high[:], start=True, stop=False)
                    M(bank[5][:], ones_r[:], o_low[:], start=False, stop=True).then_inc(dn_pe, 1)

            def att(gap, n):
                def act(name):
                    pe.wait_ge(at_act, after(AT_ACT, n, name))

                def dve(name):
                    pe.wait_ge(at_dve, after(AT_DVE, n, name))

                if gap == 1:
                    pe.wait_ge(at_dve, all_done(AT_DVE, n))
                    pe.wait_ge(dn_dve, all_done(DN_DVE, DN_HEADS))
                for i, (m, qb) in enumerate(SC):
                    if gap == 1 + 2 * i:
                        pe.wait_ge(att_pre_ready, 6 * n + (4 if m == 0 else 6))
                        if i >= 2:
                            dve(f"score{i - 2}")
                        w = (qb + 1) * P
                        M(bank[2 + i % 2][:, 0:w], pre[:, 2 + 2 * m, qb * P:(qb + 1) * P], pre[:, 3 + 2 * m, 0:w],
                          start=True, stop=True).then_inc(at_pe, 1)
                for k in range(TB):
                    if gap == 22 + 2 * k:
                        if k < 2:
                            dve("p3")
                        else:
                            act(f"p{k - 2}")
                        for q in range(k, TB):
                            at = ex_block(q).start + k * P
                            last = turn(bank[2 + k % 2][:, (q - k) * P:(q - k + 1) * P], ex[:, 0, at:at + P])
                        last.then_inc(at_pe, 1)
                if gap in (30, 31):
                    e = gap - 30
                    act("p3")
                    for k in range(TB):
                        w = (TB - k) * P
                        last = M(bank[4 + e][:, k * P:T], v_tok[:, k, e * P:(e + 1) * P], p_t[:, PT_OFF[k]:PT_OFF[k] + w],
                                 start=(k == 0), stop=(k == TB - 1), skip_group_check=True)
                    last.then_inc(at_pe, 1)
                if gap == 35:
                    pe.wait_ge(att_sum_low_ready, n + 1)
                    M(bank[2][:], ones_r[:], att_sum_high[:], start=True, stop=False)
                    M(bank[2][:], ones_r[:], att_sum_low[:], start=False, stop=True).then_inc(at_pe, 1)

            def head_unit_ready(h, j):
                first = isinstance(h, int)
                if j == 0 and not first:
                    pe.wait_ge(conv_tap, 9 * h)
                if j == 1:
                    if first:
                        pe.wait_ge(ba_summed, 1)
                    else:
                        pe.wait_ge(pre_ready, 4 * h)
                if j >= 2:
                    pe.wait_ge(conv_tap, 9 * h + 3 * (j - 1))

            def head_window(h, before):
                span = S_HEADS(h)
                for gap in range(8 * CHUNKS):
                    j, c = divmod(gap, CHUNKS)
                    if gap % 8 == 0:
                        head_unit_ready(h, gap // 8)
                    column_chunk(span, j, c, (U_HEADS + j // 2) % 2, j % 2)
                    if before is None:
                        if gap == 2:
                            pe.wait_ge(params_landed, PARAMS)
                            turn(bank[7][:, 0:TAPS * 24], conv_rows[0:TAPS * 24, :], TAPS * 24).then_inc(param_turned, 1)
                        if gap == 12:
                            gates_turned()
                    else:
                        dn(gap, before)
                    if gap == 30:
                        qk_norms(h, before)

            head_window(0, None)
            with pe.Fori(1, DN_HEADS) as h:
                head_window(h, h - 1)

            def att_window(n, before):
                span = S_ATT(n)
                for gap in range(12 * CHUNKS):
                    j, c = divmod(gap, CHUNKS)
                    if gap == 0:
                        if before is None:
                            pe.wait_ge(conv_tap, 9 * DN_HEADS)
                        else:
                            pe.wait_ge(att_pre_ready, 6 * n - 1)
                    if gap == 16:
                        if before is None:
                            pe.wait_ge(pre_ready, 4 * DN_HEADS)
                        else:
                            pe.wait_ge(att_pre_ready, 6 * n)
                    if gap in (24, 32, 40):
                        pe.wait_ge(att_pre_ready, 6 * n + gap // 8 - 1)
                    if gap < 16:
                        value_chunk(span, j, c)
                    else:
                        column_chunk(span, j, c, ATT_BANKS[j // 2], j % 2)
                    if before is None:
                        if gap < 32:
                            dn(gap, DN_HEADS - 1)
                    else:
                        att(gap, before)

            att_window(0, None)
            with pe.Fori(1, DA_HEADS) as n:
                att_window(n, n - 1)

            h_parts = (h_high, h_low)
            for gap in range(16 * CHUNKS):
                j, t = divmod(gap, CHUNKS)
                if gap < 2:
                    pe.wait_ge(att_pre_ready, 6 * DA_HEADS - 1)
                if gap == 3:
                    pe.wait_ge(att_pre_ready, 6 * DA_HEADS)
                if j < 4 and t == 0:
                    pe.wait_ge(mix_low, j + 1)
                if j % 4 == 0 and j > 0:
                    pe.wait_ge(out_added, j - 4 + t + 1)
                row_chunk(S_OUT0, j, t, h_parts, 2 * (j % 4), j % 4 == 0, j % 4 == 3)
                att(gap, DA_HEADS - 1)
            pe.wait_ge(mix_low, 9)
            with pe.Fori(0, 3) as g:
                for j in range(4):
                    for t in range(TB):
                        if j == 0:
                            pe.wait_ge(out_added, 4 * g + 12 + t + 1)
                        row_chunk(S_OUT1(g), j, t, h_parts, 8 + 2 * j, j == 0, j == 3)
            for t in range(TB):
                pe.wait_ge(out_added, 24 + t + 1)
                for j in range(4):
                    row_chunk(S_OUT1_LAST, j, t, h_parts, 8 + 2 * j, j == 0, j == 3)
            norm(1, TB - 1 + 12)

            def pair(span, j0, n, fb):
                if not isinstance(n, int) or 4 * n + fb >= 2:
                    pe.wait_ge(hid_ready, 4 * n + fb - 1)
                for j in range(4):
                    for c in range(CHUNKS):
                        if isinstance(n, int) and 4 * n + fb == 0 and j < 2:
                            turned_ready(1, j, c)
                        column_chunk(span, j0 + j, c, 2 + 2 * (fb % 2) + j // 2, j % 2)

            def down(span, j0, n, added, halves=8):
                for j in range(halves):
                    if j < 2:
                        pe.wait_ge(hid_low_ready, 4 * n + 2 * j + 2)
                    for t in range(TB):
                        if j % 2 == 0:
                            pe.wait_ge(out_added, added + 4 * (j // 2) - 4 + t + 1)
                        row_chunk(span, j0 + j, t, (hid_high, hid_low), 2 * (j % 2), j % 2 == 0, j % 2 == 1)

            for fb in range(4):
                pair(S_FF0, 4 * fb, 0, fb)
            with pe.Fori(1, FF_GROUPS) as n:
                pair(S_FF(n), 0, n, 0)
                down(S_FF(n), 4, n - 1, 16 * n + 16)
                for fb in range(1, 4):
                    pair(S_FF(n), 8 + 4 * fb, n, fb)
            down(S_END, 0, FF_GROUPS - 1, ADDED_END, halves=4)
            for t in range(TB):
                pe.wait_ge(out_added, ADDED_END + (4 + 2, 8, 8 + 2, 8 + 4)[t])
                for j in range(4, 8):
                    row_chunk(S_END, j, t, (hid_high, hid_low), 2 * (j % 2), j % 2 == 0, j % 2 == 1,
                              b=END_BANKS[t % 2][j // 2 - 2])
    return nc


_INS = ["x", "attn_norm_w", "w_in", "conv_w", "a_log", "dt_bias", "dn_norm_w", "lam_q1", "lam_k1", "lam_q2", "lam_k2",
        "da_norm_w", "w_out", "ffn_norm_w", "w_gate", "w_up", "w_down", "final_norm_w"]


def kernel(**inputs):
    import numpy as _np
    import concourse.bacc as _bacc
    from concourse import mybir as _mybir
    from concourse.bass_utils import run_bass_kernel_spmd as _run

    nc = _bacc.Bacc("TRN2", target_bir_lowering=False, num_devices=1)
    arrays, args = {}, []
    for name in _INS:
        a = _np.ascontiguousarray(inputs[name])
        arrays[f"in_{name}_dram"] = a
        args.append(nc.dram_tensor(f"in_{name}_dram", a.shape, _mybir.dt.from_np(a.dtype), kind="ExternalInput").ap())
    args.append(nc.dram_tensor("out_0_dram", (1, T, D), F32, kind="ExternalOutput").ap())
    build(nc, *args)
    r = _run(nc, [arrays], core_ids=[0])
    return r.results[0]["out_0_dram"]
```
